# Optimizing a Trainium2 kernel written in Bass

```python
import jax
import jax.numpy as jnp
from jax import lax
import numpy as np

D_MODEL = 1024
BATCH = 1
SEQ = 256
DEPTH = 2

GRID_W = 64
CTX_LEN = 256
HEAD_DIM = 64
N_BRANCH = 4
BRANCH_W = 256
A_WIDTH = 256
NA_HEADS = 4
NA_WIN_R = 8
NA_WIN_C = 16
GQA_Q_HEADS = 4
GQA_KV_HEADS = 2
GQA_GROUP = GQA_Q_HEADS // GQA_KV_HEADS
Q_BLOCK = 128
ROPE_THETA = 10000.0
RWKV_HEADS = 4
RW = RWKV_HEADS * HEAD_DIM
LORA_W = 64
LORA_A = 64
LORA_G = 128
RW_SHIFT = 3 * RW + LORA_W + LORA_A
D_FF = 2816
NORM_EPS = 1e-6
LN_X_EPS = 64e-5

COLS_A = 3 * A_WIDTH
COLS_NA = 3 * NA_HEADS * HEAD_DIM
COLS_GQA = (GQA_Q_HEADS + 2 * GQA_KV_HEADS) * HEAD_DIM
COLS_RW = RW_SHIFT + LORA_G
D_IN = COLS_A + COLS_NA + COLS_GQA + COLS_RW

kernel_name = 'hybrid_parallel_dit_block'

def rmsnorm(x, g):
    xf = x.astype(jnp.float32)
    y = xf * lax.rsqrt(jnp.mean(xf * xf, axis=-1, keepdims=True) + NORM_EPS)
    return (y * g.astype(jnp.float32)).astype(x.dtype)

def modulate(h, shift, scale):
    return h * (1 + scale) + shift

def dwconv3(x, w):
    xp = jnp.pad(x, ((0, 0), (1, 1), (0, 0)))
    return xp[:, :-2] * w[0] + xp[:, 1:-1] * w[1] + xp[:, 2:] * w[2]

def to_heads(x, n_heads):
    b, t, _ = x.shape
    return x.reshape(b, t, n_heads, HEAD_DIM).transpose(0, 2, 1, 3)

def from_heads(x):
    b, h, t, d = x.shape
    return x.transpose(0, 2, 1, 3).reshape(b, t, h * d)

def axial_rope_tables(n_tok):
    t = jnp.arange(n_tok)
    row = (t // GRID_W).astype(jnp.float32)
    col = (t % GRID_W).astype(jnp.float32)
    n_freq = HEAD_DIM // 4
    inv_freq = ROPE_THETA ** (-jnp.arange(n_freq, dtype=jnp.float32) / n_freq)
    ang = jnp.concatenate([row[:, None] * inv_freq, col[:, None] * inv_freq], axis=-1)
    return jnp.cos(ang), jnp.sin(ang)

def apply_rope(x, cos, sin):
    xf = x.astype(jnp.float32).reshape(x.shape[:-1] + (HEAD_DIM // 2, 2))
    x1, x2 = xf[..., 0], xf[..., 1]
    out = jnp.stack([x1 * cos - x2 * sin, x1 * sin + x2 * cos], axis=-1)
    return out.reshape(x.shape).astype(x.dtype)

def grouped_attend(q, k, v):
    s = jnp.einsum('bngqd,bnkd->bngqk', q, k, preferred_element_type=jnp.float32)
    p = jax.nn.softmax(s, axis=-1).astype(v.dtype)
    return jnp.einsum('bngqk,bnkd->bngqd', p, v)

def mixer_a(z, w_conv):
    bg, cg, xin = z[..., :A_WIDTH], z[..., A_WIDTH:2 * A_WIDTH], z[..., 2 * A_WIDTH:]
    return bg * dwconv3(cg * xin, w_conv)

def na_tables(rows):
    wr = min(NA_WIN_R, rows)
    i = jnp.arange(rows)
    j = jnp.arange(GRID_W)
    rs = jnp.clip(i - wr // 2, 0, rows - wr)
    cs = jnp.clip(j - NA_WIN_C // 2, 0, GRID_W - NA_WIN_C)
    kr = rs[:, None] + jnp.arange(wr)
    kc = cs[:, None] + jnp.arange(NA_WIN_C)
    key_idx = kr[:, None, :, None] * GRID_W + kc[None, :, None, :]
    dr = kr - i[:, None] + (NA_WIN_R - 1)
    dc = kc - j[:, None] + (NA_WIN_C - 1)
    bias_idx = dr[:, None, :, None] * (2 * NA_WIN_C - 1) + dc[None, :, None, :]
    n_keys = wr * NA_WIN_C
    return key_idx.reshape(rows, GRID_W, n_keys), bias_idx.reshape(rows, GRID_W, n_keys)

def na_latent(q, k, v, kc, vc, bias_flat, key_idx, bias_idx):
    b, h, t, d = q.shape
    rows = t // GRID_W
    q_rows = jnp.moveaxis(q.reshape(b, h, rows, GRID_W, d), 2, 0)

    def one_row(args):
        q_row, kidx, bidx = args
        k_nb = jnp.take(k, kidx, axis=2)
        v_nb = jnp.take(v, kidx, axis=2)
        s_loc = jnp.einsum('bhqd,bhqkd->bhqk', q_row, k_nb, preferred_element_type=jnp.float32)
        s_loc = s_loc + bias_flat[:, bidx].astype(jnp.float32)
        s_ctx = jnp.einsum('bhqd,bhkd->bhqk', q_row, kc, preferred_element_type=jnp.float32)
        p = jax.nn.softmax(jnp.concatenate([s_loc, s_ctx], axis=-1), axis=-1).astype(v.dtype)
        nk = k_nb.shape[3]
        return (jnp.einsum('bhqk,bhqkd->bhqd', p[..., :nk], v_nb)
                + jnp.einsum('bhqk,bhkd->bhqd', p[..., nk:], vc))

    out = lax.map(one_row, (q_rows, key_idx, bias_idx))
    return jnp.moveaxis(out, 0, 2).reshape(b, h, t, d)

def mixer_b(zc, zl, na_bias, key_idx, bias_idx, with_ctx):
    scale = HEAD_DIM ** -0.5
    w = NA_HEADS * HEAD_DIM
    qc, kc, vc = to_heads(zc[..., :w], NA_HEADS), to_heads(zc[..., w:2 * w], NA_HEADS), to_heads(zc[..., 2 * w:], NA_HEADS)
    ql, kl, vl = to_heads(zl[..., :w], NA_HEADS), to_heads(zl[..., w:2 * w], NA_HEADS), to_heads(zl[..., 2 * w:], NA_HEADS)
    yl = na_latent(ql * scale, kl, vl, kc, vc, na_bias.reshape(NA_HEADS, -1), key_idx, bias_idx)
    yc = None
    if with_ctx:
        yc = from_heads(grouped_attend((qc * scale)[:, :, None], kc, vc)[:, :, 0])
    return yc, from_heads(yl)

def gqa_qkv(z, q_norm, k_norm):
    nq = GQA_Q_HEADS * HEAD_DIM
    nkv = GQA_KV_HEADS * HEAD_DIM
    q = rmsnorm(to_heads(z[..., :nq], GQA_Q_HEADS), q_norm) * HEAD_DIM ** -0.5
    k = rmsnorm(to_heads(z[..., nq:nq + nkv], GQA_KV_HEADS), k_norm)
    v = to_heads(z[..., nq + nkv:], GQA_KV_HEADS)
    return q, k, v

def mixer_c(zc, zl, q_norm, k_norm, cos, sin, with_ctx):
    qc, kc, vc = gqa_qkv(zc, q_norm, k_norm)
    ql, kl, vl = gqa_qkv(zl, q_norm, k_norm)
    ql = apply_rope(ql, cos, sin)
    kl = apply_rope(kl, cos, sin)
    k_all = jnp.concatenate([kl, kc], axis=2)
    v_all = jnp.concatenate([vl, vc], axis=2)
    b, _, t, d = ql.shape
    q_blocks = jnp.moveaxis(ql.reshape(b, GQA_KV_HEADS, GQA_GROUP, t // Q_BLOCK, Q_BLOCK, d), 3, 0)
    out = lax.map(lambda blk: grouped_attend(blk, k_all, v_all), q_blocks)
    yl = jnp.moveaxis(out, 0, 3).reshape(b, GQA_Q_HEADS, t, d)
    yc = None
    if with_ctx:
        lc = qc.shape[2]
        oc = grouped_attend(qc.reshape(b, GQA_KV_HEADS, GQA_GROUP, lc, d), kc, vc)
        yc = from_heads(oc.reshape(b, GQA_Q_HEADS, lc, d))
    return yc, from_heads(yl)

def rwkv_streams(z, mu, w0, w2, a0, a2, k_k, k_a, reverse):
    b, t, _ = z.shape
    zs = z[..., :RW_SHIFT]
    if reverse:
        nb = jnp.pad(zs[:, 1:], ((0, 0), (0, 1), (0, 0)))
    else:
        nb = jnp.pad(zs[:, :-1], ((0, 0), (1, 0), (0, 0)))
    zs = zs + mu * (nb - zs)
    r, k, v = zs[..., :RW], zs[..., RW:2 * RW], zs[..., 2 * RW:3 * RW]
    lw = zs[..., 3 * RW:3 * RW + LORA_W]
    la = zs[..., 3 * RW + LORA_W:]
    w_log = (w0 + jnp.tanh(lw) @ w2).astype(jnp.float32)
    w = jnp.exp(-jnp.exp(-jax.nn.softplus(-w_log) - 0.5))
    a = jax.nn.sigmoid(a0 + la @ a2)
    kk = (k * k_k).reshape(b, t, RWKV_HEADS, HEAD_DIM).astype(jnp.float32)
    kk = kk * lax.rsqrt(jnp.maximum(jnp.sum(kk * kk, axis=-1, keepdims=True), 1e-24))
    k = k * (1 + (a - 1) * k_a)
    shp = (b, t, RWKV_HEADS, HEAD_DIM)
    return r.reshape(shp), w.reshape(shp), k.reshape(shp), v.reshape(shp), kk, a.reshape(shp)

def rwkv_scan(s0, r, w, k, v, kk, a, reverse, emit):
    seq = tuple(jnp.moveaxis(u.astype(jnp.float32), 1, 0) for u in (r, w, k, v, kk, a))

    def step(s, inp):
        r_t, w_t, k_t, v_t, kk_t, a_t = inp
        sa = jnp.einsum('bhvk,bhk->bhv', s, kk_t)
        s = (s * w_t[:, :, None, :] - sa[..., None] * (kk_t * a_t)[:, :, None, :]
             + v_t[..., None] * k_t[:, :, None, :])
        return s, (jnp.einsum('bhvk,bhk->bhv', s, r_t) if emit else None)

    s, y = lax.scan(step, s0, seq, reverse=reverse)
    return s, (jnp.moveaxis(y, 0, 1) if emit else None)

def rwkv_bonus(streams, r_k):
    r, _, k, v, _, _ = streams
    return jnp.sum(r * k * r_k, axis=-1, keepdims=True) * v

def rwkv_readout(ys, bonus, lg, g2, ln_w, ln_b):
    y = ys[0] + ys[1]
    mean = jnp.mean(y, axis=-1, keepdims=True)
    var = jnp.mean(jnp.square(y - mean), axis=-1, keepdims=True)
    y = (y - mean) * lax.rsqrt(var + LN_X_EPS) * ln_w.reshape(RWKV_HEADS, HEAD_DIM) + ln_b.reshape(RWKV_HEADS, HEAD_DIM)
    y = y.astype(lg.dtype) + bonus[0] + bonus[1]
    b, t = lg.shape[:2]
    return y.reshape(b, t, RW) * (jax.nn.sigmoid(lg) @ g2)

def mixer_d(zc, zl, mu, w0, w2, a0, a2, k_k, k_a, r_k, g2, ln_w, ln_b, with_ctx):
    b = zl.shape[0]
    ys_l, bon_l, ys_c, bon_c = [], [], [], []
    for d in range(2):
        rev = d == 1
        sc = rwkv_streams(zc, mu[d], w0[d], w2[d], a0[d], a2[d], k_k, k_a, rev)
        sl = rwkv_streams(zl, mu[d], w0[d], w2[d], a0[d], a2[d], k_k, k_a, rev)
        s0 = jnp.zeros((b, RWKV_HEADS, HEAD_DIM, HEAD_DIM), jnp.float32)
        s_ctx, yc = rwkv_scan(s0, *sc, reverse=rev, emit=with_ctx)
        _, yl = rwkv_scan(s_ctx, *sl, reverse=rev, emit=True)
        ys_l.append(yl)
        bon_l.append(rwkv_bonus(sl, r_k))
        if with_ctx:
            ys_c.append(yc)
            bon_c.append(rwkv_bonus(sc, r_k))
    out_l = rwkv_readout(ys_l, bon_l, zl[..., RW_SHIFT:], g2, ln_w, ln_b)
    out_c = rwkv_readout(ys_c, bon_c, zc[..., RW_SHIFT:], g2, ln_w, ln_b) if with_ctx else None
    return out_c, out_l

def merge_branches(h, ys, w_branch, w_gate, b_gate, w_o):
    gates = jax.nn.sigmoid(h @ w_gate + b_gate)
    acc = gates[..., :D_MODEL] * (ys[0] @ w_branch[0])
    for i in range(1, N_BRANCH):
        acc = acc + gates[..., i * D_MODEL:(i + 1) * D_MODEL] * (ys[i] @ w_branch[i])
    return acc @ w_o

def conv_ffn(h, w_up, w_conv, w_down):
    u = dwconv3(h @ w_up, w_conv)
    return (u[..., :D_FF] * jax.nn.silu(u[..., D_FF:])) @ w_down

def setup_inputs(seed: int = 0) -> dict:
    key = jax.random.key(seed)
    ks = iter(jax.random.split(key, 40))
    L = DEPTH
    D = D_MODEL

    def nrm(shape, scale):
        return jax.random.normal(next(ks), shape, jnp.float32) * scale

    def unif(shape, lo, hi):
        return jax.random.uniform(next(ks), shape, jnp.float32, lo, hi)

    return {
        'x': nrm((BATCH, SEQ, D), 1.0),
        'c': nrm((BATCH, D), 1.0),
        'ctx': nrm((BATCH, CTX_LEN, D), 1.0),
        'c_ctx': nrm((D,), 1.0),
        'ada_w': nrm((L, D, 6 * D), 0.5 * D ** -0.5),
        'ada_b': nrm((L, 6 * D), 0.02),
        'norm_mix_pre': 1.0 + nrm((L, D), 0.02),
        'norm_mix_post': 1.0 + nrm((L, D), 0.02),
        'norm_ffn_pre': 1.0 + nrm((L, D), 0.02),
        'norm_ffn_post': 1.0 + nrm((L, D), 0.02),
        'w_in': nrm((L, D, D_IN), D ** -0.5),
        'conv_a': nrm((L, 3, A_WIDTH), 3 ** -0.5),
        'na_bias': nrm((L, NA_HEADS, 2 * NA_WIN_R - 1, 2 * NA_WIN_C - 1), 0.1),
        'q_norm': 1.0 + nrm((L, HEAD_DIM), 0.02),
        'k_norm': 1.0 + nrm((L, HEAD_DIM), 0.02),
        'rw_mu': unif((L, 2, RW_SHIFT), 0.0, 1.0),
        'rw_w0': unif((L, 2, RW), -6.5, -1.5),
        'rw_w2': nrm((L, 2, LORA_W, RW), 0.1 * LORA_W ** -0.5),
        'rw_a0': nrm((L, 2, RW), 0.1),
        'rw_a2': nrm((L, 2, LORA_A, RW), 0.5 * LORA_A ** -0.5),
        'rw_kk': 0.85 + nrm((L, RW), 0.05),
        'rw_ka': 1.0 + nrm((L, RW), 0.05),
        'rw_rk': nrm((L, RWKV_HEADS, HEAD_DIM), 0.1),
        'rw_g2': nrm((L, LORA_G, RW), LORA_G ** -0.5),
        'rw_ln_w': 1.0 + nrm((L, RW), 0.02),
        'rw_ln_b': nrm((L, RW), 0.02),
        'w_branch': nrm((L, N_BRANCH, BRANCH_W, D), BRANCH_W ** -0.5),
        'w_gate': nrm((L, D, N_BRANCH * D), D ** -0.5),
        'b_gate': nrm((L, N_BRANCH * D), 0.02),
        'w_o': nrm((L, D, D), D ** -0.5),
        'ffn_up': nrm((L, D, 2 * D_FF), D ** -0.5),
        'ffn_conv': nrm((L, 3, 2 * D_FF), 3 ** -0.5),
        'ffn_down': nrm((L, D_FF, D), D_FF ** -0.5),
    }

def reference(x, c, ctx, c_ctx, ada_w, ada_b, norm_mix_pre, norm_mix_post, norm_ffn_pre, norm_ffn_post,
              w_in, conv_a, na_bias, q_norm, k_norm, rw_mu, rw_w0, rw_w2, rw_a0, rw_a2, rw_kk, rw_ka, rw_rk,
              rw_g2, rw_ln_w, rw_ln_b, w_branch, w_gate, b_gate, w_o, ffn_up, ffn_conv, ffn_down):
    n_lat = x.shape[1]
    rows = n_lat // GRID_W
    cos, sin = axial_rope_tables(n_lat)
    key_idx, bias_idx = na_tables(rows)
    e1 = COLS_A
    e2 = COLS_A + COLS_NA
    e3 = COLS_A + COLS_NA + COLS_GQA
    xl, xc = x, ctx
    for l in range(DEPTH):
        with_ctx = l < DEPTH - 1
        mod_l = jnp.split((jax.nn.silu(c) @ ada_w[l] + ada_b[l])[:, None, :], 6, axis=-1)
        mod_c = jnp.split(jax.nn.silu(c_ctx) @ ada_w[l] + ada_b[l], 6, axis=-1)
        hl = modulate(rmsnorm(xl, norm_mix_pre[l]), mod_l[0], mod_l[1])
        hc = modulate(rmsnorm(xc, norm_mix_pre[l]), mod_c[0], mod_c[1])
        zl = hl @ w_in[l]
        zc = hc @ w_in[l]
        ya_l = mixer_a(zl[..., :e1], conv_a[l])
        yb_c, yb_l = mixer_b(zc[..., e1:e2], zl[..., e1:e2], na_bias[l], key_idx, bias_idx, with_ctx)
        yc_c, yc_l = mixer_c(zc[..., e2:e3], zl[..., e2:e3], q_norm[l], k_norm[l], cos, sin, with_ctx)
        yd_c, yd_l = mixer_d(zc[..., e3:], zl[..., e3:], rw_mu[l], rw_w0[l], rw_w2[l], rw_a0[l], rw_a2[l],
                             rw_kk[l], rw_ka[l], rw_rk[l], rw_g2[l], rw_ln_w[l], rw_ln_b[l], with_ctx)
        m_l = merge_branches(hl, (ya_l, yb_l, yc_l, yd_l), w_branch[l], w_gate[l], b_gate[l], w_o[l])
        xl = xl + mod_l[2] * rmsnorm(m_l, norm_mix_post[l])
        f_l = conv_ffn(modulate(rmsnorm(xl, norm_ffn_pre[l]), mod_l[3], mod_l[4]), ffn_up[l], ffn_conv[l], ffn_down[l])
        xl = xl + mod_l[5] * rmsnorm(f_l, norm_ffn_post[l])
        if with_ctx:
            ya_c = mixer_a(zc[..., :e1], conv_a[l])
            m_c = merge_branches(hc, (ya_c, yb_c, yc_c, yd_c), w_branch[l], w_gate[l], b_gate[l], w_o[l])
            xc = xc + mod_c[2] * rmsnorm(m_c, norm_mix_post[l])
            f_c = conv_ffn(modulate(rmsnorm(xc, norm_ffn_pre[l]), mod_c[3], mod_c[4]), ffn_up[l], ffn_conv[l], ffn_down[l])
            xc = xc + mod_c[5] * rmsnorm(f_c, norm_ffn_post[l])
    return xl


_drawn_inputs = setup_inputs


def setup_inputs(seed=0):
    import zlib

    import numpy as np

    out = dict(_drawn_inputs(seed))
    spreads = {}
    factors = {'norm_mix_pre': 3.723,
     'norm_mix_post': 6.622,
     'norm_ffn_pre': 4.966,
     'norm_ffn_post': 6.781,
     'na_bias': 57.782,
     'q_norm': 33.364,
     'k_norm': 28.719,
     'rw_w2': 57.715,
     'rw_a0': 8.0,
     'rw_kk': 30.665,
     'rw_ka': 4.247,
     'rw_ln_w': 64.0,
     'rw_ln_b': 64.0,
     'b_gate': 8.0}
    for name, (base, spread) in spreads.items():
        noise = np.random.default_rng([zlib.crc32(name.encode()), seed]).standard_normal(out[name].shape)
        drawn = base * np.exp(spread * noise) if base else spread * noise
        out[name] = jnp.asarray(drawn.astype(out[name].dtype))
    for name, factor in factors.items():
        out[name] = (out[name] * factor).astype(out[name].dtype)
    return out
```

```python
from contextlib import ExitStack

import numpy as np
import concourse.bass as bass
from concourse import mybir

F32 = mybir.dt.float32
ALU = mybir.AluOpType
ACT = mybir.ActivationFunctionType
AX = mybir.AxisListType.X

P = 128
LAYERS = 2
DM = 1024
KT = DM // P
CTX = 256
LAT = 256
T = CTX + LAT
GRID_W = 64
WIN_R, WIN_C = 8, 16
ZT = 24
DFF = 2816
FT = DFF // P
HD = 64
HEADS = 4
CH = 64
NCH = T // CH
NB = T // P
LEVELS = (2, 4, 8, 16, 32)
EPS = 1e-6
LN_EPS = 64e-5
DECAY = float(np.exp(-0.5))
MASKED = -1e30
BIAS_C = 2 * WIN_C - 1
BIAS_N = (2 * WIN_R - 1) * BIAS_C

Z_BG, Z_CG, Z_XIN = 0, 2, 4
Z_NQ, Z_NK, Z_NV = 6, 8, 10
Z_GQ, Z_GK, Z_GV = 12, 14, 15
Z_R, Z_K, Z_V, Z_LORA, Z_G = 16, 18, 20, 22, 23
ACT_Z = [t for t in range(ZT) if t % 2 == 0 or t == Z_NQ + 1]
DVE_Z = [t for t in range(ZT) if t not in ACT_Z]
LATENT_ONLY = {0, 1, 2, 3, 4, 5, 6, 7, 12, 13, 23}

VEC_COLS = [("mix_pre", 8), ("mix_post", 8), ("ffn_pre", 8), ("ffn_post", 8), ("ada_b", 48), ("conv_a", 6),
            ("q_norm", 1), ("k_norm", 1), ("mu", 14), ("w0", 4), ("a0", 4), ("kk", 2), ("ka", 2), ("rk", 2),
            ("ln_w", 2), ("ln_b", 2), ("b_gate", 32), ("ffn_conv", 132)]
VEC = {}
_at = 0
for _n, _c in VEC_COLS:
    VEC[_n] = _at
    _at += _c
NVEC = _at

CONST_COLS = [("ident", P), ("ones", P), ("heads", P), ("swap", P), ("lm", 2 * P), ("m1", P), ("m1t", P),
              ("m2", P), ("m4", P), ("m8", P), ("m16", P), ("m32", P), ("cos", LAT), ("sin", LAT),
              ("reset", T), ("window", GRID_W)]
CON = {}
_at = 0
for _n, _c in CONST_COLS:
    CON[_n] = _at
    _at += _c
NCON = _at

RING = 6
SLOT_N = 256
NBANK = 8


def constants():
    p = np.arange(P)
    c = np.zeros((P, NCON), np.float32)

    def put(name, a):
        c[:, CON[name]:CON[name] + a.shape[1]] = a

    put("ident", np.eye(P))
    put("ones", np.ones((P, P)))
    put("heads", (p[:, None] // HD == p[None, :] // HD).astype(np.float32))
    sw = np.zeros((P, P))
    ev = np.arange(0, P, 2)
    sw[ev + 1, ev] = -1.0
    sw[ev, ev + 1] = 1.0
    put("swap", sw)
    s, t = p[:, None], p[None, :]
    same = s // CH == t // CH
    put("lm", np.concatenate([same & (s < t), same & (s <= t)], 1).astype(np.float32))
    m1 = (s % 2 == 1) & (t == s - 1)
    put("m1", m1)
    put("m1t", m1.T)
    for z in LEVELS:
        put(f"m{z}", ((s // z) % 2 == 1) & (t // z == s // z - 1))
    tok = np.arange(LAT)
    n_freq = HD // 4
    inv = (np.float32(10000.0) ** (-np.arange(n_freq, dtype=np.float32) / np.float32(n_freq))).astype(np.float32)
    row, col = (tok // GRID_W).astype(np.float32), (tok % GRID_W).astype(np.float32)
    ang = np.concatenate([row[None, :] * inv[:, None], col[None, :] * inv[:, None]], 0)
    ang = ang[(p % HD) // 2]
    put("cos", np.cos(ang))
    put("sin", np.sin(ang))
    put("reset", np.broadcast_to((np.arange(T) % CH != 0).astype(np.float32), (P, T)))
    j, kc = GRID_W - 1 - p[:, None] % GRID_W, np.arange(GRID_W)[None, :]
    cs = np.clip(j - WIN_C // 2, 0, GRID_W - WIN_C)
    put("window", np.where((kc >= cs) & (kc < cs + WIN_C), 0.0, MASKED))
    return c


def attention_units(l):
    tiles = range(4) if l == 0 else range(2, 4)
    return [(g, h, q) for g in "BC" for h in range(HEADS) for q in tiles]


def job_list():
    jobs = []
    for l in range(LAYERS):
        jobs += [("mod", l, n) for n in range(24)]
        jobs += [("ss", l, 0)]
        jobs += [("z", l, t) for t in range(ZT)]
        jobs += [("vt", l, i) for i in range(3)]
        jobs += [("qss", l, i) for i in range(3)]
        jobs += [("qsw", l, i) for i in range(3)]
        n = len(attention_units(l))
        for i in range(n + 2):
            if i < n:
                jobs.append(("S", l, i))
            if 1 <= i <= n:
                jobs.append(("T", l, i - 1))
            if i >= 2:
                jobs.append(("PV", l, i - 2))
        for d in range(2):
            jobs += [(k, l, d, p) for p in range(2) for k in ("wl", "al")]
            jobs += [("kss", l, d, p) for p in range(2)]
            jobs += [("bon", l, d, p) for p in range(2)]
            for h in range(HEADS):
                jobs += [("LM1", l, d, h, b) for b in range(2)]
                jobs += [("L1", l, d, h)]
                jobs += [("LM2", l, d, h, b) for b in range(2)]
            for s in LEVELS:
                jobs += [("sx", l, d, s, h) for h in range(HEADS)]
                for h in range(HEADS):
                    if s != LEVELS[-1]:
                        jobs += [("sy", l, d, s, h)]
                    jobs += [("syt", l, d, s, h)]
            jobs += [("tok", l, d, m, p) for m in "akbv" for p in range(2)]
            jobs += [("xv", l, d, p) for p in range(2)]
            jobs += [("at", l, d, p) for p in range(2)]
            jobs += [("u0", l, d, p) for p in range(2)]
            for c in range(NCH):
                jobs += [("cu", l, d, c)]
                if c < NCH - 1:
                    jobs += [("ch", l, d, c)]
                if l == 0 or c >= NCH // 2:
                    jobs += [("cy", l, d, c)]
        for k in ("mean", "var", "g2"):
            jobs += [(k, l, p) for p in range(2)]
        for J in range(4):
            for i in range(4):
                for j in (2 * J, 2 * J + 1):
                    jobs += [("gate", l, j, i), ("br", l, j, i)]
        jobs += [("wo", l, j) for j in range(8)]
        jobs += [("ss", l, 1), ("ss", l, 2)]
        for J in range(FT // 2):
            for j in (2 * J, 2 * J + 1):
                jobs += [("up", l, j, 0), ("up", l, j, 1)]
        jobs += [("down", l, j) for j in range(8)]
        jobs += [("ss", l, 3)]
    return {name: g for g, name in enumerate(jobs)}


JOB = job_list()


def slot_list():
    slots = []
    for l in range(LAYERS):
        slots += [("ada", l, n) for n in range(24)]
        slots += [("w_in", l, n) for n in range(ZT // 2)]
        for J in range(4):
            slots += [("branch", l, J)] + [("gate", l, J, i) for i in range(4)]
        slots += [("w_o", l, J) for J in range(4)]
        for J in range(FT // 2):
            slots += [("up", l, J, 0), ("up", l, J, 1)]
        for J in range(4):
            slots += [("down", l, J, q) for q in range(3)]
    return {name: n for n, name in enumerate(slots)}


SLOT = slot_list()


def last_user(name):
    k, l = name[:2]
    if k == "ada":
        return ("mod", l, name[2])
    if k == "w_in":
        return ("z", l, 2 * name[2] + 1)
    if k == "branch":
        return ("br", l, 2 * name[2] + 1, 3)
    if k == "gate":
        return ("gate", l, 2 * name[2] + 1, name[3])
    if k == "w_o":
        return ("wo", l, 2 * name[2] + 1)
    if k == "up":
        return ("up", l, 2 * name[2] + 1, name[3])
    return ("down", l, 2 * name[2] + 1)


def build(nc, a, out):
    ctx = ExitStack()
    with ctx:
        def sb(name, shape):
            return ctx.enter_context(nc.sbuf_tensor(name, shape, F32))

        def sem(name):
            return ctx.enter_context(nc.semaphore(name))

        con = sb("con", [P, NCON])
        vec = sb("vec", [P, LAYERS * NVEC])
        w2a2 = sb("w2a2", [P, 2, 256])
        g2 = sb("g2", [P, 256])
        bm = sb("bm", [P, HEADS, 6, GRID_W])
        ring = sb("ring", [P, RING, KT, SLOT_N])
        X = sb("X", [P, KT, T])
        H = sb("H", [P, KT, T])
        Z = sb("Z", [P, ZT, T])
        YB = sb("YB", [P, KT, T])
        ACC = sb("ACC", [P, KT, T])
        E = sb("E", [P, 5120])
        cvec = sb("cvec", [P, KT, 2])
        mod = sb("mod", [P, 48, 2])
        amod = sb("amod", [P, 4, 8, 2])
        omu = sb("omu", [P, 14])
        oka = sb("oka", [P, 2])
        eps = sb("eps", [P, 2])
        rs = sb("rs", [P, T])
        rt = sb("rt", [P, T])
        stat = sb("stat", [P, 3, 4])
        ps = ctx.enter_context(nc.psum_tensor("ps", [P, NBANK, 512], F32))
        xsave = nc.dram_tensor("xsave", [DM, T], F32, kind="Internal").ap()

        def K(name, n=P):
            return con[:, CON[name]:CON[name] + n]

        def vc(l, name, i=0, n=1):
            o = l * NVEC + VEC[name] + i
            return vec[:, o:o + n]

        def flat(t):
            return t[:, :, :].rearrange("p a b -> p (a b)")

        Ef, Zf, ACCf, Xf = E, flat(Z), flat(ACC), flat(X)

        def view(f, o, *dims):
            n = int(np.prod(dims))
            v = f[:, o:o + n]
            if len(dims) == 2:
                return v.rearrange("p (a b) -> p a b", a=dims[0])
            if len(dims) == 3:
                return v.rearrange("p (a b c) -> p a b c", a=dims[0], b=dims[1])
            if len(dims) == 4:
                return v.rearrange("p (a b c d) -> p a b c d", a=dims[0], b=dims[1], c=dims[2])
            return v

        nu = rt[:, 256:512].rearrange("p (h n) -> p h n", h=HEADS)
        state = rs[:, :].rearrange("p (b a n) -> p b a n", b=2, a=2)
        wend = rt[:, 0:16].rearrange("p (a c) -> p a c", a=2)
        vB = view(Ef, 0, 4, 256)
        vC = view(Ef, 1024, 4, 128)
        sbuf2 = view(ACCf, 0, 2, 512)
        prob = view(ACCf, 1024, 2, 512)
        probT = view(ACCf, 2048, 2, 4, 128)
        qtmp = view(ACCf, 3072, 512)
        qtmp2 = view(ACCf, 3584, 512)
        ar = view(Ef, 0, 2, NB, 2, P)
        betaT = view(Ef, 2048, 2, T)
        kapT = view(Ef, 3072, 2, T)
        bon = view(Ef, 4096, 2, T)
        LM1 = view(ACCf, 0, HEADS, NB, 2 * P)
        LM2 = view(Xf, 0, HEADS, NB, 2 * P)
        TT = view(Zf, 0, HEADS, NB, P)
        TN = view(Zf, 2048, HEADS, NB, P)
        XS = view(Zf, 4096, HEADS, NB, P)
        vT = view(Zf, 6144, 2, T)
        AT = view(Zf, 7168, 2, T)
        zr, zk, sg, aa = (view(ACCf, 1024 * i, 2, T) for i in range(4))
        G, kk, t1, t2 = (view(Xf, 1024 * i, 2, T) for i in range(4))
        wdec, winv = (view(Zf, 2048 + 1024 * i, 2, T) for i in range(2))
        wprev = view(Zf, 4096, 2, T)
        lora = view(Zf, 5120, T)
        tokm = {m: view(Zf, 2048 + 1024 * i, NB, 256) for i, m in enumerate("abkv")}
        XV = view(Ef, 2048, HEADS, NB, HD)
        U0 = view(Ef, 3072, HEADS, NB, HD)
        SQ = {0: ACC, 1: Z, 2: Z, 3: ACC}
        siglg = view(Zf, Z_G * T, T)

        const_in = sem("const_in")
        small_in = [sem("small_in0"), sem("small_in1")]
        x_in = sem("x_in")
        x_saved = sem("x_saved")
        x_back = sem("x_back")
        w_in_slot = [sem(f"w_slot{i}") for i in range(RING)]
        mm_done = sem("mm_done")
        bank_free = [sem(f"bank_free{i}") for i in range(NBANK)]
        silu_c = sem("silu_c")
        setup = sem("setup")
        sq_ready = sem("sq_ready")
        h_half = sem("h_half")
        h_ready = sem("h_ready")
        x_ready = sem("x_ready")
        ya_ready = sem("ya_ready")
        qsq_ready = sem("qsq_ready")
        qn_ready = sem("qn_ready")
        qk_ready = sem("qk_ready")
        q_scaled = sem("q_scaled")
        nmax_ready = sem("nmax_ready")
        p_ready = sem("p_ready")
        shift_half = sem("shift_half")
        shift_done = sem("shift_done")
        tanh_done = sem("tanh_done")
        kraw_done = sem("kraw_done")
        ksq_done = sem("ksq_done")
        scan_done = sem("scan_done")
        decay_done = sem("decay_done")
        bonus_in = sem("bonus_in")
        streams_done = sem("streams_done")
        t_done = sem("t_done")
        kroot_done = sem("kroot_done")
        ln_sq = sem("ln_sq")
        lg_done = sem("lg_done")
        gated = sem("gated")
        conv_half = sem("conv_half")
        silu_done = sem("silu_done")
        u_ready = sem("u_ready")
        act_chain = sem("act_chain")
        dve_chain = sem("dve_chain")
        pool_chain = sem("pool_chain")
        stored = sem("stored")

        def bank(name):
            return ps[:, JOB[name] % NBANK, :]

        def filled(eng, name):
            eng.wait_ge(mm_done, JOB[name] + 1)
            return bank(name)

        def frees(name):
            return bank_free[JOB[name] % NBANK]

        def emptied(eng, name):
            eng.wait_ge(frees(name), JOB[name] // NBANK + 1)

        def cols(l, t=None):
            if l == 0 or (t is not None and t not in LATENT_ONLY):
                return 0, T
            return CTX, T

        def streams(l):
            return (0, 1) if l == 0 else (1,)

        def norm_no(l, k):
            return 4 * l + k

        def added(l, j, i):
            return 24 * l + 6 * (j // 2) + 2 * (i - 1) + j % 2 + 1

        def grid_rows(v):
            return v.rearrange("p (r j) -> p r j", j=GRID_W)

        UNITS = [attention_units(l) for l in range(LAYERS)]
        UBASE = [0, len(UNITS[0])]

        block = ctx.enter_context(nc.Block())

        @block.sync
        def _(sp):
            sp.dma_start(con[:, :], a["const"]).then_inc(const_in, 16)
            sp.dma_start(vec[:, :].rearrange("p (l n) -> p l n", l=LAYERS),
                         a["vecs"].rearrange("l p n -> p l n")).then_inc(const_in, 16)
            sp.dma_start(cvec[:, :, :], a["cs"].rearrange("(k p) s -> p k s", p=P)).then_inc(const_in, 16)
            sp.dma_start(X[:, :, :], a["xin"].rearrange("(k p) t -> p k t", p=P)).then_inc(x_in, 16)
            names = list(SLOT)
            for n, name in enumerate(names):
                if n >= RING:
                    sp.wait_ge(mm_done, JOB[last_user(names[n - RING])] + 1)
                k, l = name[:2]
                dst = ring[:, n % RING, :, :]
                if k == "ada":
                    src = a["ada_w"][l, :, name[2] * SLOT_N:(name[2] + 1) * SLOT_N]
                elif k == "w_in":
                    src = a["w_in"][l, :, name[2] * SLOT_N:(name[2] + 1) * SLOT_N]
                elif k == "branch":
                    src = a["w_branch"][l, :, name[2] * SLOT_N:(name[2] + 1) * SLOT_N]
                elif k == "gate":
                    o = name[3] * DM + name[2] * SLOT_N
                    src = a["w_gate"][l, :, o:o + SLOT_N]
                elif k == "w_o":
                    src = a["w_o"][l, :, name[2] * SLOT_N:(name[2] + 1) * SLOT_N]
                elif k == "up":
                    o = name[3] * DFF + name[2] * SLOT_N
                    src = a["ffn_up"][l, :, o:o + SLOT_N]
                else:
                    k0, k1 = 8 * name[3], min(8 * name[3] + 8, FT)
                    src = a["ffn_down"][l, k0 * P:k1 * P, name[2] * SLOT_N:(name[2] + 1) * SLOT_N]
                    dst = ring[:, n % RING, 0:k1 - k0, :]
                sp.dma_start(dst, src.rearrange("(k p) n -> p k n", p=P)).then_inc(w_in_slot[n % RING], 16)

        @block.gpsimd
        def _(pool):
            links = [0]

            def link(ins):
                links[0] += 1
                ins.then_inc(pool_chain, 1)
                pool.wait_ge(pool_chain, links[0])

            def load_small(l):
                pool.dma_start(w2a2[:, :, :], a["w2a2"][l]).then_inc(small_in[l], 16)
                pool.dma_start(g2[:, :], a["g2"][l]).then_inc(small_in[l], 16)
                nb = a["na_bias"]
                for h in range(HEADS):
                    for half in range(2):
                        src = bass.AP(nb.tensor,
                                      (l * HEADS + h) * BIAS_N + (5 - half) * BIAS_C + WIN_C - 1 - (GRID_W - 1),
                                      [[1, GRID_W], [BIAS_C, 6], [1, GRID_W]])
                        pool.dma_start(bm[half * HD:(half + 1) * HD, h, :, :], src).then_inc(small_in[l], 16)

            load_small(0)
            for l in range(LAYERS):
                c0, c1 = cols(l)
                ns = len(streams(l))
                if l == 1:
                    pool.wait_ge(mm_done, JOB[("g2", 0, 1)] + 1)
                    load_small(1)
                    pool.wait_ge(x_ready, 16)
                    pool.dma_start(xsave.rearrange("(k p) t -> p k t", p=P), X[:, :, :]).then_inc(x_saved, 16)
                for p in range(2):
                    for t in (Z_BG + p, Z_CG + p, Z_XIN + p):
                        emptied(pool, ("z", l, t))
                    xc = Z[:, Z_XIN + p, c0:c1]
                    cg = Z[:, Z_CG + p, c0:c1]
                    y = YB[:, p, c0:c1]
                    link(pool.tensor_tensor(xc, xc, cg, ALU.mult))
                    link(pool.tensor_scalar(y, xc, vc(l, "conv_a", 2 + p), None, ALU.mult))
                    xs = xc.rearrange("p (s t) -> p s t", s=ns)
                    ys = y.rearrange("p (s t) -> p s t", s=ns)
                    tm = cg.rearrange("p (s t) -> p s t", s=ns)
                    link(pool.tensor_scalar(tm[:, :, 0:255], xs[:, :, 0:255], vc(l, "conv_a", p), None, ALU.mult))
                    link(pool.tensor_tensor(ys[:, :, 1:256], ys[:, :, 1:256], tm[:, :, 0:255], ALU.add))
                    link(pool.tensor_scalar(tm[:, :, 0:255], xs[:, :, 1:256], vc(l, "conv_a", 4 + p), None, ALU.mult))
                    link(pool.tensor_tensor(ys[:, :, 0:255], ys[:, :, 0:255], tm[:, :, 0:255], ALU.add))
                    pool.tensor_tensor(y, y, Z[:, Z_BG + p, c0:c1], ALU.mult).then_inc(ya_ready, 1)
                pool.wait_ge(mm_done, JOB[("cy", l, 1, NCH - 1)] + 1)
                if l == 1:
                    pool.wait_ge(x_saved, 16)
                src = a["xin"] if l == 0 else xsave
                pool.dma_start(X[:, :, :], src.rearrange("(k p) t -> p k t", p=P)).then_inc(x_back, 16)
                for j in range(FT):
                    pool.wait_ge(silu_done, l * FT + j + 1)
                    u = Z[:, j, c0:c1]
                    pool.tensor_tensor(u, u, YB[:, 4 + j % 2, c0:c1], ALU.mult).then_inc(u_ready, 1)
            for i in range(KT):
                pool.wait_ge(x_ready, 24 + i + 1)
                pool.dma_start(out[i * P:(i + 1) * P, :], X[:, i, CTX:T]).then_inc(stored, 16)
            pool.wait_ge(stored, 16 * KT)

        @block.scalar
        def _(act):
            links = [0]

            def link(ins):
                links[0] += 1
                ins.then_inc(act_chain, 1)
                act.wait_ge(act_chain, links[0])

            sqs = [0]

            def square(dst, src):
                sqs[0] += 1
                act.activation(dst, src, ACT.Square).then_inc(sq_ready, 1)
                act.wait_ge(sq_ready, sqs[0])

            def norm_root(l, k):
                c0, c1 = cols(l) if k else (0, T)
                s = filled(act, ("ss", l, k))
                act.activation(rt[:, c0:c1], s[:, c0:c1], ACT.Sqrt, bias=eps[:, 0:1], scale=1.0 / DM)\
                   .then_inc(frees(("ss", l, k)), 1)

            def norm_finish(l, k, dst):
                no = 2 * l + k // 2
                shift = 0 if k == 0 else 24
                for i in range(KT):
                    act.wait_ge(h_half, 8 * no + i + 1)
                    ss = streams(l) if k else (0, 1)
                    for s in ss:
                        v = dst[:, i, 256 * s:256 * s + 256]
                        ins = act.activation(v, v, ACT.Identity, bias=mod[:, shift + i, s:s + 1],
                                             scale=amod[:, k, i, s:s + 1])
                        if s == 1:
                            ins.then_inc(h_ready, 1)

            act.wait_ge(const_in, 48)
            act.activation(cvec[:, :, :], cvec[:, :, :], ACT.Silu).then_inc(silu_c, 1)
            act.wait_ge(x_in, 16)
            act.wait_ge(setup, 1)
            for l in range(LAYERS):
                c0, c1 = cols(l)
                W = c1 - c0
                ns = len(streams(l))
                for i in range(KT):
                    if l == 1:
                        act.wait_ge(x_ready, 8 + i + 1)
                    square(ACC[:, i, :], X[:, i, :])
                norm_root(l, 0)
                norm_finish(l, 0, H)
                for t in ACT_Z:
                    z0, z1 = cols(l, t)
                    s = filled(act, ("z", l, t))
                    if t in (Z_NQ, Z_NQ + 1):
                        if l == 0:
                            act.activation(Z[:, t, 0:CTX], s[:, 0:CTX], ACT.Copy)
                        act.activation(grid_rows(Z[:, t, CTX:T]), grid_rows(s[:, CTX:T])[:, :, ::-1], ACT.Copy)\
                           .then_inc(frees(("z", l, t)), 1)
                    else:
                        act.activation(Z[:, t, z0:z1], s[:, z0:z1], ACT.Copy).then_inc(frees(("z", l, t)), 1)
                for i in range(3):
                    z0, z1 = cols(l, Z_GQ + i)
                    emptied(act, ("z", l, Z_GQ + i))
                    if i >= 2:
                        act.wait_ge(mm_done, JOB[("qss", l, i - 2)] + 1)
                    dst = (qtmp, qtmp2)[i % 2]
                    act.activation(dst[:, z0:z1], Z[:, Z_GQ + i, z0:z1], ACT.Square).then_inc(qsq_ready, 1)
                for i in range(3):
                    z0, z1 = cols(l, Z_GQ + i)
                    s = filled(act, ("qss", l, i))
                    if i:
                        act.wait_ge(qn_ready, 3 * l + i)
                    act.activation(rt[:, z0:z1], s[:, z0:z1], ACT.Sqrt, bias=eps[:, 0:1], scale=1.0 / HD)\
                       .then_inc(frees(("qss", l, i)), 1)
                units = UNITS[l]
                for i in range(len(units) + 1):
                    if i < len(units):
                        g, h, q = units[i]
                        nk = T if q >= 2 else CTX
                        s = bank(("S", l, i))
                        src = sbuf2[:, i % 2, 0:nk] if g == "B" and q >= 2 else s[:, 0:nk]
                        act.wait_ge(nmax_ready, UBASE[l] + i + 1)
                        act.activation(prob[:, i % 2, 0:nk], src, ACT.Exp, bias=stat[:, 0, i % 4:i % 4 + 1],
                                       accum_out=stat[:, 1, i % 4:i % 4 + 1]).then_inc(frees(("S", l, i)), 1)
                    if i >= 1:
                        u = i - 1
                        nk = T if units[u][2] >= 2 else CTX
                        s = filled(act, ("T", l, u))
                        if u >= 2:
                            act.wait_ge(mm_done, JOB[("PV", l, u - 2)] + 1)
                        act.activation(probT[:, u % 2, :, :].rearrange("p k q -> p (k q)")[:, 0:nk], s[:, 0:nk],
                                       ACT.Copy).then_inc(frees(("T", l, u)), 1)
                act.wait_ge(ya_ready, 2 * l + 2)
                act.wait_ge(mm_done, JOB[("PV", l, len(units) - 1)] + 1)
                if l == 1:
                    act.wait_ge(x_saved, 16)
                for d in range(2):
                    it = 2 * l + d
                    if d == 1:
                        act.wait_ge(mm_done, JOB[("cy", l, 0, NCH - 1)] + 1)
                    step = 1 if d == 0 else -1
                    dsts = [zr[:, 0, :], zr[:, 1, :], zk[:, 0, :], zk[:, 1, :], vT[:, 0, :], vT[:, 1, :], lora]
                    for i in range(7):
                        emptied(act, ("z", l, Z_R + i))
                        src = Z[:, Z_R + i, :].rearrange("p (s t) -> p s t", s=2)[:, :, ::step]
                        act.activation(dsts[i].rearrange("p (s t) -> p s t", s=2), src, ACT.Copy,
                                       scale=omu[:, 7 * d + i:7 * d + i + 1]).then_inc(shift_half, 1)
                    act.wait_ge(shift_done, 7 * it + 7)
                    act.activation(lora[0:HD, :], lora[0:HD, :], ACT.Tanh).then_inc(tanh_done, 1)
                    for p in range(2):
                        s = filled(act, ("wl", l, d, p))
                        act.activation(sg[:, p, :], s, ACT.Sigmoid, bias=vc(l, "w0", 2 * d + p))\
                           .then_inc(frees(("wl", l, d, p)), 1)
                        s = filled(act, ("al", l, d, p))
                        act.activation(aa[:, p, :], s, ACT.Sigmoid, bias=vc(l, "a0", 2 * d + p))\
                           .then_inc(frees(("al", l, d, p)), 1)
                    for p in range(2):
                        act.wait_ge(kraw_done, 2 * it + p + 1)
                        act.activation(t1[:, p, :], kk[:, p, :], ACT.Square).then_inc(ksq_done, 1)
                    for p in range(2):
                        act.wait_ge(scan_done, 4 * it + 2 * p + 2)
                        link(act.activation(wdec[:, p, :], G[:, p, :], ACT.Exp, scale=-DECAY))
                        link(act.activation(winv[:, p, :], G[:, p, :], ACT.Exp, scale=DECAY))
                        act.activation(wprev[:, p, :], t2[:, p, :], ACT.Exp, scale=-DECAY).then_inc(decay_done, 1)
                    for p in range(2):
                        emptied(act, ("kss", l, d, p))
                        act.activation(t2[:, p, :], t2[:, p, :], ACT.Sqrt).then_inc(kroot_done, 1)
                    for m in "akbv":
                        for p in range(2):
                            s = filled(act, ("tok", l, d, m, p))
                            act.activation(tokm[m][:, :, 128 * p:128 * p + 128],
                                           s.rearrange("p (b n) -> p b n", b=NB), ACT.Copy)\
                               .then_inc(frees(("tok", l, d, m, p)), 1)
                    for p in range(2):
                        s = filled(act, ("xv", l, d, p))
                        act.activation(XV[:, 2 * p:2 * p + 2, :, :].rearrange("p h b n -> p (h b n)"), s, ACT.Copy)\
                           .then_inc(frees(("xv", l, d, p)), 1)
                    for p in range(2):
                        s = filled(act, ("at", l, d, p))
                        act.activation(AT[:, p, :], s, ACT.Copy).then_inc(frees(("at", l, d, p)), 1)
                    for p in range(2):
                        s = filled(act, ("u0", l, d, p))
                        act.activation(U0[:, 2 * p:2 * p + 2, :, :].rearrange("p h b n -> p (h b n)"), s, ACT.Copy)\
                           .then_inc(frees(("u0", l, d, p)), 1)
                for p in range(2):
                    emptied(act, ("mean", l, p))
                    act.activation(ACC[:, p, c0:c1], YB[:, 6 + p, c0:c1], ACT.Square)\
                       .then_inc(ln_sq, 1)
                act.activation(siglg[:, c0:c1], siglg[:, c0:c1], ACT.Sigmoid).then_inc(lg_done, 1)
                for p in range(2):
                    s = filled(act, ("var", l, p))
                    act.activation(ACC[:, 2 + p, c0:c1], s[:, c0:c1], ACT.Sqrt, bias=eps[:, 1:2], scale=1.0 / HD)\
                       .then_inc(frees(("var", l, p)), 1)
                for J in range(4):
                    for i in range(4):
                        for j in (2 * J, 2 * J + 1):
                            no = 8 * J + 2 * i + (j - 2 * J)
                            s = filled(act, ("gate", l, j, i))
                            if i >= 2:
                                act.wait_ge(gated, added(l, j, i - 1))
                            elif i == 1:
                                emptied(act, ("br", l, j, 0))
                            elif J:
                                act.wait_ge(gated, added(l, j - 2, 3))
                            act.activation((rt, rs)[no % 2][:, c0:c1], s[:, c0:c1], ACT.Sigmoid,
                                           bias=vc(l, "b_gate", 8 * i + j))\
                               .then_inc(frees(("gate", l, j, i)), 1)
                for j in range(KT):
                    s = filled(act, ("wo", l, j))
                    act.activation(H[:, j, c0:c1], s[:, c0:c1], ACT.Copy).then_inc(frees(("wo", l, j)), 1)
                    emptied(act, ("wo", l, j))
                    square(Z[:, j, c0:c1], H[:, j, c0:c1])
                norm_root(l, 1)
                for i in range(KT):
                    act.wait_ge(x_ready, 16 * l + i + 1)
                    square(Z[:, i, c0:c1], X[:, i, c0:c1])
                norm_root(l, 2)
                norm_finish(l, 2, ACC)
                for j in range(FT):
                    for g in range(2):
                        s = filled(act, ("up", l, j, g))
                        if g == 0:
                            dst = Z[:, j, c0:c1]
                        else:
                            if j >= 2:
                                act.wait_ge(u_ready, l * FT + j - 1)
                            dst = YB[:, 4 + j % 2, c0:c1]
                        act.activation(dst, s[:, c0:c1], ACT.Copy, scale=vc(l, "ffn_conv", 44 + 22 * g + j))\
                           .then_inc(conv_half, 1)
                    emptied(act, ("up", l, j, 1))
                    act.activation(dst, dst, ACT.Silu).then_inc(silu_done, 1)
                for j in range(KT):
                    s = filled(act, ("down", l, j))
                    act.activation(H[:, j, c0:c1], s[:, c0:c1], ACT.Copy).then_inc(frees(("down", l, j)), 1)
                    emptied(act, ("down", l, j))
                    if j == 0:
                        act.wait_ge(mm_done, JOB[("up", l, FT - 1, 1)] + 1)
                    square(ACC[:, j, c0:c1], H[:, j, c0:c1])
                norm_root(l, 3)

        @block.vector
        def _(dve):
            links = [0]

            def link(ins):
                links[0] += 1
                ins.then_inc(dve_chain, 1)
                dve.wait_ge(dve_chain, links[0])

            def root_inverse(l, k):
                c0, c1 = cols(l) if k else (0, T)
                emptied(dve, ("ss", l, k))
                link(dve.reciprocal(rs[:, c0:c1], rt[:, c0:c1]))

            def norm_apply(l, k, src, dst):
                root_inverse(l, k)
                c0, c1 = cols(l) if k else (0, T)
                for i in range(KT):
                    dve.tensor_tensor(dst[:, i, c0:c1], src[:, i, c0:c1], rs[:, c0:c1], ALU.mult).then_inc(h_half, 1)

            def residual(l, k):
                root_inverse(l, k)
                c0, c1 = cols(l)
                for i in range(KT):
                    link(dve.tensor_tensor(H[:, i, c0:c1], H[:, i, c0:c1], rs[:, c0:c1], ALU.mult))
                    for s in streams(l):
                        x = X[:, i, 256 * s:256 * s + 256]
                        ins = dve.scalar_tensor_tensor(x, H[:, i, 256 * s:256 * s + 256], amod[:, k, i, s:s + 1], x,
                                                       ALU.mult, ALU.add)
                        if s == 1:
                            ins.then_inc(x_ready, 1)

            link(dve.memset(eps[:, 0:1], EPS))
            dve.memset(eps[:, 1:2], LN_EPS).then_inc(setup, 1)
            dve.wait_ge(const_in, 48)
            for l in range(LAYERS):
                c0, c1 = cols(l)
                W = c1 - c0
                ns = len(streams(l))
                for n in range(24):
                    s = filled(dve, ("mod", l, n))
                    b = vc(l, "ada_b", 2 * n, 2).unsqueeze(2).to_broadcast([P, 2, 2])
                    dve.tensor_tensor(mod[:, 2 * n:2 * n + 2, :], s[:, 0:4].rearrange("p (a s) -> p a s", a=2), b,
                                      ALU.add).then_inc(frees(("mod", l, n)), 1)
                for n in range(16, 24):
                    emptied(dve, ("mod", l, n))
                for k, (m, g) in enumerate(((8, "mix_pre"), (16, "mix_post"), (32, "ffn_pre"), (40, "ffn_post"))):
                    gb = vc(l, g, 0, 8).unsqueeze(2).to_broadcast([P, 8, 2])
                    if k % 2 == 0:
                        link(dve.scalar_tensor_tensor(amod[:, k, :, :], mod[:, m:m + 8, :], 1.0, gb, ALU.add, ALU.mult))
                    else:
                        link(dve.tensor_tensor(amod[:, k, :, :], mod[:, m:m + 8, :], gb, ALU.mult))
                link(dve.tensor_scalar(omu[:, :], vc(l, "mu", 0, 14), -1.0, 1.0, ALU.mult, ALU.add))
                link(dve.tensor_scalar(oka[:, :], vc(l, "ka", 0, 2), -1.0, 1.0, ALU.mult, ALU.add))
                norm_apply(l, 0, X, H)
                dve.wait_ge(small_in[l], 16 * 10)
                win = K("window", GRID_W).unsqueeze(1).to_broadcast([P, HEADS * 6, GRID_W])
                bmf = bm[:, :, :, :].rearrange("p h r c -> p (h r) c")
                link(dve.tensor_tensor(bmf, bmf, win, ALU.add))
                for t in DVE_Z:
                    z0, z1 = cols(l, t)
                    s = filled(dve, ("z", l, t))
                    dve.tensor_copy(Z[:, t, z0:z1], s[:, z0:z1]).then_inc(frees(("z", l, t)), 1)
                for i in range(3):
                    s = filled(dve, ("vt", l, i))
                    dst = vB[:, :, 128 * i:128 * i + 128] if i < 2 else vC
                    dve.tensor_copy(dst, s.rearrange("p (b n) -> p b n", b=4)).then_inc(frees(("vt", l, i)), 1)
                for p in range(2):
                    z0, z1 = cols(l, Z_NQ + p)
                    emptied(dve, ("z", l, Z_NQ + p))
                    v = Z[:, Z_NQ + p, z0:z1]
                    dve.tensor_scalar(v, v, HD ** -0.5, None, ALU.mult).then_inc(q_scaled, 1)
                for i in range(3):
                    z0, z1 = cols(l, Z_GQ + i)
                    emptied(dve, ("qss", l, i))
                    link(dve.reciprocal(rs[:, z0:z1], rt[:, z0:z1]))
                    v = Z[:, Z_GQ + i, z0:z1]
                    g = vc(l, "q_norm") if i < 2 else vc(l, "k_norm")
                    if i < 2:
                        link(dve.tensor_scalar(v, v, g, HD ** -0.5, ALU.mult, ALU.mult))
                        dve.tensor_tensor(v, v, rs[:, z0:z1], ALU.mult).then_inc(qn_ready, 1)
                    else:
                        dve.scalar_tensor_tensor(v, v, g, rs[:, z0:z1], ALU.mult, ALU.mult).then_inc(qn_ready, 1)
                for i in range(3):
                    v = Z[:, Z_GQ + i, CTX:T]
                    s = filled(dve, ("qsw", l, i))
                    dve.wait_ge(mm_done, JOB[("qss", l, 2)] + 1)
                    dve.tensor_tensor(qtmp[:, 0:LAT], s[:, 0:LAT], K("sin", LAT), ALU.mult)\
                       .then_inc(frees(("qsw", l, i)), 1)
                    dve.wait_ge(qn_ready, 3 * l + i + 1)
                    link(dve.tensor_tensor(v, v, K("cos", LAT), ALU.mult))
                    emptied(dve, ("qsw", l, i))
                    dve.tensor_tensor(v, v, qtmp[:, 0:LAT], ALU.add).then_inc(qk_ready, 1)
                    dve.wait_ge(qk_ready, 3 * l + i + 1)
                units = UNITS[l]
                for i in range(len(units) + 2):
                    if i < len(units):
                        g, h, q = units[i]
                        nk = T if q >= 2 else CTX
                        s = filled(dve, ("S", l, i))
                        src = s[:, 0:nk]
                        if g == "B" and q >= 2:
                            r0 = 2 if q == 2 else 0
                            if i >= 2:
                                emptied(dve, ("S", l, i - 2))
                            link(dve.tensor_copy(sbuf2[:, i % 2, 0:CTX], s[:, 0:CTX]))
                            link(dve.tensor_tensor(sbuf2[:, i % 2, CTX:T], s[:, CTX:T],
                                                   bm[:, h, r0:r0 + 4, :].rearrange("p r c -> p (r c)"), ALU.add))
                            src = sbuf2[:, i % 2, :]
                        dve.tensor_reduce(stat[:, 0, i % 4:i % 4 + 1], src, AX, ALU.max, negate=True)\
                           .then_inc(nmax_ready, 1)
                    if 1 <= i <= len(units):
                        u = i - 1
                        nk = T if units[u][2] >= 2 else CTX
                        emptied(dve, ("S", l, u))
                        link(dve.reciprocal(stat[:, 2, u % 4:u % 4 + 1], stat[:, 1, u % 4:u % 4 + 1]))
                        dve.tensor_scalar(prob[:, u % 2, 0:nk], prob[:, u % 2, 0:nk], stat[:, 2, u % 4:u % 4 + 1],
                                          None, ALU.mult).then_inc(p_ready, 1)
                    if i >= 2:
                        g, h, q = units[i - 2]
                        half = slice(HD * (h % 2), HD * (h % 2) + HD)
                        s = filled(dve, ("PV", l, i - 2))
                        dst = YB[half, (2 if g == "B" else 4) + h // 2, 128 * q:128 * q + 128]
                        src = s[half, 0:128]
                        if g == "B" and q >= 2:
                            dst, src = grid_rows(dst), grid_rows(src)[:, :, ::-1]
                        dve.tensor_copy(dst, src).then_inc(frees(("PV", l, i - 2)), 1)
                if l == 1:
                    dve.wait_ge(x_saved, 16)
                for d in range(2):
                    it = 2 * l + d
                    step = 1 if d == 0 else -1
                    dsts = [zr[:, 0, :], zr[:, 1, :], zk[:, 0, :], zk[:, 1, :], vT[:, 0, :], vT[:, 1, :], lora]
                    for i in range(7):
                        dve.wait_ge(shift_half, 7 * it + i + 1)
                        z = Z[:, Z_R + i, :].rearrange("p (s t) -> p s t", s=2)[:, :, ::step]
                        o = dsts[i].rearrange("p (s t) -> p s t", s=2)[:, :, 1:256]
                        dve.scalar_tensor_tensor(o, z[:, :, 0:255], vc(l, "mu", 7 * d + i), o, ALU.mult, ALU.add)\
                           .then_inc(shift_done, 1)
                    dve.wait_ge(shift_done, 7 * it + 7)
                    for p in range(2):
                        dve.tensor_scalar(kk[:, p, :], zk[:, p, :], vc(l, "kk", p), None, ALU.mult)\
                           .then_inc(kraw_done, 1)
                    for p in range(2):
                        emptied(dve, ("wl", l, d, p))
                        dve.tensor_tensor_scan(G[:, p, :], K("reset", T), sg[:, p, :], 0.0, ALU.mult, ALU.add)\
                           .then_inc(scan_done, 1)
                        dve.wait_ge(scan_done, 4 * it + 2 * p + 1)
                        dve.tensor_tensor(t2[:, p, :], G[:, p, :], sg[:, p, :], ALU.subtract).then_inc(scan_done, 1)
                    for p in range(2):
                        dve.wait_ge(decay_done, 2 * it + 2)
                        s = filled(dve, ("kss", l, d, p))
                        dve.tensor_scalar(t2[:, p, :], s, 1e-24, None, ALU.max).then_inc(frees(("kss", l, d, p)), 1)
                    for p in range(2):
                        emptied(dve, ("al", l, d, p))
                        link(dve.tensor_scalar(sg[:, p, :], aa[:, p, :], vc(l, "ka", p), oka[:, p:p + 1],
                                               ALU.mult, ALU.add))
                        link(dve.tensor_tensor(zk[:, p, :], zk[:, p, :], sg[:, p, :], ALU.mult))
                        dve.scalar_tensor_tensor(sg[:, p, :], zr[:, p, :], vc(l, "rk", p), zk[:, p, :],
                                                 ALU.mult, ALU.mult).then_inc(bonus_in, 1)
                        link(dve.tensor_tensor(kapT[:, p, :], zk[:, p, :], winv[:, p, :], ALU.mult))
                        blk = lambda v: v.rearrange("p (b t) -> p b t", b=NB)
                        link(dve.tensor_tensor(ar[:, p, :, 1, :], blk(zr[:, p, :]), blk(wdec[:, p, :]), ALU.mult))
                    for p in range(2):
                        dve.wait_ge(kroot_done, 2 * it + p + 1)
                        link(dve.reciprocal(t1[:, p, :], t2[:, p, :]))
                        link(dve.tensor_tensor(kk[:, p, :], kk[:, p, :], t1[:, p, :], ALU.mult))
                        link(dve.tensor_tensor(ar[:, p, :, 0, :], blk(kk[:, p, :]), blk(wprev[:, p, :]), ALU.mult))
                        link(dve.tensor_tensor(kk[:, p, :], kk[:, p, :], aa[:, p, :], ALU.mult))
                        link(dve.tensor_tensor(betaT[:, p, :], kk[:, p, :], winv[:, p, :], ALU.mult))
                    link(dve.tensor_copy(wend[:, :, :], wdec[:, :, CH - 1::CH]))
                    for p in range(2):
                        s = filled(dve, ("bon", l, d, p))
                        if d == 0:
                            dve.tensor_tensor(bon[:, p, :], s, vT[:, p, :], ALU.mult)\
                               .then_inc(frees(("bon", l, d, p)), 1)
                        else:
                            dve.tensor_tensor(t1[:, p, :], s, vT[:, p, :], ALU.mult)\
                               .then_inc(frees(("bon", l, d, p)), 1)
                            emptied(dve, ("bon", l, d, p))
                            rev = t1[:, p, :].rearrange("p (s t) -> p s t", s=2)[:, :, ::-1]
                            bo = bon[:, p, :].rearrange("p (s t) -> p s t", s=2)
                            link(dve.tensor_tensor(bo, bo, rev, ALU.add))
                    dve.memset(state[:, 0, :, :], 0.0).then_inc(streams_done, 1)
                    lm = K("lm", 2 * P).unsqueeze(1).to_broadcast([P, 2, 2 * P])
                    m1 = K("m1").unsqueeze(1).to_broadcast([P, NB, P])
                    m1t = K("m1t").unsqueeze(1).to_broadcast([P, NB, P])
                    idb = K("ident").unsqueeze(1).to_broadcast([P, NB, P])
                    for h in range(HEADS):
                        for b in range(2):
                            s = filled(dve, ("LM1", l, d, h, b)).rearrange("p (b n) -> p b n", b=2)
                            dve.tensor_tensor(LM1[:, h, 2 * b:2 * b + 2, :], s, lm, ALU.mult)\
                               .then_inc(frees(("LM1", l, d, h, b)), 1)
                        s = filled(dve, ("L1", l, d, h)).rearrange("p (b n) -> p b n", b=NB)
                        dve.tensor_tensor(TN[:, h, :, :], s, m1, ALU.mult).then_inc(frees(("L1", l, d, h)), 1)
                        emptied(dve, ("L1", l, d, h))
                        link(dve.tensor_tensor(TN[:, h, :, :], idb, TN[:, h, :, :], ALU.subtract))
                        for b in range(2):
                            emptied(dve, ("LM1", l, d, h, b))
                        link(dve.tensor_tensor(TT[:, h, :, :], LM1[:, h, :, 0:P], m1t, ALU.mult))
                        dve.tensor_tensor(TT[:, h, :, :], idb, TT[:, h, :, :], ALU.subtract).then_inc(t_done, 1)
                        for b in range(2):
                            s = filled(dve, ("LM2", l, d, h, b)).rearrange("p (b n) -> p b n", b=2)
                            dve.tensor_tensor(LM2[:, h, 2 * b:2 * b + 2, :], s, lm, ALU.mult)\
                               .then_inc(frees(("LM2", l, d, h, b)), 1)
                    for zi, z in enumerate(LEVELS):
                        mz = K(f"m{z}").unsqueeze(1).to_broadcast([P, NB, P])
                        for h in range(HEADS):
                            s = filled(dve, ("sx", l, d, z, h)).rearrange("p (b n) -> p b n", b=NB)
                            dve.tensor_tensor(XS[:, h, :, :], s, mz, ALU.mult).then_inc(frees(("sx", l, d, z, h)), 1)
                        for h in range(HEADS):
                            if z != LEVELS[-1]:
                                s = filled(dve, ("sy", l, d, z, h)).rearrange("p (b n) -> p b n", b=NB)
                                dve.tensor_tensor(TN[:, h, :, :], TN[:, h, :, :], s, ALU.subtract)\
                                   .then_inc(frees(("sy", l, d, z, h)), 1)
                            s = filled(dve, ("syt", l, d, z, h)).rearrange("p (b n) -> p b n", b=NB)
                            dve.tensor_tensor(TT[:, h, :, :], TT[:, h, :, :], s, ALU.subtract)\
                               .then_inc(frees(("syt", l, d, z, h)), 1)
                    for p in range(2):
                        emptied(dve, ("u0", l, d, p))
                    for c in range(NCH):
                        q = slice(HD * (c % 2), HD * (c % 2) + HD)
                        s = filled(dve, ("cu", l, d, c))
                        dve.scalar_tensor_tensor(nu[q, :, :], s[q, 0:256].rearrange("p (h n) -> p h n", h=HEADS),
                                                 -1.0, U0[q, :, c // 2, :], ALU.mult, ALU.subtract)\
                           .then_inc(frees(("cu", l, d, c)), 1)
                        if c < NCH - 1:
                            s = filled(dve, ("ch", l, d, c))
                            for p in range(2):
                                ins = dve.scalar_tensor_tensor(state[:, (c + 1) % 2, p, :], s[:, P * p:P * p + P],
                                                               wend[:, p, c:c + 1], K("heads"), ALU.mult, ALU.mult)
                            ins.then_inc(frees(("ch", l, d, c)), 1)
                        if l == 0 or c >= NCH // 2:
                            s = filled(dve, ("cy", l, d, c))[:, 0:128].rearrange("p (a t) -> p a t", a=2)
                            if d == 0:
                                dve.tensor_copy(YB[:, 6:8, CH * c:CH * c + CH], s)\
                                   .then_inc(frees(("cy", l, d, c)), 1)
                            else:
                                st, r = c // 4, c % 4
                                e = 256 * st + 256 - CH * r
                                y = YB[:, 6:8, e - CH:e]
                                dve.tensor_tensor(y, y, s[:, :, ::-1], ALU.add).then_inc(frees(("cy", l, d, c)), 1)
                for p in range(2):
                    y = YB[:, 6 + p, c0:c1]
                    s = filled(dve, ("mean", l, p))
                    dve.scalar_tensor_tensor(y, s[:, c0:c1], -1.0 / HD, y, ALU.mult, ALU.add)\
                       .then_inc(frees(("mean", l, p)), 1)
                for p in range(2):
                    y = YB[:, 6 + p, c0:c1]
                    r = ACC[:, 2 + p, c0:c1]
                    emptied(dve, ("var", l, p))
                    link(dve.reciprocal(ACC[:, 4 + p, c0:c1], r))
                    link(dve.scalar_tensor_tensor(y, y, vc(l, "ln_w", p), ACC[:, 4 + p, c0:c1], ALU.mult, ALU.mult))
                    link(dve.scalar_tensor_tensor(y, y, vc(l, "ln_b", p), bon[:, p, c0:c1], ALU.add, ALU.add))
                    s = filled(dve, ("g2", l, p))
                    dve.tensor_tensor(y, y, s[:, c0:c1], ALU.mult).then_inc(frees(("g2", l, p)), 1)
                for J in range(4):
                    for i in range(4):
                        for j in (2 * J, 2 * J + 1):
                            no = 8 * J + 2 * i + (j - 2 * J)
                            gt = (rt, rs)[no % 2][:, c0:c1]
                            s = filled(dve, ("br", l, j, i))[:, c0:c1]
                            emptied(dve, ("gate", l, j, i))
                            o = ACC[:, j, c0:c1]
                            dst = o if i == 0 else gt
                            dve.tensor_tensor(dst, gt, s, ALU.mult).then_inc(frees(("br", l, j, i)), 1)
                            emptied(dve, ("br", l, j, i))
                            if i:
                                dve.tensor_tensor(o, o, gt, ALU.add).then_inc(gated, 1)
                dve.wait_ge(x_back, 16 * (l + 1))
                residual(l, 1)
                dve.wait_ge(x_ready, 16 * l + 8)
                norm_apply(l, 2, X, ACC)
                for j in range(FT):
                    for g in range(2):
                        dve.wait_ge(conv_half, 2 * (FT * l + j) + g + 1)
                        s = bank(("up", l, j, g))[:, c0:c1].rearrange("p (s t) -> p s t", s=ns)
                        o = (Z[:, j, c0:c1] if g == 0 else YB[:, 4 + j % 2, c0:c1]).rearrange("p (s t) -> p s t", s=ns)
                        link(dve.scalar_tensor_tensor(o[:, :, 1:256], s[:, :, 0:255], vc(l, "ffn_conv", 22 * g + j),
                                                      o[:, :, 1:256], ALU.mult, ALU.add))
                        dve.scalar_tensor_tensor(o[:, :, 0:255], s[:, :, 1:256], vc(l, "ffn_conv", 88 + 22 * g + j),
                                                 o[:, :, 0:255], ALU.mult, ALU.add).then_inc(frees(("up", l, j, g)), 1)
                for j in range(KT):
                    emptied(dve, ("down", l, j))
                residual(l, 3)
                dve.wait_ge(x_ready, 16 * l + 16)

        @block.tensor
        def _(pe):
            def job(name):
                g = JOB[name]
                assert g == count[0], (name, g, count[0])
                if g >= NBANK:
                    pe.wait_ge(bank_free[g % NBANK], g // NBANK)
                return ps[:, g % NBANK, :]

            count = [0]

            def done(ins):
                count[0] += 1
                ins.then_inc(mm_done, 1)

            def weights(name):
                n = SLOT[name]
                pe.wait_ge(w_in_slot[n % RING], 16 * (n // RING + 1))
                return ring[:, n % RING, :, :]

            def sum_squares(l, k, src):
                c0, c1 = cols(l) if k else (0, T)
                o = job(("ss", l, k))
                for i in range(KT):
                    pe.wait_ge(sq_ready, 8 * norm_no(l, k) + i + 1)
                    last = pe.matmul(o[:, c0:c1], K("ones"), src[:, i, c0:c1], start=(i == 0), stop=(i == KT - 1))
                done(last)

            def project(name, w, jj, rhs, c0, c1, k0=0, kn=KT):
                o = job(name)
                for k in range(kn):
                    last = pe.matmul(o[:, c0:c1], w[:, k0 + k, 128 * jj:128 * jj + 128], rhs[:, k, c0:c1],
                                     start=(k == 0), stop=(k == kn - 1))
                done(last)

            pe.wait_ge(const_in, 48)
            for l in range(LAYERS):
                c0, c1 = cols(l)
                if l == 0:
                    pe.wait_ge(silu_c, 1)
                for n in range(24):
                    w = weights(("ada", l, n))
                    o = job(("mod", l, n))
                    for jj in range(2):
                        for k in range(KT):
                            last = pe.matmul(o[:, 2 * jj:2 * jj + 2], w[:, k, 128 * jj:128 * jj + 128], cvec[:, k, :],
                                             start=(k == 0), stop=(k == KT - 1))
                    done(last)
                sum_squares(l, 0, ACC)
                for k in range(KT):
                    pe.wait_ge(h_ready, 16 * l + k + 1)
                for t in range(ZT):
                    w = weights(("w_in", l, t // 2))
                    z0, z1 = cols(l, t)
                    project(("z", l, t), w, t % 2, H, z0, z1)
                for i in range(3):
                    t = Z_NV + i if i < 2 else Z_GV
                    emptied(pe, ("z", l, t))
                    o = job(("vt", l, i))
                    for b in range(4):
                        last = pe.transpose(o[:, 128 * b:128 * b + 128], Z[:, t, 128 * b:128 * b + 128], K("ident"))
                    done(last)
                for i in range(3):
                    z0, z1 = cols(l, Z_GQ + i)
                    o = job(("qss", l, i))
                    pe.wait_ge(qsq_ready, 3 * l + i + 1)
                    done(pe.matmul(o[:, z0:z1], K("heads"), (qtmp, qtmp2)[i % 2][:, z0:z1], start=True, stop=True))
                for i in range(3):
                    o = job(("qsw", l, i))
                    pe.wait_ge(qn_ready, 3 * l + i + 1)
                    done(pe.matmul(o[:, 0:LAT], K("swap"), Z[:, Z_GQ + i, CTX:T], start=True, stop=True))
                pe.wait_ge(q_scaled, 2 * l + 2)
                pe.wait_ge(qk_ready, 3 * l + 3)
                for p in range(2):
                    emptied(pe, ("z", l, Z_NK + p))
                for i in range(3):
                    emptied(pe, ("vt", l, i))
                units = UNITS[l]
                for i in range(len(units) + 2):
                    if i < len(units):
                        g, h, q = units[i]
                        nk = T if q >= 2 else CTX
                        if g == "B":
                            half, tq, tk = h % 2, Z_NQ + h // 2, Z_NK + h // 2
                        else:
                            half, tq, tk = h // 2, Z_GQ + h % 2, Z_GK
                        r = slice(HD * half, HD * half + HD)
                        o = job(("S", l, i))
                        done(pe.matmul(o[:, 0:nk], Z[r, tq, 128 * q:128 * q + 128], Z[r, tk, 0:nk],
                                       start=True, stop=True))
                    if 1 <= i <= len(units):
                        u = i - 1
                        nt = (T if units[u][2] >= 2 else CTX) // P
                        o = job(("T", l, u))
                        pe.wait_ge(p_ready, UBASE[l] + u + 1)
                        for b in range(nt):
                            last = pe.transpose(o[:, 128 * b:128 * b + 128], prob[:, u % 2, 128 * b:128 * b + 128],
                                                K("ident"))
                        done(last)
                    if i >= 2:
                        g, h, q = units[i - 2]
                        nt = (T if q >= 2 else CTX) // P
                        o = job(("PV", l, i - 2))
                        emptied(pe, ("T", l, i - 2))
                        half = slice(HD * (h % 2), HD * (h % 2) + HD)
                        for b in range(nt):
                            v = vB[:, b, HD * h:HD * h + HD] if g == "B" else vC[:, b, HD * (h // 2):HD * (h // 2) + HD]
                            last = pe.matmul(o[half, 0:128], v, probT[:, (i - 2) % 2, b, :],
                                             start=(b == 0), stop=(b == nt - 1))
                        done(last)
                for d in range(2):
                    it = 2 * l + d
                    pe.wait_ge(small_in[l], 16 * 10)
                    for p in range(2):
                        pe.wait_ge(tanh_done, it + 1)
                        o = job(("wl", l, d, p))
                        done(pe.matmul(o, w2a2[0:HD, d, 128 * p:128 * p + 128], lora[0:HD, :], start=True, stop=True))
                        o = job(("al", l, d, p))
                        done(pe.matmul(o, w2a2[HD:P, d, 128 * p:128 * p + 128], lora[HD:P, :], start=True, stop=True))
                    for p in range(2):
                        pe.wait_ge(ksq_done, 2 * it + p + 1)
                        o = job(("kss", l, d, p))
                        done(pe.matmul(o, K("heads"), t1[:, p, :], start=True, stop=True))
                    for p in range(2):
                        pe.wait_ge(bonus_in, 2 * it + p + 1)
                        o = job(("bon", l, d, p))
                        done(pe.matmul(o, K("heads"), sg[:, p, :], start=True, stop=True))
                    pe.wait_ge(streams_done, it + 1)
                    for h in range(HEADS):
                        r, p = slice(HD * (h % 2), HD * (h % 2) + HD), h // 2

                        def products(name, lhs):
                            for b in range(2):
                                o = job((name, l, d, h, b))
                                for x in range(2):
                                    bb = 2 * b + x
                                    last = pe.matmul(o[:, 256 * x:256 * x + 256], lhs[r, p, 128 * bb:128 * bb + 128],
                                                     ar[r, p, bb, :, :].rearrange("p a t -> p (a t)"),
                                                     start=True, stop=True)
                                done(last)

                        products("LM1", betaT)
                        o = job(("L1", l, d, h))
                        for b in range(NB):
                            last = pe.matmul(o[:, 128 * b:128 * b + 128], ar[r, p, b, 0, :],
                                             betaT[r, p, 128 * b:128 * b + 128], start=True, stop=True)
                        done(last)
                        products("LM2", kapT)
                    pe.wait_ge(t_done, 4 * it + 4)
                    for zi, z in enumerate(LEVELS):
                        for h in range(HEADS):
                            if zi:
                                emptied(pe, ("sy", l, d, LEVELS[zi - 1], h))
                            o = job(("sx", l, d, z, h))
                            for b in range(NB):
                                last = pe.matmul(o[:, 128 * b:128 * b + 128], LM1[:, h, b, 0:P], TN[:, h, b, :],
                                                 start=True, stop=True)
                            done(last)
                        for h in range(HEADS):
                            emptied(pe, ("sx", l, d, z, h))
                            if zi:
                                emptied(pe, ("syt", l, d, LEVELS[zi - 1], h))
                            if z != LEVELS[-1]:
                                o = job(("sy", l, d, z, h))
                                for b in range(NB):
                                    last = pe.matmul(o[:, 128 * b:128 * b + 128], TT[:, h, b, :], XS[:, h, b, :],
                                                     start=True, stop=True)
                                done(last)
                            o = job(("syt", l, d, z, h))
                            for b in range(NB):
                                last = pe.matmul(o[:, 128 * b:128 * b + 128], XS[:, h, b, :], TT[:, h, b, :],
                                                 start=True, stop=True)
                            done(last)
                    srcs = {"a": lambda p, b: ar[:, p, b, 0, :], "b": lambda p, b: betaT[:, p, 128 * b:128 * b + 128],
                            "k": lambda p, b: kapT[:, p, 128 * b:128 * b + 128],
                            "v": lambda p, b: vT[:, p, 128 * b:128 * b + 128]}
                    for h in range(HEADS):
                        emptied(pe, ("syt", l, d, LEVELS[-1], h))
                        for b in range(2):
                            emptied(pe, ("LM2", l, d, h, b))
                    for m in "akbv":
                        for p in range(2):
                            o = job(("tok", l, d, m, p))
                            for b in range(NB):
                                last = pe.transpose(o[:, 128 * b:128 * b + 128], srcs[m](p, b), K("ident"))
                            done(last)
                    for m in "akbv":
                        for p in range(2):
                            emptied(pe, ("tok", l, d, m, p))
                    for p in range(2):
                        o = job(("xv", l, d, p))
                        for x in range(2):
                            for b in range(NB):
                                h = 2 * p + x
                                last = pe.matmul(o[:, 256 * x + 64 * b:256 * x + 64 * b + 64], LM2[:, h, b, 0:P],
                                                 tokm["v"][:, b, HD * h:HD * h + HD], start=True, stop=True)
                        done(last)
                    for p in range(2):
                        o = job(("at", l, d, p))
                        for x in range(2):
                            for b in range(NB):
                                h = 2 * p + x
                                last = pe.matmul(o[HD * x:HD * x + HD, 128 * b:128 * b + 128],
                                                 tokm["a"][:, b, HD * h:HD * h + HD], TT[:, h, b, :],
                                                 start=True, stop=True)
                        done(last)
                    for p in range(2):
                        emptied(pe, ("xv", l, d, p))
                        o = job(("u0", l, d, p))
                        for x in range(2):
                            for b in range(NB):
                                h = 2 * p + x
                                last = pe.matmul(o[:, 256 * x + 64 * b:256 * x + 64 * b + 64], TT[:, h, b, :],
                                                 XV[:, h, b, :], start=True, stop=True)
                        done(last)
                    for p in range(2):
                        emptied(pe, ("at", l, d, p))
                    for c in range(NCH):
                        b, qs = c // 2, slice(HD * (c % 2), HD * (c % 2) + HD)
                        tc = slice(HD * (c % 2), HD * (c % 2) + HD)
                        cs = slice(CH * c, CH * c + CH)
                        o = job(("cu", l, d, c))
                        if c:
                            emptied(pe, ("ch", l, d, c - 1))
                        for p in range(2):
                            last = pe.matmul(o[qs, P * p:P * p + P], AT[:, p, cs], state[:, c % 2, p, :],
                                             start=True, stop=True)
                        done(last)
                        emptied(pe, ("cu", l, d, c))
                        if c < NCH - 1:
                            o = job(("ch", l, d, c))
                            for p in range(2):
                                dst, hs = o[:, P * p:P * p + P], slice(P * p, P * p + P)
                                pe.matmul(dst, K("ident"), state[:, c % 2, p, :], start=True, stop=False)
                                pe.matmul(dst, tokm["k"][qs, b, hs], tokm["v"][qs, b, hs], start=False, stop=False)
                                last = pe.matmul(dst, tokm["b"][qs, b, hs],
                                                 nu[qs, 2 * p:2 * p + 2, :].rearrange("p h n -> p (h n)"),
                                                 start=False, stop=True)
                            done(last)
                        if l == 0 or c >= NCH // 2:
                            o = job(("cy", l, d, c))
                            for p in range(2):
                                dst = o[:, CH * p:CH * p + CH]
                                pe.matmul(dst, state[:, c % 2, p, :], ar[:, p, b, 1, tc], start=True, stop=True)
                                for h in (2 * p, 2 * p + 1):
                                    r, hs = slice(HD * (h % 2), HD * (h % 2) + HD), slice(HD * h, HD * h + HD)
                                    mc = slice(P + CH * (c % 2), P + CH * (c % 2) + CH)
                                    pe.matmul(dst[r, :], tokm["v"][qs, b, hs], LM2[qs, h, b, mc],
                                              start=False, stop=False, skip_group_check=True)
                                    last = pe.matmul(dst[r, :], nu[qs, h, :], LM1[qs, h, b, mc],
                                                     start=False, stop=False, skip_group_check=True)
                            done(last)
                for p in range(2):
                    emptied(pe, ("cy", l, 1, NCH - 1))
                    o = job(("mean", l, p))
                    done(pe.matmul(o[:, c0:c1], K("heads"), YB[:, 6 + p, c0:c1], start=True, stop=True))
                for p in range(2):
                    pe.wait_ge(ln_sq, 2 * l + p + 1)
                    o = job(("var", l, p))
                    done(pe.matmul(o[:, c0:c1], K("heads"), ACC[:, p, c0:c1], start=True, stop=True))
                pe.wait_ge(lg_done, l + 1)
                for p in range(2):
                    o = job(("g2", l, p))
                    done(pe.matmul(o[:, c0:c1], g2[:, 128 * p:128 * p + 128], siglg[:, c0:c1], start=True, stop=True))
                pe.wait_ge(ya_ready, 2 * l + 2)
                for i in range(len(units)):
                    if i >= len(units) - NBANK:
                        emptied(pe, ("PV", l, i))
                for p in range(2):
                    emptied(pe, ("g2", l, p))
                for J in range(4):
                    wb = weights(("branch", l, J))
                    for i in range(4):
                        w = weights(("gate", l, J, i))
                        for j in (2 * J, 2 * J + 1):
                            project(("gate", l, j, i), w, j - 2 * J, H, c0, c1)
                            project(("br", l, j, i), wb, j - 2 * J, YB[:, 2 * i:2 * i + 2, :], c0, c1, 2 * i, 2)
                pe.wait_ge(gated, added(l, KT - 1, 3))
                for j in range(KT):
                    project(("wo", l, j), weights(("w_o", l, j // 2)), j % 2, ACC, c0, c1)
                sum_squares(l, 1, Z)
                sum_squares(l, 2, Z)
                for k in range(KT):
                    pe.wait_ge(h_ready, 16 * l + 8 + k + 1)
                for j in range(FT):
                    for g in range(2):
                        project(("up", l, j, g), weights(("up", l, j // 2, g)), j % 2, ACC, c0, c1)
                for j in range(KT):
                    o = job(("down", l, j))
                    for k in range(FT):
                        w = weights(("down", l, j // 2, k // 8))
                        if j == 0:
                            pe.wait_ge(u_ready, FT * l + k + 1)
                        last = pe.matmul(o[:, c0:c1], w[:, k % 8, 128 * (j % 2):128 * (j % 2) + 128], Z[:, k, c0:c1],
                                         start=(k == 0), stop=(k == FT - 1))
                    done(last)
                sum_squares(l, 3, ACC)


IN_NAMES = ["const", "vecs", "cs", "xin", "w2a2", "g2", "na_bias", "ada_w", "w_in", "w_branch", "w_gate", "w_o",
            "ffn_up", "ffn_down"]


def kernel(x, c, ctx, c_ctx, ada_w, ada_b, norm_mix_pre, norm_mix_post, norm_ffn_pre, norm_ffn_post,
           w_in, conv_a, na_bias, q_norm, k_norm, rw_mu, rw_w0, rw_w2, rw_a0, rw_a2, rw_kk, rw_ka, rw_rk,
           rw_g2, rw_ln_w, rw_ln_b, w_branch, w_gate, b_gate, w_o, ffn_up, ffn_conv, ffn_down):
    import concourse.bacc as bacc
    from concourse.bass_utils import run_bass_kernel_spmd

    def columns(v):
        v = np.asarray(v)
        return v.reshape(LAYERS, -1, P).transpose(0, 2, 1)

    twice = lambda v: np.concatenate([v, v], axis=-1)
    q_norm, k_norm = np.asarray(q_norm), np.asarray(k_norm)
    parts = dict(mix_pre=norm_mix_pre, mix_post=norm_mix_post, ffn_pre=norm_ffn_pre, ffn_post=norm_ffn_post,
                 ada_b=ada_b, conv_a=conv_a, q_norm=twice(q_norm), k_norm=twice(k_norm), mu=rw_mu, w0=rw_w0,
                 a0=rw_a0, kk=rw_kk, ka=rw_ka, rk=rw_rk, ln_w=rw_ln_w, ln_b=rw_ln_b, b_gate=b_gate,
                 ffn_conv=ffn_conv)
    vecs = np.concatenate([columns(parts[n]) for n, _ in VEC_COLS], axis=2)
    order = np.arange(ZT * P)
    q0 = Z_GQ * P
    order[q0:q0 + 256] = q0 + np.concatenate([np.arange(64) + 64 * h for h in (0, 2, 1, 3)])
    arrays = dict(
        const=constants(), vecs=vecs,
        cs=np.stack([np.asarray(c_ctx), np.asarray(c)[0]], axis=1),
        xin=np.concatenate([np.asarray(ctx)[0].T, np.asarray(x)[0].T], axis=1),
        w2a2=np.concatenate([np.asarray(rw_w2), np.asarray(rw_a2)], axis=2).transpose(0, 2, 1, 3),
        g2=rw_g2, na_bias=na_bias, ada_w=ada_w, w_in=np.asarray(w_in)[:, :, order],
        w_branch=np.asarray(w_branch).reshape(LAYERS, DM, DM), w_gate=w_gate, w_o=w_o, ffn_up=ffn_up,
        ffn_down=ffn_down)
    nc = bacc.Bacc("TRN2", target_bir_lowering=False, num_devices=1)
    ins, aps = {}, {}
    for n in IN_NAMES:
        v = np.ascontiguousarray(np.asarray(arrays[n]))
        ins["in_" + n] = v
        aps[n] = nc.dram_tensor("in_" + n, v.shape, mybir.dt.from_np(v.dtype), kind="ExternalInput").ap()
    out = nc.dram_tensor("out", (DM, LAT), F32, kind="ExternalOutput").ap()
    build(nc, aps, out)
    r = run_bass_kernel_spmd(nc, [ins], core_ids=[0])
    return np.ascontiguousarray(r.results[0]["out"].T)[None]
```

```python
from contextlib import ExitStack

import numpy as np
import concourse.bass as bass
from concourse import mybir

F32 = mybir.dt.float32
F32R = mybir.dt.float32r
ALU = mybir.AluOpType
ACT = mybir.ActivationFunctionType
AX = mybir.AxisListType.X

P = 128
LAYERS = 2
DM = 1024
KT = DM // P
CTX = 256
LAT = 256
T = CTX + LAT
GRID_W = 64
WIN_R, WIN_C = 8, 16
ZT = 24
DFF = 2816
FT = DFF // P
HD = 64
HEADS = 4
CH = 64
NCH = T // CH
NB = T // P
LEVELS = (2, 4, 8, 16, 32)
EPS = 1e-6
LN_EPS = 64e-5
DECAY = float(np.exp(-0.5))
MASKED = -1e30
KK_SCALE = 1024.0
BIAS_C = 2 * WIN_C - 1
BIAS_N = (2 * WIN_R - 1) * BIAS_C

Z_BG, Z_CG, Z_XIN = 0, 2, 4
Z_NQ, Z_NK, Z_NV = 6, 8, 10
Z_GQ, Z_GK, Z_GV = 12, 14, 15
Z_R, Z_K, Z_V, Z_LORA, Z_G = 16, 18, 20, 22, 23
ACT_Z = [t for t in range(ZT) if t % 2 == 0 or t == Z_NQ + 1]
DVE_Z = [t for t in range(ZT) if t not in ACT_Z]
LATENT_ONLY = {0, 1, 2, 3, 4, 5, 6, 7, 12, 13, 23}

VEC_COLS = [("mix_pre", 8), ("mix_post", 8), ("ffn_pre", 8), ("ffn_post", 8), ("ada_b", 48), ("conv_a", 6),
            ("q_norm", 1), ("k_norm", 1), ("mu", 14), ("w0", 4), ("a0", 4), ("kk", 2), ("ka", 2), ("rk", 2),
            ("ln_w", 2), ("ln_b", 2), ("b_gate", 32), ("ffn_conv", 132)]
VEC = {}
_at = 0
for _n, _c in VEC_COLS:
    VEC[_n] = _at
    _at += _c
NVEC = _at

CONST_COLS = [("ident", P), ("ones", P), ("heads", P), ("swap", P), ("lm", 2 * P), ("m1", P), ("m1t", P),
              ("m2", P), ("m4", P), ("m8", P), ("m16", P), ("m32", P), ("cos", LAT), ("sin", LAT),
              ("reset", T), ("window", GRID_W)]
CON = {}
_at = 0
for _n, _c in CONST_COLS:
    CON[_n] = _at
    _at += _c
NCON = _at

RING = 3
SLOT_N = 256
SPLIT = 3
NBANK = 8


def constants():
    p = np.arange(P)
    c = np.zeros((P, NCON), np.float32)

    def put(name, a):
        c[:, CON[name]:CON[name] + a.shape[1]] = a

    put("ident", np.eye(P))
    put("ones", np.ones((P, P)))
    put("heads", (p[:, None] // HD == p[None, :] // HD).astype(np.float32))
    sw = np.zeros((P, P))
    ev = np.arange(0, P, 2)
    sw[ev + 1, ev] = -1.0
    sw[ev, ev + 1] = 1.0
    put("swap", sw)
    s, t = p[:, None], p[None, :]
    same = s // CH == t // CH
    put("lm", np.concatenate([same & (s < t), same & (s <= t)], 1).astype(np.float32))
    m1 = (s % 2 == 1) & (t == s - 1)
    put("m1", m1)
    put("m1t", m1.T)
    for z in LEVELS:
        put(f"m{z}", ((s // z) % 2 == 1) & (t // z == s // z - 1))
    tok = np.arange(LAT)
    n_freq = HD // 4
    inv = (np.float32(10000.0) ** (-np.arange(n_freq, dtype=np.float32) / np.float32(n_freq))).astype(np.float32)
    row, col = (tok // GRID_W).astype(np.float32), (tok % GRID_W).astype(np.float32)
    ang = np.concatenate([row[None, :] * inv[:, None], col[None, :] * inv[:, None]], 0)
    ang = ang[(p % HD) // 2]
    put("cos", np.cos(ang))
    put("sin", np.sin(ang))
    put("reset", np.broadcast_to((np.arange(T) % CH != 0).astype(np.float32), (P, T)))
    j, kc = GRID_W - 1 - p[:, None] % GRID_W, np.arange(GRID_W)[None, :]
    cs = np.clip(j - WIN_C // 2, 0, GRID_W - WIN_C)
    put("window", np.where((kc >= cs) & (kc < cs + WIN_C), 0.0, MASKED))
    return c


def attention_units(l):
    tiles = range(4) if l == 0 else range(2, 4)
    return [(g, h, q) for g in "BC" for h in range(HEADS) for q in tiles]


def modulation_jobs(blocks):
    jobs = []
    for n, b in enumerate(blocks):
        jobs.append(("mod",) + b)
        if n:
            jobs.append(("modt",) + blocks[n - 1])
    return jobs + [("modt",) + blocks[-1]]


MOD_FIRST = [(0, n) for n in range(8)]
MOD_LATER = [(0, n) for n in range(8, 24)] + [(1, n) for n in range(24)]


def fill_plan():
    points = [("att", i) for i in range(0, 32, 2)]
    points += [("lora", 0)] * 3 + [("norm", 0)] * 3 + [("bonus", 0)] * 4
    points += [("lora", 1)] * 3 + [("norm", 1)] * 3 + [("bonus", 1)] * 4 + [("post",)] * 2 + [("ffn",)] * 2
    jobs = modulation_jobs(MOD_LATER)
    plan = {}
    for n, p in enumerate(points):
        last = n == len(points) - 1
        plan.setdefault(p, []).extend(jobs[max(0, 2 * n - 1):None if last else 2 * n + 1])
    return plan


FILL = fill_plan()


def job_list():
    jobs = []
    for l in range(LAYERS):
        fill = FILL if l == 0 else {}
        jobs += [("ss", l, 0)]
        if l == 0:
            jobs += modulation_jobs(MOD_FIRST)
        jobs += [("z", l, t) for t in range(ZT)]
        jobs += [("vt", l, i) for i in range(3)]
        jobs += [("qss", l, i) for i in range(3)]
        jobs += [("qsw", l, i) for i in range(3)]
        n = len(attention_units(l))
        for i in range(n + 3):
            if i < n:
                jobs.append(("S", l, i))
            jobs += fill.get(("att", i), [])
            if 2 <= i <= n + 1:
                jobs.append(("T", l, i - 2))
            if i >= 3:
                jobs.append(("PV", l, i - 3))
        for d in range(2):
            jobs += [(k, l, d, p) for p in range(2) for k in ("wl", "al")]
            jobs += fill.get(("lora", d), [])
            jobs += [("kss", l, d, p) for p in range(2)]
            jobs += [("tok", l, d, "v", p) for p in range(2)]
            jobs += fill.get(("norm", d), [])
            jobs += [("bon", l, d, p) for p in range(2)]
            jobs += [("tok", l, d, "k", p) for p in range(2)]
            jobs += fill.get(("bonus", d), [])
            for h in range(HEADS):
                jobs += [("LM1", l, d, h, b) for b in range(2)]
                jobs += [("L1", l, d, h)]
                if h % 2:
                    jobs += [("tok", l, d, m, h // 2) for m in "ab"]
            for n, s in enumerate(LEVELS):
                jobs += [("sx", l, d, s, h) for h in range(HEADS)]
                if n < HEADS:
                    jobs += [("LM2", l, d, n, b) for b in range(2)]
                else:
                    jobs += [("xv", l, d, p) for p in range(2)]
                for h in range(HEADS):
                    if s != LEVELS[-1]:
                        jobs += [("sy", l, d, s, h)]
                    jobs += [("syt", l, d, s, h)]
            jobs += [("at", l, d, p) for p in range(2)]
            jobs += [("u0", l, d, p) for p in range(2)]
            for c in range(NCH):
                jobs += [("cu", l, d, c)]
                if c < NCH - 1:
                    jobs += [("ch", l, d, c)]
                if l == 0 or c >= NCH // 2:
                    jobs += [("cy", l, d, c)]
        for k in ("mean", "var", "g2"):
            jobs += [(k, l, p) for p in range(2)]
        for J in range(4):
            for i in range(4):
                for j in (2 * J, 2 * J + 1):
                    jobs += [("gate", l, j, i), ("br", l, j, i)]
        jobs += [("wo", l, j) for j in range(8)]
        jobs += fill.get(("post",), [])
        jobs += [("ss", l, 1)]
        jobs += fill.get(("ffn",), [])
        jobs += [("ss", l, 2)]
        for j in range(FT):
            jobs += [("up", l, j, 0), ("up", l, j, 1)]
        jobs += [("down", l, j) for j in range(8)]
        jobs += [("ss", l, 3)]
    return {name: g for g, name in enumerate(jobs)}


JOB = job_list()


def blocks_of(job):
    k, l = job[:2]
    if k == "mod":
        return [(("ada", l, job[2]), None)]
    if k == "z":
        return [(("w_in", l, job[2] // 2), job[2] % 2)]
    if k == "gate":
        return [(("gate", l, job[2] // 2, job[3]), job[2] % 2)]
    if k == "wo":
        return [(("w_o", l, job[2] // 2), job[2] % 2)]
    if k == "up":
        return [(("up", l, job[2] // 2, job[3]), job[2] % 2)]
    if k == "down":
        return [(("down", l, job[2], q), 0) for q in range(3)]
    return []


def streams_of_weights():
    slots, last_job, halves, half_job = {}, {}, {}, []
    for job in JOB:
        for raw, half in blocks_of(job):
            slots.setdefault(raw, len(slots))
            last_job[raw] = job
            if half is not None:
                halves[(raw, half)] = len(halves)
                half_job.append(job)
    return slots, last_job, halves, half_job


SLOT, LAST_JOB, HALF, HALF_JOB = streams_of_weights()
HALVES = list(HALF)


def half_no(job):
    return HALF[blocks_of(job)[0]]


def build(nc, a, out):
    ctx = ExitStack()
    with ctx:
        def sb(name, shape):
            return ctx.enter_context(nc.sbuf_tensor(name, shape, F32))

        def sem(name):
            return ctx.enter_context(nc.semaphore(name))

        con = sb("con", [P, NCON])
        vec = sb("vec", [P, LAYERS * NVEC])
        w2a2 = sb("w2a2", [P, 2, 256])
        bm = sb("bm", [P, HEADS, 6, GRID_W])
        ring = sb("ring", [P, RING, KT, SLOT_N])
        cvec = sb("cvec", [P, KT, 2])
        mod = sb("mod", [P, LAYERS, 48, 2])
        amod = sb("amod", [P, 4, 8, 2])
        omu = sb("omu", [P, 14])
        oka = sb("oka", [P, 2])
        eps = sb("eps", [P, 2])
        rs = sb("rs", [P, T])
        rt = sb("rt", [P, T])
        wendt = sb("wendt", [P, 2 * NCH])
        stat = sb("stat", [P, 3, 4])
        mrow = sb("mrow", [2, SLOT_N])
        ps = ctx.enter_context(nc.psum_tensor("ps", [P, NBANK, 512], F32))
        xsave = nc.dram_tensor("xsave", [DM, T], F32, kind="Internal").ap()
        hsave = nc.dram_tensor("hsave", [2, DM, T], F32R, kind="Internal").ap()

        def split_slots(name):
            return ctx.enter_context(nc.sbuf_tensor(name, [P, SPLIT, KT, P], F32R))

        whi, wlo = split_slots("whi"), split_slots("wlo")

        base = -(-nc.sbuf_base // 32) * 32
        ctx.enter_context(nc.sbuf_tensor("arena", [P, 132 * 256], F32))

        def at(name, kb, shape, dtype=F32):
            return nc.alloc_sbuf_tensor_at(name, [P] + shape, dtype, offset=base + 1024 * kb)

        X = at("X", 0, [KT, T])
        YB = at("YB", 16, [KT, T])
        Z = at("Z", 32, [ZT, T])
        HR = at("HR", 80, [2, KT, T], F32R)
        LMr = at("LMr", 80, [8192])
        pr = at("pr", 80, [3, T])
        prT = at("prT", 86, [3, T])
        E = at("E", 112, [5120])
        WB = at("WB", 112, [2, KT, SLOT_N])
        ACC = at("ACC", 32, [KT, T])
        RO = at("RO", 48, [6, T])
        AR = at("AR", 48, [2, KT, T], F32R)
        OB = at("OB", 80, [KT, T])
        SQB = at("SQB", 96, [KT, T])
        H2 = at("H2", 100, [2, KT, T], F32R)
        UA = at("UA", 16, [2, 20, T], F32R)
        UB = at("UB", 0, [2, FT - 20, T], F32R)
        CU = at("CU", 96, [2, T])
        F = at("F", 100, [KT, T])
        SQF = at("SQF", 116, [KT, T])

        def hidden(part, j):
            return UA[:, part, j, :] if j < 20 else UB[:, part, j - 20, :]

        def K(name, n=P):
            return con[:, CON[name]:CON[name] + n]

        def vc(l, name, i=0, n=1):
            o = l * NVEC + VEC[name] + i
            return vec[:, o:o + n]

        Ef, Lf = E, LMr
        Zf = Z[:, :, :].rearrange("p a b -> p (a b)")

        def view(f, o, *dims):
            n = int(np.prod(dims))
            v = f[:, o:o + n]
            if len(dims) == 2:
                return v.rearrange("p (a b) -> p a b", a=dims[0])
            if len(dims) == 3:
                return v.rearrange("p (a b c) -> p a b c", a=dims[0], b=dims[1])
            if len(dims) == 4:
                return v.rearrange("p (a b c d) -> p a b c d", a=dims[0], b=dims[1], c=dims[2])
            return v

        nu = rt[:, 0:256].rearrange("p (h n) -> p h n", h=HEADS)
        state = rs[:, :].rearrange("p (b a n) -> p b a n", b=2, a=2)
        wend = wendt[:, :].rearrange("p (a c) -> p a c", a=2)
        vB = view(Ef, 0, 4, 256)
        vC = view(Ef, 1024, 4, 128)
        sbuf2 = view(Ef, 1536, 3, T)
        qtmp, qtmp2 = YB[:, 6, :], YB[:, 7, :]
        KZ = Z
        ar = view(Ef, 0, 2, NB, 2, P)
        betaz = view(Ef, 2048, HEADS, T)
        kapz01, kapz23 = view(Zf, 7168, 2, T), view(Ef, 4096, 2, T)

        def kapz(h):
            return kapz01[:, h, :] if h < 2 else kapz23[:, h - 2, :]

        bon = bm[:, :, :, :].rearrange("p h r c -> p (h r c)")[:, 0:2 * T].rearrange("p (a t) -> p a t", a=2)
        g2 = bm[:, :, :, :].rearrange("p h r c -> p (h r c)")[:, 2 * T:2 * T + 256]
        LM1 = view(Lf, 0, HEADS, NB, 2 * P)
        LM2 = view(Lf, 4096, HEADS, NB, 2 * P)
        TT = view(Zf, 0, HEADS, NB, P)
        TN = view(Zf, 2048, HEADS, NB, P)
        XS = view(Zf, 4096, HEADS, NB, P)
        vT = view(Zf, 6144, 2, T)
        AT = vT
        zr, zk, sg, aa = (view(Lf, 1024 * i, 2, T) for i in range(4))
        G, kk, t1, t2 = (view(Lf, 4096 + 1024 * i, 2, T) for i in range(4))
        wdec, winv = (view(Zf, 2048 + 1024 * i, 2, T) for i in range(2))
        wprev = view(Zf, 4096, 2, T)
        lora = view(Zf, 5120, T)
        Xf = X[:, :, :].rearrange("p k t -> p (k t)")
        tokm = {m: view(Xf, 1024 * i, NB, 256) for i, m in enumerate("abkv")}
        XV = view(Ef, 2048, HEADS, NB, HD)
        U0 = view(Ef, 3072, HEADS, NB, HD)
        SQ = {0: YB, 1: SQB, 2: SQB, 3: SQF}
        siglg = view(Zf, Z_G * T, T)

        c_in = sem("c_in")
        const_in = sem("const_in")
        vec_in = sem("vec_in")
        root_ready = sem("root_ready")
        gains_ready = sem("gains_ready")
        ln_root = sem("ln_root")
        w_used = sem("w_used")
        small_in = [sem("small_in0"), sem("small_in1")]
        x_in = sem("x_in")
        g2_in = sem("g2_in")
        x_saved = sem("x_saved")
        wb_in = sem("wb_in")
        x_back = sem("x_back")
        w_in_slot = [sem(f"w_slot{i}") for i in range(RING)]
        mm_done = sem("mm_done")
        bank_free = [sem(f"bank_free{i}") for i in range(NBANK)]
        silu_c = sem("silu_c")
        hi_done = sem("hi_done")
        lo_done = sem("lo_done")
        h_hi = sem("h_hi")
        h_saved = [sem("h_saved0"), sem("h_saved1")]
        h_back = [sem("h_back0"), sem("h_back1")]
        kz_ready = sem("kz_ready")
        p_sum = sem("p_sum")
        kap_done = sem("kap_done")
        kapz_done = sem("kapz_done")
        beta_done = sem("beta_done")
        betaz_done = sem("betaz_done")
        bonus_done = sem("bonus_done")
        tt_masked = sem("tt_masked")
        acc_hi = sem("acc_hi")
        acc_lo = sem("acc_lo")
        u_hi = sem("u_hi")
        u_lo = sem("u_lo")
        setup = sem("setup")
        sq_ready = sem("sq_ready")
        h_half = sem("h_half")
        h_ready = sem("h_ready")
        x_ready = sem("x_ready")
        ya_ready = sem("ya_ready")
        qsq_ready = sem("qsq_ready")
        qn_ready = sem("qn_ready")
        qk_ready = sem("qk_ready")
        q_scaled = sem("q_scaled")
        nmax_ready = sem("nmax_ready")
        p_ready = sem("p_ready")
        shift_half = sem("shift_half")
        shift_done = sem("shift_done")
        tanh_done = sem("tanh_done")
        kraw_done = sem("kraw_done")
        ksq_done = sem("ksq_done")
        scan_done = sem("scan_done")
        decay_done = sem("decay_done")
        bonus_in = sem("bonus_in")
        streams_done = sem("streams_done")
        t_done = sem("t_done")
        kroot_done = sem("kroot_done")
        ln_sq = sem("ln_sq")
        lg_done = sem("lg_done")
        gated = sem("gated")
        conv_half = sem("conv_half")
        silu_done = sem("silu_done")
        u_ready = sem("u_ready")
        act_chain = sem("act_chain")
        dve_chain = sem("dve_chain")
        pool_chain = sem("pool_chain")
        stored = sem("stored")

        def bank(name):
            return ps[:, JOB[name] % NBANK, :]

        def filled(eng, name):
            eng.wait_ge(mm_done, JOB[name] + 1)
            return bank(name)

        def frees(name):
            return bank_free[JOB[name] % NBANK]

        def emptied(eng, name):
            eng.wait_ge(frees(name), JOB[name] // NBANK + 1)

        def cols(l, t=None):
            if l == 0 or (t is not None and t not in LATENT_ONLY):
                return 0, T
            return CTX, T

        def streams(l):
            return (0, 1) if l == 0 else (1,)

        def norm_no(l, k):
            return 4 * l + k

        def added(l, j, i):
            return 24 * l + 6 * (j // 2) + 2 * (i - 1) + j % 2 + 1

        def grid_rows(v):
            return v.rearrange("p (r j) -> p r j", j=GRID_W)

        UNITS = [attention_units(l) for l in range(LAYERS)]
        UBASE = [0, len(UNITS[0])]

        block = ctx.enter_context(nc.Block())

        @block.sync
        def _(sp):
            sp.dma_start(cvec[:, :, :], a["cs"].rearrange("(k p) s -> p k s", p=P)).then_inc(c_in, 16)
            sp.dma_start(X[:, :, :], a["xin"].rearrange("(k p) t -> p k t", p=P)).then_inc(x_in, 16)
            sp.dma_start(con[:, :], a["const"]).then_inc(const_in, 16)
            sp.dma_start(vec[:, :].rearrange("p (l n) -> p l n", l=LAYERS),
                         a["vecs"].rearrange("l p n -> p l n")).then_inc(vec_in, 16)
            names = list(SLOT)
            for n, name in enumerate(names):
                k, l = name[:2]
                if n >= RING:
                    old = names[n - RING]
                    if (old, 0) in HALF:
                        sp.wait_ge(lo_done, max(HALF[(old, x)] for x in range(2) if (old, x) in HALF) + 1)
                    else:
                        sp.wait_ge(mm_done, JOB[LAST_JOB[old]] + 1)
                dst = ring[:, n % RING, :, :]
                if k == "ada":
                    src = a["ada_w"][l, :, name[2] * SLOT_N:(name[2] + 1) * SLOT_N]
                elif k == "w_in":
                    src = a["w_in"][l, :, name[2] * SLOT_N:(name[2] + 1) * SLOT_N]
                elif k == "gate":
                    o = name[3] * DM + name[2] * SLOT_N
                    src = a["w_gate"][l, :, o:o + SLOT_N]
                elif k == "w_o":
                    src = a["w_o"][l, :, name[2] * SLOT_N:(name[2] + 1) * SLOT_N]
                elif k == "up":
                    o = name[3] * DFF + name[2] * SLOT_N
                    src = a["ffn_up"][l, :, o:o + SLOT_N]
                else:
                    k0, k1 = 8 * name[3], min(8 * name[3] + 8, FT)
                    src = a["ffn_down"][l, k0 * P:k1 * P, name[2] * P:(name[2] + 1) * P]
                    dst = ring[:, n % RING, 0:k1 - k0, 0:P]
                sp.dma_start(dst, src.rearrange("(k p) n -> p k n", p=P)).then_inc(w_in_slot[n % RING], 16)

        @block.gpsimd
        def _(pool):
            links = [0]

            def link(ins):
                links[0] += 1
                ins.then_inc(pool_chain, 1)
                pool.wait_ge(pool_chain, links[0])

            def load_small(l):
                pool.dma_start(w2a2[:, :, :], a["w2a2"][l]).then_inc(small_in[l], 16)
                nb = a["na_bias"]
                for h in range(HEADS):
                    for half in range(2):
                        src = bass.AP(nb.tensor,
                                      (l * HEADS + h) * BIAS_N + (5 - half) * BIAS_C + WIN_C - 1 - (GRID_W - 1),
                                      [[1, GRID_W], [BIAS_C, 6], [1, GRID_W]])
                        pool.dma_start(bm[half * HD:(half + 1) * HD, h, :, :], src).then_inc(small_in[l], 16)

            load_small(0)
            for l in range(LAYERS):
                c0, c1 = cols(l)
                ns = len(streams(l))
                if l == 1:
                    emptied(pool, ("g2", 0, 1))
                    load_small(1)
                pool.wait_ge(h_ready, 16 * l + 8)
                for part in range(2):
                    pool.dma_start(hsave[part, :, c0:T].rearrange("(k p) t -> p k t", p=P), HR[:, part, :, c0:T])\
                        .then_inc(h_saved[l], 16)
                if l:
                    pool.dma_start(xsave[:, :].rearrange("(k p) t -> p k t", p=P), X[:, :, :]).then_inc(x_saved, 16)
                for p in range(2):
                    for t in (Z_BG + p, Z_CG + p, Z_XIN + p):
                        emptied(pool, ("z", l, t))
                    xc = Z[:, Z_XIN + p, c0:c1]
                    cg = Z[:, Z_CG + p, c0:c1]
                    y = YB[:, p, c0:c1]
                    link(pool.tensor_tensor(xc, xc, cg, ALU.mult))
                    link(pool.tensor_scalar(y, xc, vc(l, "conv_a", 2 + p), None, ALU.mult))
                    xs = xc.rearrange("p (s t) -> p s t", s=ns)
                    ys = y.rearrange("p (s t) -> p s t", s=ns)
                    tm = cg.rearrange("p (s t) -> p s t", s=ns)
                    link(pool.tensor_scalar(tm[:, :, 0:255], xs[:, :, 0:255], vc(l, "conv_a", p), None, ALU.mult))
                    link(pool.tensor_tensor(ys[:, :, 1:256], ys[:, :, 1:256], tm[:, :, 0:255], ALU.add))
                    link(pool.tensor_scalar(tm[:, :, 0:255], xs[:, :, 1:256], vc(l, "conv_a", 4 + p), None, ALU.mult))
                    link(pool.tensor_tensor(ys[:, :, 0:255], ys[:, :, 0:255], tm[:, :, 0:255], ALU.add))
                    pool.tensor_tensor(y, y, Z[:, Z_BG + p, c0:c1], ALU.mult).then_inc(ya_ready, 1)
                units = UNITS[l]
                for u in range(len(units)):
                    nk = T if units[u][2] >= 2 else CTX
                    pool.wait_ge(p_sum, UBASE[l] + u + 1)
                    pool.tensor_scalar(pr[:, u % 3, 0:nk], pr[:, u % 3, 0:nk], stat[:, 2, u % 4:u % 4 + 1],
                                       None, ALU.mult).then_inc(p_ready, 1)
                pool.wait_ge(mm_done, JOB[("PV", l, len(units) - 1)] + 1)
                pool.dma_start(g2[:, :], a["g2"][l]).then_inc(g2_in, 16)
                idb = K("ident").unsqueeze(1).to_broadcast([P, NB, P])
                for d in range(2):
                    it = 2 * l + d
                    for p in range(2):
                        emptied(pool, ("bon", l, d, p))
                        if d == 0:
                            pool.tensor_tensor(bon[:, p, :], bon[:, p, :], vT[:, p, :], ALU.mult).then_inc(bonus_done, 1)
                        else:
                            link(pool.tensor_tensor(G[:, p, :], G[:, p, :], vT[:, p, :], ALU.mult))
                            rev = G[:, p, :].rearrange("p (s t) -> p s t", s=2)[:, :, ::-1]
                            bo = bon[:, p, :].rearrange("p (s t) -> p s t", s=2)
                            pool.tensor_tensor(bo, bo, rev, ALU.add).then_inc(bonus_done, 1)
                    for h in range(HEADS):
                        emptied(pool, ("L1", l, d, h))
                        pool.tensor_tensor(TN[:, h, :, :], idb, TN[:, h, :, :], ALU.subtract).then_inc(t_done, 1)
                        pool.wait_ge(tt_masked, 4 * it + h + 1)
                        pool.tensor_tensor(TT[:, h, :, :], idb, TT[:, h, :, :], ALU.subtract).then_inc(t_done, 1)
                pool.wait_ge(mm_done, JOB[("cy", l, 1, NCH - 1)] + 1)
                pool.wait_ge(h_saved[l], 32)
                for part in range(2):
                    pool.dma_start(HR[:, part, :, c0:T], hsave[part, :, c0:T].rearrange("(k p) t -> p k t", p=P))\
                        .then_inc(h_back[l], 16)
                for J in range(4):
                    if J >= 2:
                        pool.wait_ge(mm_done, JOB[("br", l, 2 * J - 3, 3)] + 1)
                    elif J == 0:
                        emptied(pool, ("cu", l, 1, NCH - 1))
                    pool.dma_start(WB[:, J % 2, :, :],
                                   a["w_branch"][l, :, J * SLOT_N:(J + 1) * SLOT_N].rearrange("(k p) n -> p k n", p=P))\
                        .then_inc(wb_in, 16)
                    if J == 1:
                        if l:
                            pool.wait_ge(x_saved, 32)
                        pool.dma_start(X[:, :, c0:c1],
                                       (xsave if l else a["xin"])[:, c0:c1].rearrange("(k p) t -> p k t", p=P))\
                            .then_inc(x_back, 16)
                    pool.wait_ge(wb_in, 16 * (4 * l + J + 1))
                pool.wait_ge(x_ready, 16 * l + 8)
                pool.dma_start(xsave[:, c0:c1].rearrange("(k p) t -> p k t", p=P), X[:, :, c0:c1]).then_inc(x_saved, 16)
                for j in range(FT):
                    pool.wait_ge(silu_done, l * FT + j + 1)
                    u = CU[:, j % 2, c0:c1]
                    pool.tensor_tensor(u, u, (rs, rt)[j % 2][:, c0:c1], ALU.mult).then_inc(u_ready, 1)
                pool.wait_ge(mm_done, JOB[("down", l, KT - 1)] + 1)
                pool.wait_ge(x_saved, 16 * (2 * l + 1))
                pool.dma_start(X[:, :, c0:c1], xsave[:, c0:c1].rearrange("(k p) t -> p k t", p=P)).then_inc(x_back, 16)
            for i in range(KT):
                pool.wait_ge(x_ready, 24 + i + 1)
                pool.dma_start(out[i * P:(i + 1) * P, :], X[:, i, CTX:T]).then_inc(stored, 16)
            pool.wait_ge(stored, 16 * KT)

        @block.scalar
        def _(act):
            links = [0]

            def link(ins):
                links[0] += 1
                ins.then_inc(act_chain, 1)
                act.wait_ge(act_chain, links[0])

            sqs = [0]

            def square(dst, src):
                sqs[0] += 1
                act.activation(dst, src, ACT.Square).then_inc(sq_ready, 1)
                act.wait_ge(sq_ready, sqs[0])

            def norm_root(l, k):
                c0, c1 = cols(l) if k else (0, T)
                s = filled(act, ("ss", l, k))
                act.activation(rt[:, c0:c1], s[:, c0:c1], ACT.Ln, bias=eps[:, 0:1], scale=1.0 / DM)\
                   .then_inc(frees(("ss", l, k)), 1)
                emptied(act, ("ss", l, k))
                act.activation(rs[:, c0:c1], rt[:, c0:c1], ACT.Exp, scale=-0.5).then_inc(root_ready, 1)

            halves = [0]

            def split_until(n):
                while halves[0] < n:
                    m = halves[0]
                    raw, half = HALVES[m]
                    kn = FT % KT if raw[0] == "down" and raw[3] == 2 else KT
                    act.wait_ge(w_in_slot[SLOT[raw] % RING], 16 * (SLOT[raw] // RING + 1))
                    if m >= SPLIT:
                        old = HALVES[m - SPLIT][0]
                        if old[0] == "down" and old[3] < 2:
                            act.wait_ge(w_used, 2 * (KT * old[1] + old[2]) + old[3] + 1)
                        else:
                            act.wait_ge(mm_done, JOB[HALF_JOB[m - SPLIT]] + 1)
                    act.activation(whi[:, m % SPLIT, 0:kn, :],
                                   ring[:, SLOT[raw] % RING, 0:kn, P * half:P * half + P], ACT.Copy).then_inc(hi_done, 1)
                    halves[0] += 1

            def fill(point):
                for job in (FILL.get(point, []) if isinstance(point, tuple) else modulation_jobs(MOD_FIRST)):
                    if job[0] == "mod":
                        s = filled(act, job)
                        if rows[0]:
                            act.wait_ge(mm_done, JOB[("modt",) + rows[0]] + 1)
                        rows[0] = job[1:]
                        act.activation(mrow[:, :], s[0:2, 0:SLOT_N], ACT.Copy).then_inc(frees(job), 1)

            rows = [None]

            def norm_finish(l, k, src, dst):
                no = 2 * l + k // 2
                act.wait_ge(gains_ready, 3 if l else 1 + k // 2)
                shift = 0 if k == 0 else 24
                for i in range(KT):
                    act.wait_ge(h_half, 8 * no + i + 1)
                    ss = streams(l) if k else (0, 1)
                    for s in ss:
                        v = src[:, i, 256 * s:256 * s + 256]
                        link(act.activation(v, v, ACT.Identity, bias=mod[:, l, shift + i, s:s + 1],
                                            scale=amod[:, k, i, s:s + 1]))
                    c0, c1 = cols(l) if k else (0, T)
                    act.activation(dst[:, 0, i, c0:c1], src[:, i, c0:c1], ACT.Copy).then_inc(h_hi, 1)

            act.wait_ge(c_in, 16)
            act.activation(cvec[:, :, :], cvec[:, :, :], ACT.Silu).then_inc(silu_c, 1)
            act.wait_ge(x_in, 16)
            act.wait_ge(setup, 1)
            for i in range(KT):
                square(YB[:, i, :], X[:, i, :])
            norm_root(0, 0)
            fill(None)
            act.wait_ge(vec_in, 16)
            for l in range(LAYERS):
                c0, c1 = cols(l)
                W = c1 - c0
                ns = len(streams(l))
                for i in range(KT if l else 0):
                    act.wait_ge(x_ready, 8 + i + 1)
                    square(YB[:, i, :], X[:, i, :])
                split_until(half_no(("z", l, 0)) + SPLIT)
                if l:
                    norm_root(l, 0)
                norm_finish(l, 0, Z, HR)
                for t in range(ZT):
                    act.wait_ge(mm_done, JOB[("z", l, t)] + 1)
                    split_until(min(half_no(("z", l, t)) + 1 + SPLIT, half_no(("z", l, ZT - 1)) + 1))
                    if t not in ACT_Z:
                        continue
                    z0, z1 = cols(l, t)
                    s = filled(act, ("z", l, t))
                    if t in (Z_NQ, Z_NQ + 1):
                        if l == 0:
                            act.activation(Z[:, t, 0:CTX], s[:, 0:CTX], ACT.Copy)
                        act.activation(grid_rows(Z[:, t, CTX:T]), grid_rows(s[:, CTX:T])[:, :, ::-1], ACT.Copy)\
                           .then_inc(frees(("z", l, t)), 1)
                    else:
                        act.activation(Z[:, t, z0:z1], s[:, z0:z1], ACT.Copy).then_inc(frees(("z", l, t)), 1)
                for i in range(3):
                    z0, z1 = cols(l, Z_GQ + i)
                    emptied(act, ("z", l, Z_GQ + i))
                    if i >= 2:
                        act.wait_ge(mm_done, JOB[("qss", l, i - 2)] + 1)
                    dst = (qtmp, qtmp2)[i % 2]
                    act.activation(dst[:, z0:z1], Z[:, Z_GQ + i, z0:z1], ACT.Square).then_inc(qsq_ready, 1)
                for i in range(3):
                    z0, z1 = cols(l, Z_GQ + i)
                    s = filled(act, ("qss", l, i))
                    if i:
                        act.wait_ge(qn_ready, 3 * l + i)
                    act.activation(rt[:, z0:z1], s[:, z0:z1], ACT.Sqrt, bias=eps[:, 0:1], scale=1.0 / HD)\
                       .then_inc(frees(("qss", l, i)), 1)
                units = UNITS[l]
                act.wait_ge(h_saved[l], 32)
                for i in range(len(units) + 2):
                    if i < len(units):
                        g, h, q = units[i]
                        nk = T if q >= 2 else CTX
                        s = bank(("S", l, i))
                        src = sbuf2[:, i % 3, 0:nk] if g == "B" and q >= 2 else s[:, 0:nk]
                        act.wait_ge(nmax_ready, UBASE[l] + i + 1)
                        act.activation(pr[:, i % 3, 0:nk], src, ACT.Exp, bias=stat[:, 0, i % 4:i % 4 + 1],
                                       accum_out=stat[:, 1, i % 4:i % 4 + 1]).then_inc(frees(("S", l, i)), 1)
                    if l == 0:
                        fill(("att", i))
                    if i >= 2:
                        u = i - 2
                        nk = T if units[u][2] >= 2 else CTX
                        s = filled(act, ("T", l, u))
                        if u >= 3:
                            act.wait_ge(mm_done, JOB[("PV", l, u - 3)] + 1)
                        act.activation(prT[:, u % 3, 0:nk], s[:, 0:nk], ACT.Copy).then_inc(frees(("T", l, u)), 1)
                act.wait_ge(ya_ready, 2 * l + 2)
                act.wait_ge(mm_done, JOB[("PV", l, len(units) - 1)] + 1)
                for d in range(2):
                    it = 2 * l + d
                    if d == 1:
                        act.wait_ge(mm_done, JOB[("cy", l, 0, NCH - 1)] + 1)
                    step = 1 if d == 0 else -1
                    dsts = [zr[:, 0, :], zr[:, 1, :], zk[:, 0, :], zk[:, 1, :], vT[:, 0, :], vT[:, 1, :], lora]
                    for i in range(7):
                        emptied(act, ("z", l, Z_R + i))
                        src = Z[:, Z_R + i, :].rearrange("p (s t) -> p s t", s=2)[:, :, ::step]
                        act.activation(dsts[i].rearrange("p (s t) -> p s t", s=2), src, ACT.Copy,
                                       scale=omu[:, 7 * d + i:7 * d + i + 1]).then_inc(shift_half, 1)
                    act.wait_ge(shift_done, 7 * it + 7)
                    act.activation(lora[0:HD, :], lora[0:HD, :], ACT.Tanh).then_inc(tanh_done, 1)
                    for p in range(2):
                        s = filled(act, ("wl", l, d, p))
                        act.activation(sg[:, p, :], s, ACT.Sigmoid, bias=vc(l, "w0", 2 * d + p))\
                           .then_inc(frees(("wl", l, d, p)), 1)
                        s = filled(act, ("al", l, d, p))
                        act.activation(aa[:, p, :], s, ACT.Sigmoid, bias=vc(l, "a0", 2 * d + p))\
                           .then_inc(frees(("al", l, d, p)), 1)
                    if l == 0:
                        fill(("lora", d))
                    for p in range(2):
                        act.wait_ge(kraw_done, 2 * it + p + 1)
                        act.activation(t1[:, p, :], kk[:, p, :], ACT.Square).then_inc(ksq_done, 1)
                    for p in range(2):
                        act.wait_ge(scan_done, 4 * it + 2 * p + 2)
                        link(act.activation(wdec[:, p, :], G[:, p, :], ACT.Exp, scale=-DECAY))
                        link(act.activation(winv[:, p, :], G[:, p, :], ACT.Exp, scale=DECAY))
                        act.activation(wprev[:, p, :], t2[:, p, :], ACT.Exp, scale=-DECAY).then_inc(decay_done, 1)
                    def token_major(m, p):
                        s = filled(act, ("tok", l, d, m, p))
                        act.activation(tokm[m][:, :, 128 * p:128 * p + 128], s.rearrange("p (b n) -> p b n", b=NB),
                                       ACT.Copy).then_inc(frees(("tok", l, d, m, p)), 1)

                    if l:
                        act.wait_ge(x_saved, 32)
                    for p in range(2):
                        token_major("v", p)
                    for p in range(2):
                        emptied(act, ("kss", l, d, p))
                        link(act.activation(t2[:, p, :], t2[:, p, :], ACT.Ln))
                        act.activation(t1[:, p, :], t2[:, p, :], ACT.Exp, scale=-0.5).then_inc(kroot_done, 1)
                    if l == 0:
                        fill(("norm", d))
                    for p in range(2):
                        act.wait_ge(kap_done, 2 * it + p + 1)
                        for x in range(2):
                            act.activation(kapz(2 * p + x), zk[:, p, :], ACT.Copy,
                                           scale=K("heads")[:, HD * x:HD * x + 1]).then_inc(kapz_done, 1)
                    for p in range(2):
                        s = filled(act, ("bon", l, d, p))
                        act.activation((G if d else bon)[:, p, :], s, ACT.Copy).then_inc(frees(("bon", l, d, p)), 1)
                    for p in range(2):
                        token_major("k", p)
                    if l == 0:
                        fill(("bonus", d))
                    for p in range(2):
                        act.wait_ge(beta_done, 2 * it + p + 1)
                        for x in range(2):
                            act.activation(betaz[:, 2 * p + x, :], kk[:, p, :], ACT.Copy,
                                           scale=K("heads")[:, HD * x:HD * x + 1]).then_inc(betaz_done, 1)
                    for p in range(2):
                        for m in "ab":
                            token_major(m, p)
                    for p in range(2):
                        s = filled(act, ("xv", l, d, p))
                        act.activation(XV[:, 2 * p:2 * p + 2, :, :].rearrange("p h b n -> p (h b n)"), s, ACT.Copy)\
                           .then_inc(frees(("xv", l, d, p)), 1)
                    act.wait_ge(bonus_done, 2 * it + 2)
                    for p in range(2):
                        s = filled(act, ("at", l, d, p))
                        act.activation(AT[:, p, :], s, ACT.Copy).then_inc(frees(("at", l, d, p)), 1)
                    for p in range(2):
                        s = filled(act, ("u0", l, d, p))
                        act.activation(U0[:, 2 * p:2 * p + 2, :, :].rearrange("p h b n -> p (h b n)"), s, ACT.Copy)\
                           .then_inc(frees(("u0", l, d, p)), 1)
                for p in range(2):
                    emptied(act, ("mean", l, p))
                    act.activation(RO[:, p, c0:c1], YB[:, 6 + p, c0:c1], ACT.Square)\
                       .then_inc(ln_sq, 1)
                act.activation(siglg[:, c0:c1], siglg[:, c0:c1], ACT.Sigmoid).then_inc(lg_done, 1)
                for p in range(2):
                    s = filled(act, ("var", l, p))
                    act.activation(RO[:, 2 + p, c0:c1], s[:, c0:c1], ACT.Ln, bias=eps[:, 1:2], scale=1.0 / HD)\
                       .then_inc(frees(("var", l, p)), 1)
                    emptied(act, ("var", l, p))
                    act.activation(RO[:, 4 + p, c0:c1], RO[:, 2 + p, c0:c1], ACT.Exp, scale=-0.5)\
                       .then_inc(ln_root, 1)
                split_until(half_no(("gate", l, 0, 0)) + SPLIT)
                for J in range(4):
                    for i in range(4):
                        for j in (2 * J, 2 * J + 1):
                            no = 8 * J + 2 * i + (j - 2 * J)
                            s = filled(act, ("gate", l, j, i))
                            split_until(min(half_no(("gate", l, j, i)) + 1 + SPLIT, half_no(("wo", l, 0)) + SPLIT))
                            if i >= 2:
                                act.wait_ge(gated, added(l, j, i - 1))
                            elif i == 1:
                                emptied(act, ("br", l, j, 0))
                            elif J:
                                act.wait_ge(gated, added(l, j - 2, 3))
                            act.activation((rt, rs)[no % 2][:, c0:c1], s[:, c0:c1], ACT.Sigmoid,
                                           bias=vc(l, "b_gate", 8 * i + j))\
                               .then_inc(frees(("gate", l, j, i)), 1)
                    for j in (2 * J, 2 * J + 1):
                        act.wait_ge(gated, added(l, j, 3))
                        act.activation(AR[:, 0, j, c0:c1], ACC[:, j, c0:c1], ACT.Copy).then_inc(acc_hi, 1)
                for j in range(KT):
                    s = filled(act, ("wo", l, j))
                    split_until(min(half_no(("wo", l, j)) + 1 + SPLIT, half_no(("up", l, 0, 0)) + SPLIT * l))
                    act.activation(OB[:, j, c0:c1], s[:, c0:c1], ACT.Copy).then_inc(frees(("wo", l, j)), 1)
                    emptied(act, ("wo", l, j))
                    square(SQB[:, j, c0:c1], OB[:, j, c0:c1])
                if l == 0:
                    fill(("post",))
                norm_root(l, 1)
                if l == 0:
                    fill(("ffn",))
                    split_until(half_no(("up", l, 0, 0)) + SPLIT)
                for i in range(KT):
                    act.wait_ge(x_ready, 16 * l + i + 1)
                    square(SQB[:, i, c0:c1], X[:, i, c0:c1])
                norm_root(l, 2)
                norm_finish(l, 2, YB, H2)
                def product_hi(j):
                    act.wait_ge(u_ready, l * FT + j + 1)
                    if j == 20:
                        act.wait_ge(x_saved, 16 * (2 * l + 1))
                    act.activation(hidden(0, j)[:, c0:c1], CU[:, j % 2, c0:c1], ACT.Copy).then_inc(u_hi, 1)

                for j in range(FT):
                    for g in range(2):
                        s = filled(act, ("up", l, j, g))
                        split_until(min(half_no(("up", l, j, g)) + 1 + SPLIT, half_no(("down", l, 0)) + SPLIT))
                        if g == 0:
                            if j >= 2:
                                act.wait_ge(u_lo, l * FT + j - 1)
                            dst = CU[:, j % 2, c0:c1]
                        else:
                            dst = (rs, rt)[j % 2][:, c0:c1]
                        act.activation(dst, s[:, c0:c1], ACT.Copy, scale=vc(l, "ffn_conv", 44 + 22 * g + j))\
                           .then_inc(conv_half, 1)
                    if j:
                        product_hi(j - 1)
                    emptied(act, ("up", l, j, 1))
                    act.activation(dst, dst, ACT.Silu).then_inc(silu_done, 1)
                product_hi(FT - 1)
                for j in range(KT):
                    split_until(half_no(("down", l, j)) + (5 if j < KT - 1 else 3))
                    s = filled(act, ("down", l, j))
                    if j < KT - 1:
                        split_until(half_no(("down", l, j)) + 6)
                    act.activation(F[:, j, c0:c1], s[:, c0:c1], ACT.Copy).then_inc(frees(("down", l, j)), 1)
                    emptied(act, ("down", l, j))
                    square(SQF[:, j, c0:c1], F[:, j, c0:c1])
                norm_root(l, 3)

        @block.vector
        def _(dve):
            links = [0]

            def link(ins):
                links[0] += 1
                ins.then_inc(dve_chain, 1)
                dve.wait_ge(dve_chain, links[0])

            halves = [0]

            def split_until(n):
                while halves[0] < n:
                    m = halves[0]
                    raw, half = HALVES[m]
                    kn = FT % KT if raw[0] == "down" and raw[3] == 2 else KT
                    dve.wait_ge(hi_done, m + 1)
                    dve.tensor_tensor(wlo[:, m % SPLIT, 0:kn, :],
                                      ring[:, SLOT[raw] % RING, 0:kn, P * half:P * half + P],
                                      whi[:, m % SPLIT, 0:kn, :].bitcast(F32), ALU.subtract).then_inc(lo_done, 1)
                    halves[0] += 1

            def fill(point):
                for job in (FILL.get(point, []) if isinstance(point, tuple) else modulation_jobs(MOD_FIRST)):
                    if job[0] == "modt":
                        _, l, n = job
                        s = filled(dve, job)
                        b = vc(l, "ada_b", 2 * n, 2).unsqueeze(2).to_broadcast([P, 2, 2])
                        dve.tensor_tensor(mod[:, l, 2 * n:2 * n + 2, :], s[:, 0:4].rearrange("p (a s) -> p a s", a=2),
                                          b, ALU.add).then_inc(frees(job), 1)

            def gains(l, ks):
                for n in range(24):
                    if l or 0 not in ks or n < 8:
                        emptied(dve, ("modt", l, n))
                for k in ks:
                    m, g = ((8, "mix_pre"), (16, "mix_post"), (32, "ffn_pre"), (40, "ffn_post"))[k]
                    gb = vc(l, g, 0, 8).unsqueeze(2).to_broadcast([P, 8, 2])
                    if k % 2 == 0:
                        ins = dve.scalar_tensor_tensor(amod[:, k, :, :], mod[:, l, m:m + 8, :], 1.0, gb,
                                                       ALU.add, ALU.mult)
                    else:
                        ins = dve.tensor_tensor(amod[:, k, :, :], mod[:, l, m:m + 8, :], gb, ALU.mult)
                ins.then_inc(gains_ready, 1)
                called[0] += 1
                dve.wait_ge(gains_ready, called[0])

            called = [0]

            def norm_apply(l, k, src, tmp, dst):
                c0, c1 = cols(l) if k else (0, T)

                def low(i):
                    dve.wait_ge(h_hi, 8 * (2 * l + k // 2) + i + 1)
                    dve.tensor_tensor(dst[:, 1, i, c0:c1], tmp[:, i, c0:c1], dst[:, 0, i, c0:c1].bitcast(F32),
                                      ALU.subtract).then_inc(h_ready, 1)

                for i in range(KT):
                    if (l, k) != (0, 0):
                        over_rms(l, k, src, tmp, i)
                    if i >= 2:
                        low(i - 2)
                for i in range(KT - 2, KT):
                    low(i)

            def over_rms(l, k, src, tmp, i):
                c0, c1 = cols(l) if k else (0, T)
                dve.wait_ge(root_ready, norm_no(l, k) + 1)
                dve.tensor_tensor(tmp[:, i, c0:c1], src[:, i, c0:c1], rs[:, c0:c1], ALU.mult).then_inc(h_half, 1)

            def residual(l, k, O):
                c0, c1 = cols(l)
                dve.wait_ge(root_ready, norm_no(l, k) + 1)
                for i in range(KT):
                    link(dve.tensor_tensor(O[:, i, c0:c1], O[:, i, c0:c1], rs[:, c0:c1], ALU.mult))
                    for s in streams(l):
                        x = X[:, i, 256 * s:256 * s + 256]
                        ins = dve.scalar_tensor_tensor(x, O[:, i, 256 * s:256 * s + 256], amod[:, k, i, s:s + 1], x,
                                                       ALU.mult, ALU.add)
                        if s == 1:
                            ins.then_inc(x_ready, 1)

            link(dve.memset(eps[:, 0:1], EPS))
            dve.memset(eps[:, 1:2], LN_EPS).then_inc(setup, 1)
            dve.wait_ge(x_in, 16)
            for i in range(KT):
                over_rms(0, 0, X, Z, i)
            dve.wait_ge(const_in, 16)
            dve.wait_ge(vec_in, 16)
            for l in range(LAYERS):
                c0, c1 = cols(l)
                W = c1 - c0
                ns = len(streams(l))
                if l == 0:
                    fill(None)
                gains(l, (0, 1, 2, 3) if l else (0,))
                link(dve.tensor_scalar(omu[:, :], vc(l, "mu", 0, 14), -1.0, 1.0, ALU.mult, ALU.add))
                link(dve.tensor_scalar(oka[:, :], vc(l, "ka", 0, 2), -1.0, 1.0, ALU.mult, ALU.add))
                split_until(half_no(("z", l, 0)) + SPLIT)
                norm_apply(l, 0, X, Z, HR)
                dve.wait_ge(small_in[l], 16 * 9)
                win = K("window", GRID_W).unsqueeze(1).to_broadcast([P, HEADS * 6, GRID_W])
                bmf = bm[:, :, :, :].rearrange("p h r c -> p (h r) c")
                link(dve.tensor_tensor(bmf, bmf, win, ALU.add))
                for t in range(ZT):
                    split_until(min(half_no(("z", l, t)) + SPLIT, half_no(("z", l, ZT - 1)) + 1))
                    if t not in DVE_Z:
                        continue
                    z0, z1 = cols(l, t)
                    s = filled(dve, ("z", l, t))
                    dve.tensor_copy(Z[:, t, z0:z1], s[:, z0:z1]).then_inc(frees(("z", l, t)), 1)
                for i in range(3):
                    s = filled(dve, ("vt", l, i))
                    dst = vB[:, :, 128 * i:128 * i + 128] if i < 2 else vC
                    dve.tensor_copy(dst, s.rearrange("p (b n) -> p b n", b=4)).then_inc(frees(("vt", l, i)), 1)
                for p in range(2):
                    z0, z1 = cols(l, Z_NQ + p)
                    emptied(dve, ("z", l, Z_NQ + p))
                    v = Z[:, Z_NQ + p, z0:z1]
                    dve.tensor_scalar(v, v, HD ** -0.5, None, ALU.mult).then_inc(q_scaled, 1)
                for i in range(3):
                    z0, z1 = cols(l, Z_GQ + i)
                    emptied(dve, ("qss", l, i))
                    link(dve.reciprocal(rs[:, z0:z1], rt[:, z0:z1]))
                    v = Z[:, Z_GQ + i, z0:z1]
                    g = vc(l, "q_norm") if i < 2 else vc(l, "k_norm")
                    if i < 2:
                        link(dve.tensor_scalar(v, v, g, HD ** -0.5, ALU.mult, ALU.mult))
                        dve.tensor_tensor(v, v, rs[:, z0:z1], ALU.mult).then_inc(qn_ready, 1)
                    else:
                        dve.scalar_tensor_tensor(v, v, g, rs[:, z0:z1], ALU.mult, ALU.mult).then_inc(qn_ready, 1)
                for i in range(3):
                    v = Z[:, Z_GQ + i, CTX:T]
                    s = filled(dve, ("qsw", l, i))
                    dve.wait_ge(mm_done, JOB[("qss", l, 2)] + 1)
                    dve.tensor_tensor(qtmp[:, 0:LAT], s[:, 0:LAT], K("sin", LAT), ALU.mult)\
                       .then_inc(frees(("qsw", l, i)), 1)
                    dve.wait_ge(qn_ready, 3 * l + i + 1)
                    link(dve.tensor_tensor(v, v, K("cos", LAT), ALU.mult))
                    emptied(dve, ("qsw", l, i))
                    dve.tensor_tensor(v, v, qtmp[:, 0:LAT], ALU.add).then_inc(qk_ready, 1)
                    dve.wait_ge(qk_ready, 3 * l + i + 1)
                dve.wait_ge(ya_ready, 2 * l + 2)
                for h in range(HEADS):
                    emptied(dve, ("z", l, Z_NK + h // 2))
                    dve.tensor_scalar(KZ[:, h, :], Z[:, Z_NK + h // 2, :], K("heads")[:, HD * (h % 2):HD * (h % 2) + 1],
                                      None, ALU.mult).then_inc(kz_ready, 1)
                for g in range(2):
                    dve.tensor_scalar(KZ[:, 4 + g, :], Z[:, Z_GK, :], K("heads")[:, HD * g:HD * g + 1],
                                      None, ALU.mult).then_inc(kz_ready, 1)
                units = UNITS[l]
                for i in range(len(units) + 3):
                    if i < len(units):
                        g, h, q = units[i]
                        nk = T if q >= 2 else CTX
                        s = filled(dve, ("S", l, i))
                        src = s[:, 0:nk]
                        if g == "B" and q >= 2:
                            r0 = 2 if q == 2 else 0
                            if i >= 3:
                                emptied(dve, ("S", l, i - 3))
                            link(dve.tensor_copy(sbuf2[:, i % 3, 0:CTX], s[:, 0:CTX]))
                            link(dve.tensor_tensor(sbuf2[:, i % 3, CTX:T], s[:, CTX:T],
                                                   bm[:, h, r0:r0 + 4, :].rearrange("p r c -> p (r c)"), ALU.add))
                            src = sbuf2[:, i % 3, :]
                        dve.tensor_reduce(stat[:, 0, i % 4:i % 4 + 1], src, AX, ALU.max, negate=True)\
                           .then_inc(nmax_ready, 1)
                    if 1 <= i <= len(units):
                        u = i - 1
                        emptied(dve, ("S", l, u))
                        dve.reciprocal(stat[:, 2, u % 4:u % 4 + 1], stat[:, 1, u % 4:u % 4 + 1]).then_inc(p_sum, 1)
                    if l == 0:
                        fill(("att", i))
                    if i >= 3:
                        g, h, q = units[i - 3]
                        half = slice(HD * (h % 2), HD * (h % 2) + HD)
                        s = filled(dve, ("PV", l, i - 3))
                        dst = YB[half, (2 if g == "B" else 4) + h // 2, 128 * q:128 * q + 128]
                        src = s[half, 0:128]
                        if g == "B" and q >= 2:
                            dst, src = grid_rows(dst), grid_rows(src)[:, :, ::-1]
                        dve.tensor_copy(dst, src).then_inc(frees(("PV", l, i - 3)), 1)
                for d in range(2):
                    it = 2 * l + d
                    step = 1 if d == 0 else -1
                    dsts = [zr[:, 0, :], zr[:, 1, :], zk[:, 0, :], zk[:, 1, :], vT[:, 0, :], vT[:, 1, :], lora]
                    for i in range(7):
                        dve.wait_ge(shift_half, 7 * it + i + 1)
                        z = Z[:, Z_R + i, :].rearrange("p (s t) -> p s t", s=2)[:, :, ::step]
                        o = dsts[i].rearrange("p (s t) -> p s t", s=2)[:, :, 1:256]
                        dve.scalar_tensor_tensor(o, z[:, :, 0:255], vc(l, "mu", 7 * d + i), o, ALU.mult, ALU.add)\
                           .then_inc(shift_done, 1)
                    dve.wait_ge(shift_done, 7 * it + 7)
                    for p in range(2):
                        dve.tensor_scalar(kk[:, p, :], zk[:, p, :], vc(l, "kk", p), None, ALU.mult)\
                           .then_inc(kraw_done, 1)
                    for p in range(2):
                        emptied(dve, ("wl", l, d, p))
                        dve.tensor_tensor_scan(G[:, p, :], K("reset", T), sg[:, p, :], 0.0, ALU.mult, ALU.add)\
                           .then_inc(scan_done, 1)
                        dve.wait_ge(scan_done, 4 * it + 2 * p + 1)
                        dve.tensor_tensor(t2[:, p, :], G[:, p, :], sg[:, p, :], ALU.subtract).then_inc(scan_done, 1)
                    if l == 0:
                        fill(("lora", d))
                    for p in range(2):
                        dve.wait_ge(decay_done, 2 * it + 2)
                        s = filled(dve, ("kss", l, d, p))
                        dve.tensor_scalar(t2[:, p, :], s, 1e-24, KK_SCALE ** 2, ALU.max, ALU.mult)\
                           .then_inc(frees(("kss", l, d, p)), 1)
                    for p in range(2):
                        emptied(dve, ("al", l, d, p))
                        link(dve.tensor_scalar(sg[:, p, :], aa[:, p, :], vc(l, "ka", p), oka[:, p:p + 1],
                                               ALU.mult, ALU.add))
                        link(dve.tensor_tensor(zk[:, p, :], zk[:, p, :], sg[:, p, :], ALU.mult))
                        dve.scalar_tensor_tensor(sg[:, p, :], zr[:, p, :], vc(l, "rk", p), zk[:, p, :],
                                                 ALU.mult, ALU.mult).then_inc(bonus_in, 1)
                        dve.wait_ge(bonus_in, 2 * it + p + 1)
                        dve.tensor_tensor(zk[:, p, :], zk[:, p, :], winv[:, p, :], ALU.mult).then_inc(kap_done, 1)
                        blk = lambda v: v.rearrange("p (b t) -> p b t", b=NB)
                        link(dve.tensor_tensor(ar[:, p, :, 1, :], blk(zr[:, p, :]), blk(wdec[:, p, :]), ALU.mult))
                    if l == 0:
                        fill(("norm", d))
                    for p in range(2):
                        dve.wait_ge(kroot_done, 2 * it + p + 1)
                        link(dve.scalar_tensor_tensor(kk[:, p, :], kk[:, p, :], KK_SCALE, t1[:, p, :],
                                                      ALU.mult, ALU.mult))
                        link(dve.tensor_tensor(ar[:, p, :, 0, :], blk(kk[:, p, :]), blk(wprev[:, p, :]), ALU.mult))
                        link(dve.tensor_tensor(kk[:, p, :], kk[:, p, :], aa[:, p, :], ALU.mult))
                        dve.tensor_tensor(kk[:, p, :], kk[:, p, :], winv[:, p, :], ALU.mult).then_inc(beta_done, 1)
                    link(dve.tensor_copy(wend[:, :, :], wdec[:, :, CH - 1::CH]))
                    dve.memset(state[:, 0, :, :], 0.0).then_inc(streams_done, 1)
                    if l == 0:
                        fill(("bonus", d))
                    lm = K("lm", 2 * P).unsqueeze(1).to_broadcast([P, 2, 2 * P])
                    m1 = K("m1").unsqueeze(1).to_broadcast([P, NB, P])
                    m1t = K("m1t").unsqueeze(1).to_broadcast([P, NB, P])
                    for h in range(HEADS):
                        for b in range(2):
                            s = filled(dve, ("LM1", l, d, h, b)).rearrange("p (b n) -> p b n", b=2)
                            dve.tensor_tensor(LM1[:, h, 2 * b:2 * b + 2, :], s, lm, ALU.mult)\
                               .then_inc(frees(("LM1", l, d, h, b)), 1)
                        s = filled(dve, ("L1", l, d, h)).rearrange("p (b n) -> p b n", b=NB)
                        dve.tensor_tensor(TN[:, h, :, :], s, m1, ALU.mult).then_inc(frees(("L1", l, d, h)), 1)
                        for b in range(2):
                            emptied(dve, ("LM1", l, d, h, b))
                        dve.tensor_tensor(TT[:, h, :, :], LM1[:, h, :, 0:P], m1t, ALU.mult).then_inc(tt_masked, 1)
                    for zi, z in enumerate(LEVELS):
                        mz = K(f"m{z}").unsqueeze(1).to_broadcast([P, NB, P])
                        for h in range(HEADS):
                            s = filled(dve, ("sx", l, d, z, h)).rearrange("p (b n) -> p b n", b=NB)
                            dve.tensor_tensor(XS[:, h, :, :], s, mz, ALU.mult).then_inc(frees(("sx", l, d, z, h)), 1)
                        if zi < HEADS:
                            dve.wait_ge(bonus_done, 2 * it + 2)
                            for b in range(2):
                                s = filled(dve, ("LM2", l, d, zi, b)).rearrange("p (b n) -> p b n", b=2)
                                dve.tensor_tensor(LM2[:, zi, 2 * b:2 * b + 2, :], s, lm, ALU.mult)\
                                   .then_inc(frees(("LM2", l, d, zi, b)), 1)
                        for h in range(HEADS):
                            if z != LEVELS[-1]:
                                s = filled(dve, ("sy", l, d, z, h)).rearrange("p (b n) -> p b n", b=NB)
                                dve.tensor_tensor(TN[:, h, :, :], TN[:, h, :, :], s, ALU.subtract)\
                                   .then_inc(frees(("sy", l, d, z, h)), 1)
                            s = filled(dve, ("syt", l, d, z, h)).rearrange("p (b n) -> p b n", b=NB)
                            dve.tensor_tensor(TT[:, h, :, :], TT[:, h, :, :], s, ALU.subtract)\
                               .then_inc(frees(("syt", l, d, z, h)), 1)
                    for p in range(2):
                        emptied(dve, ("u0", l, d, p))
                    for c in range(NCH):
                        q = slice(HD * (c % 2), HD * (c % 2) + HD)
                        s = filled(dve, ("cu", l, d, c))
                        dve.scalar_tensor_tensor(nu[q, :, :], s[q, 0:256].rearrange("p (h n) -> p h n", h=HEADS),
                                                 -1.0, U0[q, :, c // 2, :], ALU.mult, ALU.subtract)\
                           .then_inc(frees(("cu", l, d, c)), 1)
                        if c < NCH - 1:
                            s = filled(dve, ("ch", l, d, c))
                            for p in range(2):
                                ins = dve.scalar_tensor_tensor(state[:, (c + 1) % 2, p, :], s[:, P * p:P * p + P],
                                                               wend[:, p, c:c + 1], K("heads"), ALU.mult, ALU.mult)
                            ins.then_inc(frees(("ch", l, d, c)), 1)
                        if l == 0 or c >= NCH // 2:
                            s = filled(dve, ("cy", l, d, c))[:, 0:128].rearrange("p (a t) -> p a t", a=2)
                            if d == 0:
                                dve.tensor_copy(YB[:, 6:8, CH * c:CH * c + CH], s)\
                                   .then_inc(frees(("cy", l, d, c)), 1)
                            else:
                                st, r = c // 4, c % 4
                                e = 256 * st + 256 - CH * r
                                y = YB[:, 6:8, e - CH:e]
                                dve.tensor_tensor(y, y, s[:, :, ::-1], ALU.add).then_inc(frees(("cy", l, d, c)), 1)
                for p in range(2):
                    y = YB[:, 6 + p, c0:c1]
                    s = filled(dve, ("mean", l, p))
                    dve.scalar_tensor_tensor(y, s[:, c0:c1], -1.0 / HD, y, ALU.mult, ALU.add)\
                       .then_inc(frees(("mean", l, p)), 1)
                for p in range(2):
                    y = YB[:, 6 + p, c0:c1]
                    dve.wait_ge(ln_root, 2 * l + p + 1)
                    link(dve.scalar_tensor_tensor(y, y, vc(l, "ln_w", p), RO[:, 4 + p, c0:c1], ALU.mult, ALU.mult))
                    link(dve.scalar_tensor_tensor(y, y, vc(l, "ln_b", p), bon[:, p, c0:c1], ALU.add, ALU.add))
                    s = filled(dve, ("g2", l, p))
                    dve.tensor_tensor(y, y, s[:, c0:c1], ALU.mult).then_inc(frees(("g2", l, p)), 1)
                split_until(half_no(("gate", l, 0, 0)) + SPLIT)
                for J in range(4):
                    for i in range(4):
                        for j in (2 * J, 2 * J + 1):
                            split_until(min(half_no(("gate", l, j, i)) + SPLIT, half_no(("wo", l, 0)) + SPLIT))
                            no = 8 * J + 2 * i + (j - 2 * J)
                            gt = (rt, rs)[no % 2][:, c0:c1]
                            s = filled(dve, ("br", l, j, i))[:, c0:c1]
                            emptied(dve, ("gate", l, j, i))
                            o = ACC[:, j, c0:c1]
                            dst = o if i == 0 else gt
                            dve.tensor_tensor(dst, gt, s, ALU.mult).then_inc(frees(("br", l, j, i)), 1)
                            emptied(dve, ("br", l, j, i))
                            if i:
                                dve.tensor_tensor(o, o, gt, ALU.add).then_inc(gated, 1)
                    for j in (2 * J, 2 * J + 1):
                        dve.wait_ge(acc_hi, 8 * l + j + 1)
                        dve.tensor_tensor(AR[:, 1, j, c0:c1], ACC[:, j, c0:c1], AR[:, 0, j, c0:c1].bitcast(F32),
                                          ALU.subtract).then_inc(acc_lo, 1)
                for j in range(KT):
                    split_until(min(half_no(("wo", l, j)) + 1 + SPLIT, half_no(("up", l, 0, 0)) + SPLIT * l))
                if l == 0:
                    fill(("post",))
                    fill(("ffn",))
                    gains(0, (1, 2, 3))
                    split_until(half_no(("up", l, 0, 0)) + SPLIT)
                dve.wait_ge(x_back, 32 * l + 16)
                residual(l, 1, OB)
                dve.wait_ge(x_ready, 16 * l + 8)
                norm_apply(l, 2, X, YB, H2)
                def product_lo(j):
                    dve.wait_ge(u_hi, l * FT + j + 1)
                    dve.tensor_tensor(hidden(1, j)[:, c0:c1], CU[:, j % 2, c0:c1],
                                      hidden(0, j)[:, c0:c1].bitcast(F32), ALU.subtract).then_inc(u_lo, 1)

                for j in range(FT):
                    for g in range(2):
                        split_until(min(half_no(("up", l, j, g)) + SPLIT, half_no(("down", l, 0)) + SPLIT))
                        dve.wait_ge(conv_half, 2 * (FT * l + j) + g + 1)
                        s = bank(("up", l, j, g))[:, c0:c1].rearrange("p (s t) -> p s t", s=ns)
                        o = (CU[:, j % 2, c0:c1] if g == 0 else (rs, rt)[j % 2][:, c0:c1])\
                            .rearrange("p (s t) -> p s t", s=ns)
                        link(dve.scalar_tensor_tensor(o[:, :, 1:256], s[:, :, 0:255], vc(l, "ffn_conv", 22 * g + j),
                                                      o[:, :, 1:256], ALU.mult, ALU.add))
                        dve.scalar_tensor_tensor(o[:, :, 0:255], s[:, :, 1:256], vc(l, "ffn_conv", 88 + 22 * g + j),
                                                 o[:, :, 0:255], ALU.mult, ALU.add).then_inc(frees(("up", l, j, g)), 1)
                    if j:
                        product_lo(j - 1)
                product_lo(FT - 1)
                split_until(half_no(("down", l, 0)) + 3 * KT)
                for j in range(KT):
                    emptied(dve, ("down", l, j))
                dve.wait_ge(x_back, 32 * (l + 1))
                residual(l, 3, F)
                dve.wait_ge(x_ready, 16 * l + 16)

        @block.tensor
        def _(pe):
            def job(name, ahead=0):
                g = JOB[name]
                assert g == count[0] + ahead, (name, g, count[0])
                if g >= NBANK:
                    pe.wait_ge(bank_free[g % NBANK], g // NBANK)
                return ps[:, g % NBANK, :]

            count = [0]

            def done(ins):
                count[0] += 1
                ins.then_inc(mm_done, 1)

            def weights(name):
                n = SLOT[name]
                pe.wait_ge(w_in_slot[n % RING], 16 * (n // RING + 1))
                return ring[:, n % RING, :, :]

            def sum_squares(l, k, src):
                c0, c1 = cols(l) if k else (0, T)
                o = job(("ss", l, k))
                for i in range(KT):
                    pe.wait_ge(sq_ready, 8 * norm_no(l, k) + i + 1)
                    last = pe.matmul(o[:, c0:c1], K("ones"), src[:, i, c0:c1], start=(i == 0), stop=(i == KT - 1))
                done(last)

            def halves(name):
                for raw in blocks_of(name):
                    m = HALF[raw]
                    pe.wait_ge(lo_done, m + 1)
                    yield whi[:, m % SPLIT, :, :], wlo[:, m % SPLIT, :, :]

            def project(name, part, c0, c1, kn=KT, made=None):
                o = job(name)
                k = 0
                for hi, lo in halves(name):
                    for i in range(min(KT, kn - k)):
                        if made:
                            pe.wait_ge(made[0], made[1] + k + 1)
                        pe.matmul(o[:, c0:c1], hi[:, i, :], part(0, k), start=(k == 0), stop=False)
                        pe.matmul(o[:, c0:c1], hi[:, i, :], part(1, k), start=False, stop=False)
                        last = pe.matmul(o[:, c0:c1], lo[:, i, :], part(0, k), start=False, stop=(k == kn - 1))
                        k += 1
                    if k < kn:
                        last.then_inc(w_used, 1)
                done(last)

            def fill(point):
                for name in (FILL.get(point, []) if isinstance(point, tuple) else modulation_jobs(MOD_FIRST)):
                    if name[0] == "mod":
                        w = weights(("ada",) + name[1:])
                        o = job(name)
                        for k in range(KT):
                            last = pe.matmul(o[0:2, 0:SLOT_N], cvec[:, k, :], w[:, k, :],
                                             start=(k == 0), stop=(k == KT - 1))
                    else:
                        emptied(pe, ("mod",) + name[1:])
                        o = job(name)
                        for x in range(2):
                            last = pe.transpose(o[:, 2 * x:2 * x + 2], mrow[:, P * x:P * x + P], K("ident")[0:2, 0:2])
                    done(last)

            pe.wait_ge(const_in, 16)
            for l in range(LAYERS):
                c0, c1 = cols(l)
                sum_squares(l, 0, YB)
                if l == 0:
                    pe.wait_ge(silu_c, 1)
                    fill(None)
                for t in range(ZT):
                    z0, z1 = cols(l, t)
                    project(("z", l, t), lambda x, k: HR[:, x, k, z0:z1], z0, z1,
                            made=None if t else (h_ready, 16 * l))
                for i in range(3):
                    t = Z_NV + i if i < 2 else Z_GV
                    emptied(pe, ("z", l, t))
                    o = job(("vt", l, i))
                    for b in range(4):
                        last = pe.transpose(o[:, 128 * b:128 * b + 128], Z[:, t, 128 * b:128 * b + 128], K("ident"))
                    done(last)
                for i in range(3):
                    z0, z1 = cols(l, Z_GQ + i)
                    o = job(("qss", l, i))
                    pe.wait_ge(qsq_ready, 3 * l + i + 1)
                    done(pe.matmul(o[:, z0:z1], K("heads"), (qtmp, qtmp2)[i % 2][:, z0:z1], start=True, stop=True))
                for i in range(3):
                    o = job(("qsw", l, i))
                    pe.wait_ge(qn_ready, 3 * l + i + 1)
                    done(pe.matmul(o[:, 0:LAT], K("swap"), Z[:, Z_GQ + i, CTX:T], start=True, stop=True))
                pe.wait_ge(q_scaled, 2 * l + 2)
                pe.wait_ge(qk_ready, 3 * l + 3)
                pe.wait_ge(kz_ready, 6 * l + 6)
                for i in range(3):
                    emptied(pe, ("vt", l, i))
                units = UNITS[l]
                for i in range(len(units) + 3):
                    if i < len(units):
                        g, h, q = units[i]
                        nk = T if q >= 2 else CTX
                        tq, tk = (Z_NQ + h // 2, h) if g == "B" else (Z_GQ + h % 2, 4 + h // 2)
                        o = job(("S", l, i))
                        done(pe.matmul(o[:, 0:nk], Z[:, tq, 128 * q:128 * q + 128], KZ[:, tk, 0:nk],
                                       start=True, stop=True))
                    if l == 0:
                        fill(("att", i))
                    if 2 <= i <= len(units) + 1:
                        u = i - 2
                        nt = (T if units[u][2] >= 2 else CTX) // P
                        o = job(("T", l, u))
                        pe.wait_ge(p_ready, UBASE[l] + u + 1)
                        for b in range(nt):
                            last = pe.transpose(o[:, 128 * b:128 * b + 128], pr[:, u % 3, 128 * b:128 * b + 128],
                                                K("ident"))
                        done(last)
                    if i >= 3:
                        g, h, q = units[i - 3]
                        nt = (T if q >= 2 else CTX) // P
                        o = job(("PV", l, i - 3))
                        emptied(pe, ("T", l, i - 3))
                        half = slice(HD * (h % 2), HD * (h % 2) + HD)
                        for b in range(nt):
                            v = vB[:, b, HD * h:HD * h + HD] if g == "B" else vC[:, b, HD * (h // 2):HD * (h // 2) + HD]
                            last = pe.matmul(o[half, 0:128], v, prT[:, (i - 3) % 3, 128 * b:128 * b + 128],
                                             start=(b == 0), stop=(b == nt - 1))
                        done(last)
                for d in range(2):
                    it = 2 * l + d
                    pe.wait_ge(small_in[l], 16 * 9)

                    def token_major(m, p, src):
                        o = job(("tok", l, d, m, p))
                        for b in range(NB):
                            last = pe.transpose(o[:, 128 * b:128 * b + 128], src[:, 128 * b:128 * b + 128], K("ident"))
                        done(last)

                    def products(name, h, lhs):
                        for b in range(2):
                            o = job((name, l, d, h, b))
                            for x in range(2):
                                bb = 2 * b + x
                                last = pe.matmul(o[:, 256 * x:256 * x + 256], lhs[:, 128 * bb:128 * bb + 128],
                                                 ar[:, h // 2, bb, :, :].rearrange("p a t -> p (a t)"),
                                                 start=True, stop=True)
                            done(last)

                    for p in range(2):
                        pe.wait_ge(tanh_done, it + 1)
                        o = job(("wl", l, d, p))
                        done(pe.matmul(o, w2a2[0:HD, d, 128 * p:128 * p + 128], lora[0:HD, :], start=True, stop=True))
                        o = job(("al", l, d, p))
                        done(pe.matmul(o, w2a2[HD:P, d, 128 * p:128 * p + 128], lora[HD:P, :], start=True, stop=True))
                    if l == 0:
                        fill(("lora", d))
                    for p in range(2):
                        pe.wait_ge(ksq_done, 2 * it + p + 1)
                        o = job(("kss", l, d, p))
                        done(pe.matmul(o, K("heads"), t1[:, p, :], start=True, stop=True))
                    pe.wait_ge(shift_done, 7 * it + 6)
                    for p in range(2):
                        token_major("v", p, vT[:, p, :])
                    if l == 0:
                        fill(("norm", d))
                    for p in range(2):
                        pe.wait_ge(bonus_in, 2 * it + p + 1)
                        o = job(("bon", l, d, p))
                        done(pe.matmul(o, K("heads"), sg[:, p, :], start=True, stop=True))
                    for p in range(2):
                        pe.wait_ge(kap_done, 2 * it + p + 1)
                        token_major("k", p, zk[:, p, :])
                    if l == 0:
                        fill(("bonus", d))
                    for h in range(HEADS):
                        p = h // 2
                        pe.wait_ge(betaz_done, 4 * it + h + 1)
                        products("LM1", h, betaz[:, h, :])
                        o = job(("L1", l, d, h))
                        for b in range(NB):
                            last = pe.matmul(o[:, 128 * b:128 * b + 128], ar[:, p, b, 0, :],
                                             betaz[:, h, 128 * b:128 * b + 128], start=True, stop=True)
                        done(last)
                        if h % 2:
                            pe.wait_ge(beta_done, 2 * it + p + 1)
                            o = job(("tok", l, d, "a", p))
                            for b in range(NB):
                                last = pe.transpose(o[:, 128 * b:128 * b + 128], ar[:, p, b, 0, :], K("ident"))
                            done(last)
                            token_major("b", p, kk[:, p, :])
                    pe.wait_ge(kapz_done, 4 * it + 4)
                    for zi, z in enumerate(LEVELS):
                        for h in range(HEADS):
                            if zi:
                                emptied(pe, ("sy", l, d, LEVELS[zi - 1], h))
                            else:
                                pe.wait_ge(t_done, 8 * it + 2 * h + 1)
                                for b in range(2):
                                    emptied(pe, ("LM1", l, d, h, b))
                            o = job(("sx", l, d, z, h))
                            for b in range(NB):
                                last = pe.matmul(o[:, 128 * b:128 * b + 128], LM1[:, h, b, 0:P], TN[:, h, b, :],
                                                 start=True, stop=True)
                            done(last)
                        if zi < HEADS:
                            products("LM2", zi, kapz(zi))
                        else:
                            for h in range(HEADS):
                                for b in range(2):
                                    emptied(pe, ("LM2", l, d, h, b))
                            for p in range(2):
                                emptied(pe, ("tok", l, d, "v", p))
                            for p in range(2):
                                o = job(("xv", l, d, p))
                                for x in range(2):
                                    for b in range(NB):
                                        h = 2 * p + x
                                        last = pe.matmul(o[:, 256 * x + 64 * b:256 * x + 64 * b + 64],
                                                         LM2[:, h, b, 0:P], tokm["v"][:, b, HD * h:HD * h + HD],
                                                         start=True, stop=True)
                                done(last)
                        for h in range(HEADS):
                            if zi == 0:
                                pe.wait_ge(t_done, 8 * it + 2 * h + 2)
                            emptied(pe, ("sx", l, d, z, h))
                            if zi:
                                emptied(pe, ("syt", l, d, LEVELS[zi - 1], h))
                            if z != LEVELS[-1]:
                                o = job(("sy", l, d, z, h))
                                for b in range(NB):
                                    last = pe.matmul(o[:, 128 * b:128 * b + 128], TT[:, h, b, :], XS[:, h, b, :],
                                                     start=True, stop=True)
                                done(last)
                            o = job(("syt", l, d, z, h))
                            for b in range(NB):
                                last = pe.matmul(o[:, 128 * b:128 * b + 128], XS[:, h, b, :], TT[:, h, b, :],
                                                 start=True, stop=True)
                            done(last)
                    for h in range(HEADS):
                        emptied(pe, ("syt", l, d, LEVELS[-1], h))
                    for m in "akbv":
                        for p in range(2):
                            emptied(pe, ("tok", l, d, m, p))
                    for p in range(2):
                        o = job(("at", l, d, p))
                        for x in range(2):
                            for b in range(NB):
                                h = 2 * p + x
                                last = pe.matmul(o[HD * x:HD * x + HD, 128 * b:128 * b + 128],
                                                 tokm["a"][:, b, HD * h:HD * h + HD], TT[:, h, b, :],
                                                 start=True, stop=True)
                        done(last)
                    for p in range(2):
                        emptied(pe, ("xv", l, d, p))
                        o = job(("u0", l, d, p))
                        for x in range(2):
                            for b in range(NB):
                                h = 2 * p + x
                                last = pe.matmul(o[:, 256 * x + 64 * b:256 * x + 64 * b + 64], TT[:, h, b, :],
                                                 XV[:, h, b, :], start=True, stop=True)
                        done(last)
                    for p in range(2):
                        emptied(pe, ("at", l, d, p))
                    pe.wait_ge(streams_done, it + 1)
                    for c in range(NCH):
                        b, qs = c // 2, slice(HD * (c % 2), HD * (c % 2) + HD)
                        tc = slice(HD * (c % 2), HD * (c % 2) + HD)
                        cs = slice(CH * c, CH * c + CH)
                        o = job(("cu", l, d, c))
                        if c:
                            emptied(pe, ("ch", l, d, c - 1))
                        for p in range(2):
                            last = pe.matmul(o[qs, P * p:P * p + P], AT[:, p, cs], state[:, c % 2, p, :],
                                             start=True, stop=True)
                        done(last)
                        mc = slice(P + CH * (c % 2), P + CH * (c % 2) + CH)
                        carried, read = c < NCH - 1, l == 0 or c >= NCH // 2
                        if carried:
                            och = job(("ch", l, d, c))
                            for p in range(2):
                                dst, hs = och[:, P * p:P * p + P], slice(P * p, P * p + P)
                                pe.matmul(dst, K("ident"), state[:, c % 2, p, :], start=(p == 0), stop=(p == 0),
                                          skip_group_check=True)
                                pe.matmul(dst, tokm["k"][qs, b, hs], tokm["v"][qs, b, hs], start=False, stop=False,
                                          skip_group_check=True)
                        if read:
                            ocy = job(("cy", l, d, c), 1 if carried else 0)
                            for p in range(2):
                                dst = ocy[:, CH * p:CH * p + CH]
                                pe.matmul(dst, state[:, c % 2, p, :], ar[:, p, b, 1, tc], start=(p == 0), stop=(p == 0),
                                          skip_group_check=True)
                                for h in (2 * p, 2 * p + 1):
                                    r, hs = slice(HD * (h % 2), HD * (h % 2) + HD), slice(HD * h, HD * h + HD)
                                    pe.matmul(dst[r, :], tokm["v"][qs, b, hs], LM2[qs, h, b, mc],
                                              start=False, stop=False, skip_group_check=True)
                        emptied(pe, ("cu", l, d, c))
                        if carried:
                            for p in range(2):
                                dst, hs = och[:, P * p:P * p + P], slice(P * p, P * p + P)
                                last = pe.matmul(dst, tokm["b"][qs, b, hs],
                                                 nu[qs, 2 * p:2 * p + 2, :].rearrange("p h n -> p (h n)"),
                                                 start=False, stop=False, skip_group_check=True)
                            done(last)
                        if read:
                            for h in range(HEADS):
                                dst = ocy[HD * (h % 2):HD * (h % 2) + HD, CH * (h // 2):CH * (h // 2) + CH]
                                last = pe.matmul(dst, nu[qs, h, :], LM1[qs, h, b, mc],
                                                 start=False, stop=False, skip_group_check=True)
                            done(last)
                for p in range(2):
                    emptied(pe, ("cy", l, 1, NCH - 1))
                    o = job(("mean", l, p))
                    done(pe.matmul(o[:, c0:c1], K("heads"), YB[:, 6 + p, c0:c1], start=True, stop=True))
                for p in range(2):
                    pe.wait_ge(ln_sq, 2 * l + p + 1)
                    o = job(("var", l, p))
                    done(pe.matmul(o[:, c0:c1], K("heads"), RO[:, p, c0:c1], start=True, stop=True))
                pe.wait_ge(lg_done, l + 1)
                pe.wait_ge(g2_in, 16 * (l + 1))
                for p in range(2):
                    o = job(("g2", l, p))
                    done(pe.matmul(o[:, c0:c1], g2[:, 128 * p:128 * p + 128], siglg[:, c0:c1], start=True, stop=True))
                pe.wait_ge(ya_ready, 2 * l + 2)
                for i in range(len(units)):
                    if i >= len(units) - NBANK:
                        emptied(pe, ("PV", l, i))
                for p in range(2):
                    emptied(pe, ("g2", l, p))
                pe.wait_ge(h_back[l], 32)
                for J in range(4):
                    for i in range(4):
                        for j in (2 * J, 2 * J + 1):
                            project(("gate", l, j, i), lambda x, k: HR[:, x, k, c0:c1], c0, c1)
                            wb = WB[:, J % 2, :, :]
                            pe.wait_ge(wb_in, 16 * (4 * l + J + 1))
                            o = job(("br", l, j, i))
                            for k in range(2):
                                last = pe.matmul(o[:, c0:c1], wb[:, 2 * i + k, P * (j % 2):P * (j % 2) + P],
                                                 YB[:, 2 * i + k, c0:c1], start=(k == 0), stop=(k == 1))
                            done(last)
                for j in range(KT):
                    project(("wo", l, j), lambda x, k: AR[:, x, k, c0:c1], c0, c1,
                            made=None if j else (acc_lo, 8 * l))
                if l == 0:
                    fill(("post",))
                sum_squares(l, 1, SQB)
                if l == 0:
                    fill(("ffn",))
                sum_squares(l, 2, SQB)
                for j in range(FT):
                    for g in range(2):
                        project(("up", l, j, g), lambda x, k: H2[:, x, k, c0:c1], c0, c1,
                                made=None if j or g else (h_ready, 16 * l + 8))
                for j in range(KT):
                    project(("down", l, j), lambda x, k: hidden(x, k)[:, c0:c1], c0, c1, FT,
                            made=None if j else (u_lo, FT * l))
                sum_squares(l, 3, SQF)


IN_NAMES = ["const", "vecs", "cs", "xin", "w2a2", "g2", "na_bias", "ada_w", "w_in", "w_branch", "w_gate", "w_o",
            "ffn_up", "ffn_down"]


def kernel(x, c, ctx, c_ctx, ada_w, ada_b, norm_mix_pre, norm_mix_post, norm_ffn_pre, norm_ffn_post,
           w_in, conv_a, na_bias, q_norm, k_norm, rw_mu, rw_w0, rw_w2, rw_a0, rw_a2, rw_kk, rw_ka, rw_rk,
           rw_g2, rw_ln_w, rw_ln_b, w_branch, w_gate, b_gate, w_o, ffn_up, ffn_conv, ffn_down):
    import concourse.bacc as bacc
    from concourse.bass_utils import run_bass_kernel_spmd

    def columns(v):
        v = np.asarray(v)
        return v.reshape(LAYERS, -1, P).transpose(0, 2, 1)

    twice = lambda v: np.concatenate([v, v], axis=-1)
    q_norm, k_norm = np.asarray(q_norm), np.asarray(k_norm)
    parts = dict(mix_pre=norm_mix_pre, mix_post=norm_mix_post, ffn_pre=norm_ffn_pre, ffn_post=norm_ffn_post,
                 ada_b=ada_b, conv_a=conv_a, q_norm=twice(q_norm), k_norm=twice(k_norm), mu=rw_mu, w0=rw_w0,
                 a0=rw_a0, kk=rw_kk, ka=rw_ka, rk=rw_rk, ln_w=rw_ln_w, ln_b=rw_ln_b, b_gate=b_gate,
                 ffn_conv=ffn_conv)
    vecs = np.concatenate([columns(parts[n]) for n, _ in VEC_COLS], axis=2)
    order = np.arange(ZT * P)
    q0 = Z_GQ * P
    order[q0:q0 + 256] = q0 + np.concatenate([np.arange(64) + 64 * h for h in (0, 2, 1, 3)])
    arrays = dict(
        const=constants(), vecs=vecs,
        cs=np.stack([np.asarray(c_ctx), np.asarray(c)[0]], axis=1),
        xin=np.concatenate([np.asarray(ctx)[0].T, np.asarray(x)[0].T], axis=1),
        w2a2=np.concatenate([np.asarray(rw_w2), np.asarray(rw_a2)], axis=2).transpose(0, 2, 1, 3),
        g2=rw_g2, na_bias=na_bias, ada_w=ada_w, w_in=np.asarray(w_in)[:, :, order],
        w_branch=np.asarray(w_branch).reshape(LAYERS, DM, DM), w_gate=w_gate, w_o=w_o, ffn_up=ffn_up,
        ffn_down=ffn_down)
    nc = bacc.Bacc("TRN2", target_bir_lowering=False, num_devices=1)
    ins, aps = {}, {}
    for n in IN_NAMES:
        v = np.ascontiguousarray(np.asarray(arrays[n]))
        ins["in_" + n] = v
        aps[n] = nc.dram_tensor("in_" + n, v.shape, mybir.dt.from_np(v.dtype), kind="ExternalInput").ap()
    out = nc.dram_tensor("out", (DM, LAT), F32, kind="ExternalOutput").ap()
    build(nc, aps, out)
    r = run_bass_kernel_spmd(nc, [ins], core_ids=[0])
    return np.ascontiguousarray(r.results[0]["out"].T)[None]
```

```python
from contextlib import ExitStack

import numpy as np
import concourse.bass as bass
from concourse import mybir

F32 = mybir.dt.float32
F32R = mybir.dt.float32r
ALU = mybir.AluOpType
ACT = mybir.ActivationFunctionType
AX = mybir.AxisListType.X

P = 128
LAYERS = 2
DM = 1024
KT = DM // P
CTX = 256
LAT = 256
T = CTX + LAT
GRID_W = 64
WIN_R, WIN_C = 8, 16
ZT = 24
DFF = 2816
FT = DFF // P
HD = 64
HEADS = 4
CH = 64
NCH = T // CH
NB = T // P
LEVELS = (2, 4, 8, 16, 32)
EPS = 1e-6
LN_EPS = 64e-5
DECAY = float(np.exp(-0.5))
MASKED = -1e30
KK_SCALE = 1024.0
BIAS_C = 2 * WIN_C - 1
BIAS_N = (2 * WIN_R - 1) * BIAS_C

Z_BG, Z_CG, Z_XIN = 0, 2, 4
Z_NQ, Z_NK, Z_NV = 6, 8, 10
Z_GQ, Z_GK, Z_GV = 12, 14, 15
Z_R, Z_K, Z_V, Z_LORA, Z_G = 16, 18, 20, 22, 23
Z_ORDER = [12, 13, 14, 15] + list(range(12)) + list(range(16, 24))
READOUT = {(0, 0): "var", (0, 1): "g2"}
SHIFTS = [6, 2, 3, 4, 5, 0, 1]
ACT_Z = [t for t in range(ZT) if t % 2 == 0 or t == Z_NQ + 1]
DVE_Z = [t for t in range(ZT) if t not in ACT_Z]
LATENT_ONLY = {0, 1, 2, 3, 4, 5, 6, 7, 12, 13, 16, 17, 23}

VEC_COLS = [("mix_pre", 8), ("mix_post", 8), ("ffn_pre", 8), ("ffn_post", 8), ("ada_b", 48), ("conv_a", 6),
            ("q_norm", 1), ("k_norm", 1), ("mu", 14), ("w0", 4), ("a0", 4), ("kk", 2), ("ka", 2), ("rk", 2),
            ("ln_w", 2), ("ln_b", 2), ("b_gate", 32), ("ffn_conv", 132)]
VEC = {}
_at = 0
for _n, _c in VEC_COLS:
    VEC[_n] = _at
    _at += _c
NVEC = _at

CONST_COLS = [("ident", P), ("ones", P), ("heads", P), ("swap", P), ("lm", 2 * P), ("m1t", P),
              ("m2", P), ("m4", P), ("m8", P), ("m16", P), ("m32", P), ("cos", LAT), ("sin", LAT),
              ("reset", T), ("window", GRID_W)]
CON = {}
_at = 0
for _n, _c in CONST_COLS:
    CON[_n] = _at
    _at += _c
NCON = _at

RING = 3
SLOT_N = 256
SPLIT = 3
NBANK = 8


def constants():
    p = np.arange(P)
    c = np.zeros((P, NCON), np.float32)

    def put(name, a):
        c[:, CON[name]:CON[name] + a.shape[1]] = a

    put("ident", np.eye(P))
    put("ones", np.ones((P, P)))
    put("heads", (p[:, None] // HD == p[None, :] // HD).astype(np.float32))
    sw = np.zeros((P, P))
    ev = np.arange(0, P, 2)
    sw[ev + 1, ev] = -1.0
    sw[ev, ev + 1] = 1.0
    put("swap", sw)
    s, t = p[:, None], p[None, :]
    same = s // CH == t // CH
    put("lm", np.concatenate([same & (s < t), same & (s <= t)], 1).astype(np.float32))
    put("m1t", (t % 2 == 1) & (s == t - 1))
    for z in LEVELS:
        put(f"m{z}", ((s // z) % 2 == 1) & (t // z == s // z - 1))
    tok = np.arange(LAT)
    n_freq = HD // 4
    inv = (np.float32(10000.0) ** (-np.arange(n_freq, dtype=np.float32) / np.float32(n_freq))).astype(np.float32)
    row, col = (tok // GRID_W).astype(np.float32), (tok % GRID_W).astype(np.float32)
    ang = np.concatenate([row[None, :] * inv[:, None], col[None, :] * inv[:, None]], 0)
    ang = ang[(p % HD) // 2]
    put("cos", np.cos(ang))
    put("sin", np.sin(ang))
    put("reset", np.broadcast_to((np.arange(T) % CH != 0).astype(np.float32), (P, T)))
    j, kc = GRID_W - 1 - p[:, None] % GRID_W, np.arange(GRID_W)[None, :]
    cs = np.clip(j - WIN_C // 2, 0, GRID_W - WIN_C)
    put("window", np.where((kc >= cs) & (kc < cs + WIN_C), 0.0, MASKED))
    return c


def attention_units(l):
    tiles = range(4) if l == 0 else range(2, 4)
    return [(g, h, q) for g in "BC" for h in range(HEADS) for q in tiles]


def modulation_jobs(blocks):
    jobs = []
    for n, b in enumerate(blocks):
        jobs.append(("mod",) + b)
        if n:
            jobs.append(("modt",) + blocks[n - 1])
    return jobs + [("modt",) + blocks[-1]]


MOD_FIRST = [(0, n) for n in range(8)]
MOD_BEFORE = [(0, n) for n in range(8, 24)] + [(1, n) for n in range(8)]
MOD_AFTER = [(1, n) for n in range(8, 24)]


def fill_plan():
    def rwkv(l, *counts):
        return [(kind, l, d) for d in range(2) for kind, n in zip(("lora", "norm", "bonus"), counts) for _ in range(n)]

    first = modulation_jobs(MOD_FIRST)
    plan = {("start", 0, 0): first[:5], ("start", 0, 1): first[5:]}
    before = [("att", 0, i) for i in range(0, 32, 2)] + rwkv(0, 2, 1, 1)
    after = [("end", 0, 0)] * 3 + [("att", 1, i) for i in range(0, 14, 2)] + rwkv(1, 1, 1, 1)
    for blocks, points in ((MOD_BEFORE, before), (MOD_AFTER, after)):
        jobs = modulation_jobs(blocks)
        assert len(points) == len(blocks)
        for n, p in enumerate(points):
            last = n == len(points) - 1
            plan.setdefault(p, []).extend(jobs[max(0, 2 * n - 1):None if last else 2 * n + 1])
    return plan


FILL = fill_plan()


def job_list():
    jobs = []
    for l in range(LAYERS):
        jobs += FILL.get(("start", l, 0), []) + [("ss", l, 0)] + FILL.get(("start", l, 1), [])
        for n, t in enumerate(Z_ORDER):
            jobs += [("z", l, t)]
            jobs += [(k, l, i) for k, at in (("qss", 5), ("qsw", 14), ("vt", 17)) if n == at for i in range(3)]
        n = len(attention_units(l))
        for i in range(n + 3):
            if i < n:
                jobs.append(("S", l, i))
            jobs += FILL.get(("att", l, i), [])
            if 2 <= i <= n + 1:
                jobs.append(("T", l, i - 2))
            if i >= 3:
                jobs.append(("PV", l, i - 3))
        for d in range(2):
            jobs += [(k, l, d, p) for p in range(2) for k in ("wl", "al")]
            jobs += [("kss", l, d, p) for p in range(2)]
            jobs += FILL.get(("lora", l, d), [])
            jobs += [("tok", l, d, "v", p) for p in range(2)]
            jobs += FILL.get(("norm", l, d), [])
            jobs += [("bon", l, d, p) for p in range(2)]
            jobs += [("tok", l, d, "k", p) for p in range(2)]
            jobs += FILL.get(("bonus", l, d), [])
            for h in range(HEADS):
                jobs += [("LM1", l, d, h, b) for b in range(2)]
                if h % 2:
                    jobs += [("tok", l, d, m, h // 2) for m in "ab"]
            jobs += [("tn", l, d, h) for h in range(HEADS)]
            for n, s in enumerate(LEVELS):
                if n == 0:
                    jobs += [("LM2", l, d, 0, b) for b in range(2)]
                jobs += [("sx", l, d, s, h) for h in range(HEADS)]
                if n:
                    jobs += [("tt", l, d, s, h) for h in range(HEADS)]
                if 0 < n < HEADS:
                    jobs += [("LM2", l, d, n, b) for b in range(2)]
                if n == HEADS:
                    jobs += [("xv", l, d, p) for p in range(2)]
                jobs += [("sy" if s != LEVELS[-1] else "syt", l, d, s, h) for h in range(HEADS)]
            jobs += [("at", l, d, p) for p in range(2)]
            jobs += [("u0", l, d, p) for p in range(2)]
            for c in range(NCH):
                jobs += [("cu", l, d, c)]
                if c < NCH - 1:
                    jobs += [("ch", l, d, c)]
                if l == 0 or c >= NCH // 2:
                    jobs += [("cy", l, d, c)]
        jobs += [("mean", l, p) for p in range(2)]
        for J in range(4):
            for i in range(4):
                for j in (2 * J, 2 * J + 1):
                    jobs += [("gate", l, j, i), ("br", l, j, i)]
                jobs += [(READOUT[J, i], l, p) for p in range(2) if (J, i) in READOUT]
        jobs += [("wo", l, j) for j in range(8)]
        jobs += [("ss", l, 1)]
        jobs += [("ss", l, 2)]
        for j in range(FT):
            jobs += [("up", l, j, 0), ("up", l, j, 1)]
        jobs += [("down", l, j) for j in range(8)]
        jobs += [("ss", l, 3)] + FILL.get(("end", l, 0), [])
    return {name: g for g, name in enumerate(jobs)}


JOB = job_list()


def blocks_of(job):
    k, l = job[:2]
    if k == "mod":
        return [(("ada", l, job[2]), None)]
    if k == "z":
        return [(("w_in", l, job[2] // 2), job[2] % 2)]
    if k == "gate":
        return [(("gate", l, job[2] // 2, job[3]), job[2] % 2)]
    if k == "wo":
        return [(("w_o", l, job[2] // 2), job[2] % 2)]
    if k == "up":
        return [(("up", l, job[2] // 2, job[3]), job[2] % 2)]
    if k == "down":
        return [(("down", l, job[2], q), 0) for q in range(3)]
    return []


def streams_of_weights():
    slots, last_job, halves, half_job = {}, {}, {}, []
    for job in JOB:
        for raw, half in blocks_of(job):
            slots.setdefault(raw, len(slots))
            last_job[raw] = job
            if half is not None:
                halves[(raw, half)] = len(halves)
                half_job.append(job)
    return slots, last_job, halves, half_job


SLOT, LAST_JOB, HALF, HALF_JOB = streams_of_weights()
HALVES = list(HALF)


def half_no(job):
    return HALF[blocks_of(job)[0]]


def build(nc, a, out):
    ctx = ExitStack()
    with ctx:
        def sb(name, shape):
            return ctx.enter_context(nc.sbuf_tensor(name, shape, F32))

        def sem(name):
            return ctx.enter_context(nc.semaphore(name))

        con = sb("con", [P, NCON])
        vec = sb("vec", [P, LAYERS * NVEC])
        bm = sb("bm", [P, HEADS, 6, GRID_W])
        ring = sb("ring", [P, RING, KT, SLOT_N])
        cvec = sb("cvec", [P, KT, 2])
        mod = sb("mod", [P, LAYERS, 48, 2])
        amod = sb("amod", [P, 4, 8, 2])
        omu = sb("omu", [P, 14])
        oka = sb("oka", [P, 2])
        eps = sb("eps", [P, 2])
        rs = sb("rs", [P, T])
        rt = sb("rt", [P, T])
        wendt = sb("wendt", [P, 2 * NCH])
        stat = sb("stat", [P, 3, 4])
        mrow = sb("mrow", [2, SLOT_N])
        ps = ctx.enter_context(nc.psum_tensor("ps", [P, NBANK, 512], F32))
        xsave = nc.dram_tensor("xsave", [DM, T], F32, kind="Internal").ap()
        hsave = nc.dram_tensor("hsave", [2, DM, T], F32R, kind="Internal").ap()

        base = -(-nc.sbuf_base // 32) * 32
        ctx.enter_context(nc.sbuf_tensor("arena", [P, 156 * 256], F32))

        def at(name, kb, shape, dtype=F32):
            return nc.alloc_sbuf_tensor_at(name, [P] + shape, dtype, offset=base + 1024 * kb)

        X = at("X", 0, [KT, T])
        YB = at("YB", 16, [KT, T])
        Z = at("Z", 32, [ZT, T])
        HR = at("HR", 80, [2, KT, T], F32R)
        LMr = at("LMr", 80, [8192])
        pr = at("pr", 80, [3, T])
        prT = at("prT", 86, [3, T])
        E = at("E", 112, [5120])
        WB = at("WB", 112, [2, KT, SLOT_N])
        ACC = at("ACC", 32, [KT, T])
        RO = at("RO", 36, [5, T])
        HG = at("HG", 48, [2, KT, T], F32R)
        AR = at("AR", 80, [2, KT, T], F32R)
        OB = at("OB", 48, [KT, T])
        SQB = at("SQB", 64, [KT, T])
        H2 = at("H2", 100, [2, KT, T], F32R)
        UA = at("UA", 16, [2, 20, T], F32R)
        UB = at("UB", 0, [2, FT - 20, T], F32R)
        CU = at("CU", 96, [2, T])
        F = at("F", 100, [KT, T])
        SQF = at("SQF", 116, [KT, T])

        whi = at("whi", 132, [SPLIT, KT, P], F32R)
        wlo = at("wlo", 144, [SPLIT, KT, P], F32R)
        VM = at("VM", 132, [2, NB, 256])
        w2a2 = at("w2a2", 140, [2, 2, 256])

        def hidden(part, j):
            return UA[:, part, j, :] if j < 20 else UB[:, part, j - 20, :]

        def K(name, n=P):
            return con[:, CON[name]:CON[name] + n]

        def vc(l, name, i=0, n=1):
            o = l * NVEC + VEC[name] + i
            return vec[:, o:o + n]

        Ef, Lf = E, LMr
        Zf = Z[:, :, :].rearrange("p a b -> p (a b)")

        def view(f, o, *dims):
            n = int(np.prod(dims))
            v = f[:, o:o + n]
            if len(dims) == 2:
                return v.rearrange("p (a b) -> p a b", a=dims[0])
            if len(dims) == 3:
                return v.rearrange("p (a b c) -> p a b c", a=dims[0], b=dims[1])
            if len(dims) == 4:
                return v.rearrange("p (a b c d) -> p a b c d", a=dims[0], b=dims[1], c=dims[2])
            return v

        nu = rt[:, :].rearrange("p (x h n) -> p x h n", x=2, h=HEADS)
        state = rs[:, :].rearrange("p (b a n) -> p b a n", b=2, a=2)
        wend = wendt[:, :].rearrange("p (a c) -> p a c", a=2)
        vB = view(Ef, 0, 4, 256)
        vC = view(Ef, 1024, 4, 128)
        sbuf2 = view(Ef, 1536, 3, T)
        qtmp = YB[:, 6, :]
        qsq = [YB[:, 6, :], YB[:, 7, :], YB[:, 5, :]]
        qroot = [rs, rt, YB[:, 4, :]]
        KZ = Z
        ar = view(Ef, 0, 2, NB, 2, P)
        betaz = view(Ef, 2048, HEADS, T)
        kapz01, kapz23 = view(Zf, 7168, 2, T), view(Ef, 4096, 2, T)

        def kapz(h):
            return kapz01[:, h, :] if h < 2 else kapz23[:, h - 2, :]

        bon = bm[:, :, :, :].rearrange("p h r c -> p (h r c)")[:, 0:2 * T].rearrange("p (a t) -> p a t", a=2)
        g2 = bm[:, :, :, :].rearrange("p h r c -> p (h r c)")[:, 2 * T:2 * T + 256]
        LM1 = view(Lf, 0, HEADS, NB, 2 * P)
        LM2 = view(Lf, 4096, HEADS, NB, 2 * P)
        TT = view(Zf, 0, HEADS, NB, P)
        TN = view(Zf, 2048, HEADS, NB, P)
        XS = view(Zf, 4096, HEADS, NB, P)
        vT = view(Zf, 6144, 2, T)
        AT = view(Zf, 2048, 2, T)
        zr, zk, sg, aa = (view(Lf, 1024 * i, 2, T) for i in range(4))
        G, kk, t1, t2 = (view(Lf, 4096 + 1024 * i, 2, T) for i in range(4))
        wdec, winv = (view(Zf, 2048 + 1024 * i, 2, T) for i in range(2))
        wprev = view(Zf, 4096, 2, T)
        kscale = view(Zf, 0, 2, T)
        awinv = view(Zf, 1024, 2, T)
        lora = view(Zf, 5120, T)
        Xf = X[:, :, :].rearrange("p k t -> p (k t)")
        tokm = {m: view(Xf, 1024 * i, NB, 256) for i, m in enumerate("abkv")}
        XV = view(Ef, 2048, HEADS, NB, HD)
        U0 = view(Ef, 3072, HEADS, NB, HD)
        siglg = RO[:, 4, :]

        c_in = sem("c_in")
        const_in = sem("const_in")
        vec_in = sem("vec_in")
        root_ready = sem("root_ready")
        gains_ready = sem("gains_ready")
        ln_root = sem("ln_root")
        w_used = sem("w_used")
        lora_in = sem("lora_in")
        small_in = [sem("small_in0"), sem("small_in1")]
        x_in = sem("x_in")
        g2_in = sem("g2_in")
        x_saved = sem("x_saved")
        wb_in = sem("wb_in")
        x_back = sem("x_back")
        w_in_slot = [sem(f"w_slot{i}") for i in range(RING)]
        mm_done = sem("mm_done")
        bank_free = [sem(f"bank_free{i}") for i in range(NBANK)]
        silu_c = sem("silu_c")
        hi_done = sem("hi_done")
        lo_done = sem("lo_done")
        h_hi = sem("h_hi")
        h_saved = [sem("h_saved0"), sem("h_saved1")]
        h_back = [sem("h_back0"), sem("h_back1")]
        kz_ready = sem("kz_ready")
        p_sum = sem("p_sum")
        kap_done = sem("kap_done")
        kapz_done = sem("kapz_done")
        beta_done = sem("beta_done")
        betaz_done = sem("betaz_done")
        bonus_done = sem("bonus_done")
        tt_masked = sem("tt_masked")
        acc_hi = sem("acc_hi")
        acc_lo = sem("acc_lo")
        u_hi = sem("u_hi")
        u_lo = sem("u_lo")
        setup = sem("setup")
        sq_ready = sem("sq_ready")
        h_full = sem("h_full")
        scaled = sem("scaled")
        h_half = sem("h_half")
        h_ready = sem("h_ready")
        x_ready = sem("x_ready")
        ya_ready = sem("ya_ready")
        qsq_ready = sem("qsq_ready")
        qn_ready = sem("qn_ready")
        qk_ready = sem("qk_ready")
        q_scaled = sem("q_scaled")
        nmax_ready = sem("nmax_ready")
        p_ready = sem("p_ready")
        shift_half = sem("shift_half")
        shift_done = sem("shift_done")
        tanh_done = sem("tanh_done")
        kraw_done = sem("kraw_done")
        ksq_done = sem("ksq_done")
        scan_done = sem("scan_done")
        prev_done = sem("prev_done")
        kscale_done = sem("kscale_done")
        awinv_done = sem("awinv_done")
        vm_done = sem("vm_done")
        rho_done = sem("rho_done")
        decay_done = sem("decay_done")
        bonus_in = sem("bonus_in")
        streams_done = sem("streams_done")
        state_half = sem("state_half")
        t_done = sem("t_done")
        kroot_done = sem("kroot_done")
        ln_sq = sem("ln_sq")
        lg_done = sem("lg_done")
        gated = sem("gated")
        conv_half = sem("conv_half")
        silu_done = sem("silu_done")
        u_ready = sem("u_ready")
        act_chain = sem("act_chain")
        dve_chain = sem("dve_chain")
        pool_chain = sem("pool_chain")
        stored = sem("stored")

        def bank(name):
            return ps[:, JOB[name] % NBANK, :]

        def filled(eng, name):
            eng.wait_ge(mm_done, JOB[name] + 1)
            return bank(name)

        def frees(name):
            return bank_free[JOB[name] % NBANK]

        def emptied(eng, name):
            eng.wait_ge(frees(name), JOB[name] // NBANK + 1)

        def cols(l, t=None):
            if l == 0 or (t is not None and t not in LATENT_ONLY):
                return 0, T
            return CTX, T

        def streams(l):
            return (0, 1) if l == 0 else (1,)

        def norm_no(l, k):
            return 4 * l + k

        def added(l, j, i):
            return 24 * l + 6 * (j // 2) + 2 * (i - 1) + j % 2 + 1

        def width(l, b):
            return 2 * P if l == 0 or b >= NB // 2 else P

        def grid_rows(v):
            return v.rearrange("p (r j) -> p r j", j=GRID_W)

        UNITS = [attention_units(l) for l in range(LAYERS)]
        UBASE = [0, len(UNITS[0])]

        block = ctx.enter_context(nc.Block())

        @block.sync
        def _(sp):
            sp.dma_start(cvec[:, :, :], a["cs"].rearrange("(k p) s -> p k s", p=P)).then_inc(c_in, 16)
            names = list(SLOT)
            for n, name in enumerate(names):
                k, l = name[:2]
                if n == 1:
                    sp.dma_start(con[:, :], a["const"]).then_inc(const_in, 16)
                if n == 3:
                    sp.dma_start(X[:, :, :], a["xin"].rearrange("(k p) t -> p k t", p=P)).then_inc(x_in, 16)
                    sp.dma_start(vec[:, :].rearrange("p (l n) -> p l n", l=LAYERS),
                                 a["vecs"].rearrange("l p n -> p l n")).then_inc(vec_in, 16)
                if n >= RING:
                    old = names[n - RING]
                    if (old, 0) in HALF:
                        sp.wait_ge(lo_done, max(HALF[(old, x)] for x in range(2) if (old, x) in HALF) + 1)
                    else:
                        sp.wait_ge(mm_done, JOB[LAST_JOB[old]] + 1)
                dst = ring[:, n % RING, :, :]
                if k == "ada":
                    src = a["ada_w"][l, :, name[2] * SLOT_N:(name[2] + 1) * SLOT_N]
                elif k == "w_in":
                    src = a["w_in"][l, :, name[2] * SLOT_N:(name[2] + 1) * SLOT_N]
                elif k == "gate":
                    o = name[3] * DM + name[2] * SLOT_N
                    src = a["w_gate"][l, :, o:o + SLOT_N]
                elif k == "w_o":
                    src = a["w_o"][l, :, name[2] * SLOT_N:(name[2] + 1) * SLOT_N]
                elif k == "up":
                    o = name[3] * DFF + name[2] * SLOT_N
                    src = a["ffn_up"][l, :, o:o + SLOT_N]
                else:
                    k0, k1 = 8 * name[3], min(8 * name[3] + 8, FT)
                    src = a["ffn_down"][l, k0 * P:k1 * P, name[2] * P:(name[2] + 1) * P]
                    dst = ring[:, n % RING, 0:k1 - k0, 0:P]
                sp.dma_start(dst, src.rearrange("(k p) n -> p k n", p=P)).then_inc(w_in_slot[n % RING], 16)

        @block.gpsimd
        def _(pool):
            links = [0]

            def link(ins):
                links[0] += 1
                ins.then_inc(pool_chain, 1)
                pool.wait_ge(pool_chain, links[0])

            def load_small(l):
                nb = a["na_bias"]
                for h in range(HEADS):
                    for half in range(2):
                        src = bass.AP(nb.tensor,
                                      (l * HEADS + h) * BIAS_N + (5 - half) * BIAS_C + WIN_C - 1 - (GRID_W - 1),
                                      [[1, GRID_W], [BIAS_C, 6], [1, GRID_W]])
                        pool.dma_start(bm[half * HD:(half + 1) * HD, h, :, :], src).then_inc(small_in[l], 16)

            load_small(0)
            for l in range(LAYERS):
                c0, c1 = cols(l)
                ns = len(streams(l))
                if l == 1:
                    emptied(pool, ("g2", 0, 1))
                    load_small(1)
                pool.wait_ge(h_ready, 16 * l + 8)
                for part in range(2):
                    pool.dma_start(hsave[part, :, c0:T].rearrange("(k p) t -> p k t", p=P), HR[:, part, :, c0:T])\
                        .then_inc(h_saved[l], 16)
                if l:
                    pool.dma_start(xsave[:, :].rearrange("(k p) t -> p k t", p=P), X[:, :, :]).then_inc(x_saved, 16)
                for p in range(2):
                    for t in (Z_BG + p, Z_CG + p, Z_XIN + p):
                        emptied(pool, ("z", l, t))
                    xc = Z[:, Z_XIN + p, c0:c1]
                    cg = Z[:, Z_CG + p, c0:c1]
                    y = YB[:, p, c0:c1]
                    link(pool.tensor_tensor(xc, xc, cg, ALU.mult))
                    link(pool.tensor_scalar(y, xc, vc(l, "conv_a", 2 + p), None, ALU.mult))
                    xs = xc.rearrange("p (s t) -> p s t", s=ns)
                    ys = y.rearrange("p (s t) -> p s t", s=ns)
                    tm = cg.rearrange("p (s t) -> p s t", s=ns)
                    link(pool.tensor_scalar(tm[:, :, 0:255], xs[:, :, 0:255], vc(l, "conv_a", p), None, ALU.mult))
                    link(pool.tensor_tensor(ys[:, :, 1:256], ys[:, :, 1:256], tm[:, :, 0:255], ALU.add))
                    link(pool.tensor_scalar(tm[:, :, 0:255], xs[:, :, 1:256], vc(l, "conv_a", 4 + p), None, ALU.mult))
                    link(pool.tensor_tensor(ys[:, :, 0:255], ys[:, :, 0:255], tm[:, :, 0:255], ALU.add))
                    pool.tensor_tensor(y, y, Z[:, Z_BG + p, c0:c1], ALU.mult).then_inc(ya_ready, 1)
                pool.wait_ge(mm_done, JOB[("z", l, ZT - 1)] + 1)
                pool.dma_start(w2a2[:, :, :, :], a["w2a2"][l]).then_inc(lora_in, 16)
                units = UNITS[l]
                for u in range(len(units)):
                    nk = T if units[u][2] >= 2 else CTX
                    pool.wait_ge(p_sum, UBASE[l] + u + 1)
                    pool.tensor_scalar(pr[:, u % 3, 0:nk], pr[:, u % 3, 0:nk], stat[:, 2, u % 4:u % 4 + 1],
                                       None, ALU.mult).then_inc(p_ready, 1)
                pool.wait_ge(mm_done, JOB[("PV", l, len(units) - 1)] + 1)
                pool.dma_start(g2[:, :], a["g2"][l]).then_inc(g2_in, 16)
                idb = K("ident").unsqueeze(1).to_broadcast([P, NB, P])
                for d in range(2):
                    it = 2 * l + d
                    blk = lambda v: v.rearrange("p (b t) -> p b t", b=NB)[:, c0 // P:]
                    for p in range(2):
                        pool.wait_ge(scan_done, 2 * it + p + 1)
                        pool.tensor_tensor(t2[:, p, :], G[:, p, :], sg[:, p, :], ALU.subtract).then_inc(prev_done, 1)
                    for p in range(2):
                        pool.wait_ge(decay_done, 2 * it + p + 1)
                        pool.tensor_tensor(awinv[:, p, :], aa[:, p, :], winv[:, p, :], ALU.mult).then_inc(awinv_done, 1)
                    pool.wait_ge(shift_done, 7 * it + 7)
                    for p in range(2):
                        pool.tensor_tensor(ar[:, p, c0 // P:, 1, :], blk(zr[:, p, :]), blk(wdec[:, p, :]), ALU.mult)\
                            .then_inc(rho_done, 1)
                    for p in range(2):
                        emptied(pool, ("bon", l, d, p))
                        v = vT[:, p, c0:T]
                        if d == 0:
                            bo = bon[:, p, c0:T]
                            pool.tensor_tensor(bo, bo, v, ALU.mult).then_inc(bonus_done, 1)
                        else:
                            link(pool.tensor_tensor(G[:, p, c0:T], G[:, p, c0:T], v, ALU.mult))
                            rev = G[:, p, c0:T].rearrange("p (s t) -> p s t", s=ns)[:, :, ::-1]
                            bo = bon[:, p, c0:T].rearrange("p (s t) -> p s t", s=ns)
                            pool.tensor_tensor(bo, bo, rev, ALU.add).then_inc(bonus_done, 1)
                    for h in range(HEADS):
                        pool.wait_ge(tt_masked, 4 * it + h + 1)
                        pool.tensor_tensor(TT[:, h, :, :], idb, TT[:, h, :, :], ALU.subtract).then_inc(t_done, 1)
                pool.wait_ge(mm_done, JOB[("syt", l, 1, LEVELS[-1], HEADS - 1)] + 1)
                pool.wait_ge(lg_done, l + 1)
                pool.wait_ge(h_saved[l], 32)
                for part in range(2):
                    pool.dma_start(HG[:, part, :, c0:T], hsave[part, :, c0:T].rearrange("(k p) t -> p k t", p=P))\
                        .then_inc(h_back[l], 16)
                pool.wait_ge(mm_done, JOB[("cy", l, 1, NCH - 1)] + 1)
                for J in range(4):
                    if J >= 2:
                        pool.wait_ge(mm_done, JOB[("br", l, 2 * J - 3, 3)] + 1)
                    elif J == 0:
                        emptied(pool, ("cu", l, 1, NCH - 1))
                    pool.dma_start(WB[:, J % 2, :, :],
                                   a["w_branch"][l, :, J * SLOT_N:(J + 1) * SLOT_N].rearrange("(k p) n -> p k n", p=P))\
                        .then_inc(wb_in, 16)
                    if J == 1:
                        if l:
                            pool.wait_ge(x_saved, 32)
                        pool.dma_start(X[:, :, c0:c1],
                                       (xsave if l else a["xin"])[:, c0:c1].rearrange("(k p) t -> p k t", p=P))\
                            .then_inc(x_back, 16)
                    pool.wait_ge(wb_in, 16 * (4 * l + J + 1))
                pool.wait_ge(x_ready, 16 * l + 8)
                pool.dma_start(xsave[:, c0:c1].rearrange("(k p) t -> p k t", p=P), X[:, :, c0:c1]).then_inc(x_saved, 16)
                for j in range(FT):
                    pool.wait_ge(silu_done, l * FT + j + 1)
                    u = CU[:, j % 2, c0:c1]
                    pool.tensor_tensor(u, u, (rs, rt)[j % 2][:, c0:c1], ALU.mult).then_inc(u_ready, 1)
                pool.wait_ge(mm_done, JOB[("down", l, KT - 1)] + 1)
                pool.wait_ge(x_saved, 16 * (2 * l + 1))
                pool.dma_start(X[:, :, c0:c1], xsave[:, c0:c1].rearrange("(k p) t -> p k t", p=P)).then_inc(x_back, 16)
            for i in range(KT):
                pool.wait_ge(x_ready, 24 + i + 1)
                pool.dma_start(out[i * P:(i + 1) * P, :], X[:, i, CTX:T]).then_inc(stored, 16)
            pool.wait_ge(stored, 16 * KT)

        @block.scalar
        def _(act):
            links = [0]

            def link(ins):
                links[0] += 1
                ins.then_inc(act_chain, 1)
                act.wait_ge(act_chain, links[0])

            def square(dst, src):
                act.activation(dst, src, ACT.Square).then_inc(sq_ready, 1)

            def norm_root(l, k):
                c0, c1 = cols(l) if k else (0, T)
                s = filled(act, ("ss", l, k))
                act.activation(rt[:, c0:c1], s[:, c0:c1], ACT.Ln, bias=eps[:, 0:1], scale=1.0 / DM)\
                   .then_inc(frees(("ss", l, k)), 1)
                emptied(act, ("ss", l, k))
                act.activation(rs[:, c0:c1], rt[:, c0:c1], ACT.Exp, scale=-0.5).then_inc(root_ready, 1)

            halves = [0]

            def split_until(n):
                while halves[0] < n:
                    m = halves[0]
                    raw, half = HALVES[m]
                    kn = FT % KT if raw[0] == "down" and raw[3] == 2 else KT
                    act.wait_ge(w_in_slot[SLOT[raw] % RING], 16 * (SLOT[raw] // RING + 1))
                    if m >= SPLIT:
                        old = HALVES[m - SPLIT][0]
                        if old[0] == "down" and old[3] < 2:
                            act.wait_ge(w_used, 2 * (KT * old[1] + old[2]) + old[3] + 1)
                        else:
                            act.wait_ge(mm_done, JOB[HALF_JOB[m - SPLIT]] + 1)
                    act.activation(whi[:, m % SPLIT, 0:kn, :],
                                   ring[:, SLOT[raw] % RING, 0:kn, P * half:P * half + P], ACT.Copy).then_inc(hi_done, 1)
                    halves[0] += 1

            def fill(point):
                for job in FILL.get(point, []):
                    if job[0] == "mod":
                        s = filled(act, job)
                        if rows[0]:
                            act.wait_ge(mm_done, JOB[("modt",) + rows[0]] + 1)
                        rows[0] = job[1:]
                        act.activation(mrow[:, :], s[0:2, 0:SLOT_N], ACT.Copy).then_inc(frees(job), 1)

            rows = [None]

            def norm_finish(l, k, src, dst):
                no = 2 * l + k // 2
                act.wait_ge(gains_ready, 2 * l + 1 + k // 2)
                shift = 0 if k == 0 else 24
                ss = streams(l) if k else (0, 1)
                c0, c1 = cols(l) if k else (0, T)
                for i in range(KT + 1):
                    if i < KT:
                        act.wait_ge(h_half, 8 * no + i + 1)
                        for s in ss:
                            v = src[:, i, 256 * s:256 * s + 256]
                            ins = act.activation(v, v, ACT.Identity, bias=mod[:, l, shift + i, s:s + 1],
                                                 scale=amod[:, k, i, s:s + 1])
                        ins.then_inc(h_full, 1)
                    if i:
                        act.wait_ge(h_full, 8 * no + i)
                        act.activation(dst[:, 0, i - 1, c0:c1], src[:, i - 1, c0:c1], ACT.Copy).then_inc(h_hi, 1)

            act.wait_ge(c_in, 16)
            act.activation(cvec[:, :, :], cvec[:, :, :], ACT.Silu).then_inc(silu_c, 1)
            fill(("start", 0, 0))
            act.wait_ge(x_in, 16)
            act.wait_ge(setup, 1)
            for i in range(KT):
                square(YB[:, i, :], X[:, i, :])
            norm_root(0, 0)
            fill(("start", 0, 1))
            act.wait_ge(vec_in, 16)
            for l in range(LAYERS):
                c0, c1 = cols(l)
                W = c1 - c0
                ns = len(streams(l))
                for i in range(KT if l else 0):
                    act.wait_ge(x_ready, 8 + i + 1)
                    square(YB[:, i, :], X[:, i, :])
                split_until(half_no(("z", l, Z_ORDER[0])) + SPLIT)
                if l:
                    norm_root(l, 0)
                norm_finish(l, 0, Z, HR)
                for n, t in enumerate(Z_ORDER):
                    act.wait_ge(mm_done, JOB[("z", l, t)] + 1)
                    split_until(min(half_no(("z", l, t)) + 1 + SPLIT, half_no(("z", l, ZT - 1)) + 1))
                    z0, z1 = cols(l, t)
                    s = bank(("z", l, t))
                    if t not in ACT_Z:
                        pass
                    elif t in (Z_NQ, Z_NQ + 1):
                        if l == 0:
                            act.activation(Z[:, t, 0:CTX], s[:, 0:CTX], ACT.Copy)
                        act.activation(grid_rows(Z[:, t, CTX:T]), grid_rows(s[:, CTX:T])[:, :, ::-1], ACT.Copy)\
                           .then_inc(frees(("z", l, t)), 1)
                    else:
                        act.activation(Z[:, t, z0:z1], s[:, z0:z1], ACT.Copy).then_inc(frees(("z", l, t)), 1)
                    if n == 4:
                        for i in range(3):
                            q0, q1 = cols(l, Z_GQ + i)
                            emptied(act, ("z", l, Z_GQ + i))
                            act.activation(qsq[i][:, q0:q1], Z[:, Z_GQ + i, q0:q1], ACT.Square).then_inc(qsq_ready, 1)
                    if n == 6:
                        for i in range(3):
                            q0, q1 = cols(l, Z_GQ + i)
                            s = filled(act, ("qss", l, i))
                            act.activation(qroot[i][:, q0:q1], s[:, q0:q1], ACT.Sqrt, bias=eps[:, 0:1], scale=1.0 / HD)\
                               .then_inc(frees(("qss", l, i)), 1)
                units = UNITS[l]
                act.wait_ge(h_saved[l], 32)
                for i in range(len(units) + 2):
                    if i < len(units):
                        g, h, q = units[i]
                        nk = T if q >= 2 else CTX
                        s = bank(("S", l, i))
                        src = sbuf2[:, i % 3, 0:nk] if g == "B" and q >= 2 else s[:, 0:nk]
                        act.wait_ge(nmax_ready, UBASE[l] + i + 1)
                        act.activation(pr[:, i % 3, 0:nk], src, ACT.Exp, bias=stat[:, 0, i % 4:i % 4 + 1],
                                       accum_out=stat[:, 1, i % 4:i % 4 + 1]).then_inc(frees(("S", l, i)), 1)
                    fill(("att", l, i))
                    if i >= 2:
                        u = i - 2
                        nk = T if units[u][2] >= 2 else CTX
                        s = filled(act, ("T", l, u))
                        if u >= 3:
                            act.wait_ge(mm_done, JOB[("PV", l, u - 3)] + 1)
                        act.activation(prT[:, u % 3, 0:nk], s[:, 0:nk], ACT.Copy).then_inc(frees(("T", l, u)), 1)
                act.wait_ge(ya_ready, 2 * l + 2)
                act.wait_ge(mm_done, JOB[("PV", l, len(units) - 1)] + 1)
                for d in range(2):
                    it = 2 * l + d
                    if d == 1:
                        act.wait_ge(mm_done, JOB[("cy", l, 0, NCH - 1)] + 1)
                    step = 1 if d == 0 else -1
                    dsts = [zr[:, 0, :], zr[:, 1, :], zk[:, 0, :], zk[:, 1, :], vT[:, 0, :], vT[:, 1, :], lora]
                    def shift_copy(n):
                        i = SHIFTS[n]
                        emptied(act, ("z", l, Z_R + i))
                        s0 = c0 // 256 if i < 2 else 0
                        src = Z[:, Z_R + i, :].rearrange("p (s t) -> p s t", s=2)[:, s0:, ::step]
                        act.activation(dsts[i].rearrange("p (s t) -> p s t", s=2)[:, s0:], src, ACT.Copy,
                                       scale=omu[:, 7 * d + i:7 * d + i + 1]).then_inc(shift_half, 1)

                    for n in range(3):
                        shift_copy(n)
                    act.wait_ge(shift_done, 7 * it + 1)
                    act.activation(lora[0:HD, :], lora[0:HD, :], ACT.Tanh).then_inc(tanh_done, 1)
                    for p in range(2):
                        act.wait_ge(kraw_done, 2 * it + p + 1)
                        act.activation(t1[:, p, :], kk[:, p, :], ACT.Square).then_inc(ksq_done, 1)
                    for n in range(3, 5):
                        shift_copy(n)
                    for p in range(2):
                        s = filled(act, ("wl", l, d, p))
                        act.activation(sg[:, p, :], s, ACT.Sigmoid, bias=vc(l, "w0", 2 * d + p))\
                           .then_inc(frees(("wl", l, d, p)), 1)
                        s = filled(act, ("al", l, d, p))
                        act.activation(aa[:, p, :], s, ACT.Sigmoid, bias=vc(l, "a0", 2 * d + p))\
                           .then_inc(frees(("al", l, d, p)), 1)
                        emptied(act, ("al", l, d, p))
                        act.activation(kscale[:, p, :], aa[:, p, :], ACT.Identity, bias=oka[:, p:p + 1],
                                       scale=vc(l, "ka", p)).then_inc(kscale_done, 1)
                    for n in range(5, 7):
                        shift_copy(n)
                    for p in range(2):
                        act.wait_ge(scan_done, 2 * it + p + 1)
                        act.activation(wdec[:, p, :], G[:, p, :], ACT.Exp, scale=-DECAY)
                        act.activation(winv[:, p, :], G[:, p, :], ACT.Exp, scale=DECAY)
                        act.wait_ge(prev_done, 2 * it + p + 1)
                        act.activation(wprev[:, p, :], t2[:, p, :], ACT.Exp, scale=-DECAY).then_inc(decay_done, 1)
                    fill(("lora", l, d))
                    for p in range(2):
                        emptied(act, ("kss", l, d, p))
                        link(act.activation((rs, rt)[p][:, :], (rs, rt)[p][:, :], ACT.Ln))
                    for p in range(2):
                        act.activation(t1[:, p, :], (rs, rt)[p][:, :], ACT.Exp, scale=-0.5).then_inc(kroot_done, 1)

                    def token_major(m, p):
                        s = filled(act, ("tok", l, d, m, p))
                        act.activation(tokm[m][:, :, 128 * p:128 * p + 128], s.rearrange("p (b n) -> p b n", b=NB),
                                       ACT.Copy).then_inc(frees(("tok", l, d, m, p)), 1)

                    if l:
                        act.wait_ge(x_saved, 32)
                    for p in range(2):
                        token_major("v", p)
                    fill(("norm", l, d))
                    for p in range(2):
                        act.wait_ge(kap_done, 2 * it + p + 1)
                        for x in range(2):
                            act.activation(kapz(2 * p + x), zk[:, p, :], ACT.Copy,
                                           scale=K("heads")[:, HD * x:HD * x + 1]).then_inc(kapz_done, 1)
                    for p in range(2):
                        s = filled(act, ("bon", l, d, p))
                        act.activation((G if d else bon)[:, p, c0:T], s[:, c0:T], ACT.Copy).then_inc(frees(("bon", l, d, p)), 1)
                    for p in range(2):
                        token_major("k", p)
                    fill(("bonus", l, d))
                    for p in range(2):
                        act.wait_ge(beta_done, 2 * it + p + 1)
                        for x in range(2):
                            act.activation(betaz[:, 2 * p + x, :], kk[:, p, :], ACT.Copy,
                                           scale=K("heads")[:, HD * x:HD * x + 1]).then_inc(betaz_done, 1)
                    for p in range(2):
                        for m in "ab":
                            token_major(m, p)
                    for h in range(HEADS):
                        s = filled(act, ("tn", l, d, h)).rearrange("p (b n) -> p b n", b=NB)
                        act.activation(TN[:, h, :, :], s, ACT.Copy).then_inc(frees(("tn", l, d, h)), 1)
                    for p in range(2):
                        emptied(act, ("tok", l, d, "v", p))
                    for x in range(2):
                        act.activation(VM[:, x, :, :], tokm["v"][:, :, :], ACT.Copy,
                                       scale=K("heads")[:, CH * x:CH * x + 1]).then_inc(vm_done, 1)
                    for z in LEVELS[1:]:
                        for h in range(HEADS):
                            s = filled(act, ("tt", l, d, z, h)).rearrange("p (b n) -> p b n", b=NB)
                            act.activation(TT[:, h, :, :], s, ACT.Copy).then_inc(frees(("tt", l, d, z, h)), 1)
                    for p in range(2):
                        s = filled(act, ("xv", l, d, p))
                        act.activation(XV[:, 2 * p:2 * p + 2, :, :].rearrange("p h b n -> p (h b n)"), s, ACT.Copy)\
                           .then_inc(frees(("xv", l, d, p)), 1)
                    act.wait_ge(bonus_done, 2 * it + 2)
                    for p in range(2):
                        s = filled(act, ("at", l, d, p))
                        act.activation(AT[:, p, :], s, ACT.Copy).then_inc(frees(("at", l, d, p)), 1)
                    for p in range(2):
                        s = filled(act, ("u0", l, d, p))
                        act.activation(U0[:, 2 * p:2 * p + 2, :, :].rearrange("p h b n -> p (h b n)"), s, ACT.Copy)\
                           .then_inc(frees(("u0", l, d, p)), 1)
                    if d == 1:
                        act.activation(siglg[:, c0:c1], Z[:, Z_G, c0:c1], ACT.Sigmoid).then_inc(lg_done, 1)
                def roots():
                    for p in range(2):
                        s = filled(act, ("var", l, p))
                        act.activation(RO[:, 2 + p, c0:c1], s[:, c0:c1], ACT.Ln, bias=eps[:, 1:2], scale=1.0 / HD)\
                           .then_inc(frees(("var", l, p)), 1)
                        emptied(act, ("var", l, p))
                        act.activation(RO[:, 2 + p, c0:c1], RO[:, 2 + p, c0:c1], ACT.Exp, scale=-0.5)\
                           .then_inc(ln_root, 1)

                act.wait_ge(mm_done, JOB[("cu", l, 1, NCH - 1)] + 1)
                split_until(half_no(("gate", l, 0, 0)) + SPLIT)
                for p in range(2):
                    emptied(act, ("mean", l, p))
                    act.activation(RO[:, p, c0:c1], YB[:, 6 + p, c0:c1], ACT.Square).then_inc(ln_sq, 1)
                for J in range(4):
                    for i in range(4):
                        for j in (2 * J, 2 * J + 1):
                            no = 8 * J + 2 * i + (j - 2 * J)
                            s = filled(act, ("gate", l, j, i))
                            split_until(min(half_no(("gate", l, j, i)) + 1 + SPLIT, half_no(("wo", l, 0)) + SPLIT))
                            if i >= 2:
                                act.wait_ge(gated, added(l, j, i - 1))
                            elif i == 1:
                                emptied(act, ("br", l, j, 0))
                            elif J:
                                act.wait_ge(gated, added(l, j - 2, 3))
                            act.activation((rt, rs)[no % 2][:, c0:c1], s[:, c0:c1], ACT.Sigmoid,
                                           bias=vc(l, "b_gate", 8 * i + j))\
                               .then_inc(frees(("gate", l, j, i)), 1)
                        if READOUT.get((J, i)) == "var":
                            roots()
                    for j in (2 * J, 2 * J + 1):
                        act.wait_ge(gated, added(l, j, 3))
                        act.activation(AR[:, 0, j, c0:c1], ACC[:, j, c0:c1], ACT.Copy).then_inc(acc_hi, 1)
                for j in range(KT):
                    s = filled(act, ("wo", l, j))
                    split_until(min(half_no(("wo", l, j)) + 1 + SPLIT, half_no(("up", l, 0, 0)) + SPLIT))
                    act.activation(OB[:, j, c0:c1], s[:, c0:c1], ACT.Copy).then_inc(frees(("wo", l, j)), 1)
                    emptied(act, ("wo", l, j))
                    square(SQB[:, j, c0:c1], OB[:, j, c0:c1])
                norm_root(l, 1)
                for i in range(KT):
                    act.wait_ge(x_ready, 16 * l + i + 1)
                    square(SQB[:, i, c0:c1], X[:, i, c0:c1])
                norm_root(l, 2)
                norm_finish(l, 2, YB, H2)
                def product_hi(j):
                    act.wait_ge(u_ready, l * FT + j + 1)
                    if j == 20:
                        act.wait_ge(x_saved, 16 * (2 * l + 1))
                    act.activation(hidden(0, j)[:, c0:c1], CU[:, j % 2, c0:c1], ACT.Copy).then_inc(u_hi, 1)

                for j in range(FT):
                    for g in range(2):
                        s = filled(act, ("up", l, j, g))
                        split_until(min(half_no(("up", l, j, g)) + 1 + SPLIT, half_no(("down", l, 0)) + SPLIT))
                        if g == 0:
                            if j >= 2:
                                act.wait_ge(u_lo, l * FT + j - 1)
                            dst = CU[:, j % 2, c0:c1]
                        else:
                            dst = (rs, rt)[j % 2][:, c0:c1]
                        act.activation(dst, s[:, c0:c1], ACT.Copy, scale=vc(l, "ffn_conv", 44 + 22 * g + j))\
                           .then_inc(conv_half, 1)
                    if j:
                        product_hi(j - 1)
                    emptied(act, ("up", l, j, 1))
                    act.activation(dst, dst, ACT.Silu).then_inc(silu_done, 1)
                product_hi(FT - 1)
                for j in range(KT):
                    split_until(half_no(("down", l, j)) + (5 if j < KT - 1 else 3))
                    s = filled(act, ("down", l, j))
                    if j < KT - 1:
                        split_until(half_no(("down", l, j)) + 6)
                    act.activation(F[:, j, c0:c1], s[:, c0:c1], ACT.Copy).then_inc(frees(("down", l, j)), 1)
                    emptied(act, ("down", l, j))
                    square(SQF[:, j, c0:c1], F[:, j, c0:c1])
                norm_root(l, 3)
                fill(("end", l, 0))

        @block.vector
        def _(dve):
            links = [0]

            def link(ins):
                links[0] += 1
                ins.then_inc(dve_chain, 1)
                dve.wait_ge(dve_chain, links[0])

            halves = [0]

            def split_until(n):
                while halves[0] < n:
                    m = halves[0]
                    raw, half = HALVES[m]
                    kn = FT % KT if raw[0] == "down" and raw[3] == 2 else KT
                    dve.wait_ge(hi_done, m + 1)
                    dve.tensor_tensor(wlo[:, m % SPLIT, 0:kn, :],
                                      ring[:, SLOT[raw] % RING, 0:kn, P * half:P * half + P],
                                      whi[:, m % SPLIT, 0:kn, :].bitcast(F32), ALU.subtract).then_inc(lo_done, 1)
                    halves[0] += 1

            def fill(point):
                for job in FILL.get(point, []):
                    if job[0] == "modt":
                        _, l, n = job
                        s = filled(dve, job)
                        b = vc(l, "ada_b", 2 * n, 2).unsqueeze(2).to_broadcast([P, 2, 2])
                        dve.tensor_tensor(mod[:, l, 2 * n:2 * n + 2, :], s[:, 0:4].rearrange("p (a s) -> p a s", a=2),
                                          b, ALU.add).then_inc(frees(job), 1)

            def gains(l, ks):
                for n in range(24):
                    if 0 not in ks or n < 8:
                        emptied(dve, ("modt", l, n))
                for k in ks:
                    m, g = ((8, "mix_pre"), (16, "mix_post"), (32, "ffn_pre"), (40, "ffn_post"))[k]
                    gb = vc(l, g, 0, 8).unsqueeze(2).to_broadcast([P, 8, 2])
                    if k % 2 == 0:
                        ins = dve.scalar_tensor_tensor(amod[:, k, :, :], mod[:, l, m:m + 8, :], 1.0, gb,
                                                       ALU.add, ALU.mult)
                    else:
                        ins = dve.tensor_tensor(amod[:, k, :, :], mod[:, l, m:m + 8, :], gb, ALU.mult)
                ins.then_inc(gains_ready, 1)
                called[0] += 1
                dve.wait_ge(gains_ready, called[0])

            called = [0]

            def norm_apply(l, k, src, tmp, dst):
                c0, c1 = cols(l) if k else (0, T)

                def low(i):
                    dve.wait_ge(h_hi, 8 * (2 * l + k // 2) + i + 1)
                    dve.tensor_tensor(dst[:, 1, i, c0:c1], tmp[:, i, c0:c1], dst[:, 0, i, c0:c1].bitcast(F32),
                                      ALU.subtract).then_inc(h_ready, 1)

                for i in range(KT):
                    if (l, k) != (0, 0):
                        over_rms(l, k, src, tmp, i)
                    if i >= 2:
                        low(i - 2)
                for i in range(KT - 2, KT):
                    low(i)

            def over_rms(l, k, src, tmp, i):
                c0, c1 = cols(l) if k else (0, T)
                dve.wait_ge(root_ready, norm_no(l, k) + 1)
                dve.tensor_tensor(tmp[:, i, c0:c1], src[:, i, c0:c1], rs[:, c0:c1], ALU.mult).then_inc(h_half, 1)

            def residual(l, k, O):
                c0, c1 = cols(l)
                dve.wait_ge(root_ready, norm_no(l, k) + 1)
                for i in range(KT + 1):
                    if i < KT:
                        dve.tensor_tensor(O[:, i, c0:c1], O[:, i, c0:c1], rs[:, c0:c1], ALU.mult).then_inc(scaled, 1)
                    if i:
                        dve.wait_ge(scaled, 8 * (2 * l + k // 2) + i)
                        for s in streams(l):
                            x = X[:, i - 1, 256 * s:256 * s + 256]
                            ins = dve.scalar_tensor_tensor(x, O[:, i - 1, 256 * s:256 * s + 256],
                                                           amod[:, k, i - 1, s:s + 1], x, ALU.mult, ALU.add)
                        ins.then_inc(x_ready, 1)

            link(dve.memset(eps[:, 0:1], EPS))
            dve.memset(eps[:, 1:2], LN_EPS).then_inc(setup, 1)
            dve.wait_ge(x_in, 16)
            for i in range(KT):
                over_rms(0, 0, X, Z, i)
            dve.wait_ge(const_in, 16)
            dve.wait_ge(vec_in, 16)
            for l in range(LAYERS):
                c0, c1 = cols(l)
                W = c1 - c0
                ns = len(streams(l))
                if l == 0:
                    fill(("start", 0, 0))
                    fill(("start", 0, 1))
                gains(l, (0,))
                link(dve.tensor_scalar(omu[:, :], vc(l, "mu", 0, 14), -1.0, 1.0, ALU.mult, ALU.add))
                link(dve.tensor_scalar(oka[:, :], vc(l, "ka", 0, 2), -1.0, 1.0, ALU.mult, ALU.add))
                split_until(half_no(("z", l, Z_ORDER[0])) + SPLIT)
                norm_apply(l, 0, X, Z, HR)
                dve.wait_ge(small_in[l], 16 * 8)
                win = K("window", GRID_W).unsqueeze(1).to_broadcast([P, HEADS * 6, GRID_W])
                bmf = bm[:, :, :, :].rearrange("p h r c -> p (h r) c")
                link(dve.tensor_tensor(bmf, bmf, win, ALU.add))
                for n, t in enumerate(Z_ORDER):
                    split_until(min(half_no(("z", l, t)) + SPLIT, half_no(("z", l, ZT - 1)) + 1))
                    if t in DVE_Z:
                        z0, z1 = cols(l, t)
                        s = filled(dve, ("z", l, t))
                        dve.tensor_copy(Z[:, t, z0:z1], s[:, z0:z1]).then_inc(frees(("z", l, t)), 1)
                    if n in (8, 10, 12):
                        i = (n - 8) // 2
                        z0, z1 = cols(l, Z_GQ + i)
                        emptied(dve, ("qss", l, i))
                        link(dve.reciprocal(qroot[i][:, z0:z1], qroot[i][:, z0:z1]))
                        v = Z[:, Z_GQ + i, z0:z1]
                        if i < 2:
                            link(dve.tensor_scalar(v, v, vc(l, "q_norm"), HD ** -0.5, ALU.mult, ALU.mult))
                            dve.tensor_tensor(v, v, qroot[i][:, z0:z1], ALU.mult).then_inc(qn_ready, 1)
                        else:
                            dve.scalar_tensor_tensor(v, v, vc(l, "k_norm"), qroot[i][:, z0:z1], ALU.mult, ALU.mult)\
                               .then_inc(qn_ready, 1)
                    if n in (16, 17, 18):
                        i = n - 16
                        v = Z[:, Z_GQ + i, CTX:T]
                        s = filled(dve, ("qsw", l, i))
                        dve.tensor_tensor(qtmp[:, 0:LAT], s[:, 0:LAT], K("sin", LAT), ALU.mult)\
                           .then_inc(frees(("qsw", l, i)), 1)
                        dve.wait_ge(qn_ready, 3 * l + i + 1)
                        link(dve.tensor_tensor(v, v, K("cos", LAT), ALU.mult))
                        emptied(dve, ("qsw", l, i))
                        dve.tensor_tensor(v, v, qtmp[:, 0:LAT], ALU.add).then_inc(qk_ready, 1)
                        dve.wait_ge(qk_ready, 3 * l + i + 1)
                    if n == 19:
                        for i in range(3):
                            s = filled(dve, ("vt", l, i))
                            dst = vB[:, :, 128 * i:128 * i + 128] if i < 2 else vC
                            dve.tensor_copy(dst, s.rearrange("p (b n) -> p b n", b=4)).then_inc(frees(("vt", l, i)), 1)
                    if n == 20:
                        for p in range(2):
                            z0, z1 = cols(l, Z_NQ + p)
                            emptied(dve, ("z", l, Z_NQ + p))
                            v = Z[:, Z_NQ + p, z0:z1]
                            dve.tensor_scalar(v, v, HD ** -0.5, None, ALU.mult).then_inc(q_scaled, 1)
                    if n == 21:
                        dve.wait_ge(ya_ready, 2 * l + 2)
                        for h in range(HEADS):
                            emptied(dve, ("z", l, Z_NK + h // 2))
                            dve.tensor_scalar(KZ[:, h, :], Z[:, Z_NK + h // 2, :],
                                              K("heads")[:, HD * (h % 2):HD * (h % 2) + 1], None, ALU.mult)\
                               .then_inc(kz_ready, 1)
                        for g in range(2):
                            dve.tensor_scalar(KZ[:, 4 + g, :], Z[:, Z_GK, :], K("heads")[:, HD * g:HD * g + 1],
                                              None, ALU.mult).then_inc(kz_ready, 1)
                units = UNITS[l]
                for i in range(len(units) + 3):
                    if i < len(units):
                        g, h, q = units[i]
                        nk = T if q >= 2 else CTX
                        s = filled(dve, ("S", l, i))
                        src = s[:, 0:nk]
                        if g == "B" and q >= 2:
                            r0 = 2 if q == 2 else 0
                            if i >= 3:
                                emptied(dve, ("S", l, i - 3))
                            dve.tensor_copy(sbuf2[:, i % 3, 0:CTX], s[:, 0:CTX])
                            link(dve.tensor_tensor(sbuf2[:, i % 3, CTX:T], s[:, CTX:T],
                                                   bm[:, h, r0:r0 + 4, :].rearrange("p r c -> p (r c)"), ALU.add))
                            src = sbuf2[:, i % 3, :]
                        dve.tensor_reduce(stat[:, 0, i % 4:i % 4 + 1], src, AX, ALU.max, negate=True)\
                           .then_inc(nmax_ready, 1)
                    if 1 <= i <= len(units):
                        u = i - 1
                        emptied(dve, ("S", l, u))
                        dve.reciprocal(stat[:, 2, u % 4:u % 4 + 1], stat[:, 1, u % 4:u % 4 + 1]).then_inc(p_sum, 1)
                    fill(("att", l, i))
                    if i >= 3:
                        g, h, q = units[i - 3]
                        half = slice(HD * (h % 2), HD * (h % 2) + HD)
                        s = filled(dve, ("PV", l, i - 3))
                        dst = YB[half, (2 if g == "B" else 4) + h // 2, 128 * q:128 * q + 128]
                        src = s[half, 0:128]
                        if g == "B" and q >= 2:
                            dst, src = grid_rows(dst), grid_rows(src)[:, :, ::-1]
                        dve.tensor_copy(dst, src).then_inc(frees(("PV", l, i - 3)), 1)
                for d in range(2):
                    it = 2 * l + d
                    step = 1 if d == 0 else -1
                    dsts = [zr[:, 0, :], zr[:, 1, :], zk[:, 0, :], zk[:, 1, :], vT[:, 0, :], vT[:, 1, :], lora]
                    def shifted(n):
                        i = SHIFTS[n]
                        dve.wait_ge(shift_half, 7 * it + n + 1)
                        s0 = c0 // 256 if i < 2 else 0
                        z = Z[:, Z_R + i, :].rearrange("p (s t) -> p s t", s=2)[:, s0:, ::step]
                        o = dsts[i].rearrange("p (s t) -> p s t", s=2)[:, s0:, 1:256]
                        dve.scalar_tensor_tensor(o, z[:, :, 0:255], vc(l, "mu", 7 * d + i), o, ALU.mult, ALU.add)\
                           .then_inc(shift_done, 1)

                    for n in range(3):
                        shifted(n)
                    dve.wait_ge(shift_done, 7 * it + 3)
                    for p in range(2):
                        dve.tensor_scalar(kk[:, p, :], zk[:, p, :], vc(l, "kk", p), None, ALU.mult)\
                           .then_inc(kraw_done, 1)
                    for n in range(3, 5):
                        shifted(n)
                    for p in range(2):
                        emptied(dve, ("wl", l, d, p))
                        dve.tensor_tensor_scan(G[:, p, :], K("reset", T), sg[:, p, :], 0.0, ALU.mult, ALU.add)\
                           .then_inc(scan_done, 1)
                    for p in range(2):
                        s = filled(dve, ("kss", l, d, p))
                        dve.tensor_scalar((rs, rt)[p][:, :], s, 1e-24, KK_SCALE ** 2, ALU.max, ALU.mult)\
                           .then_inc(frees(("kss", l, d, p)), 1)
                    for n in range(5, 7):
                        shifted(n)
                    fill(("lora", l, d))
                    for p in range(2):
                        dve.wait_ge(decay_done, 2 * it + p + 1)
                    blk = lambda v: v.rearrange("p (b t) -> p b t", b=NB)
                    for p in range(2):
                        dve.wait_ge(prev_done, 2 * it + p + 1)
                    dve.wait_ge(shift_done, 7 * it + 7)
                    for p in range(2):
                        dve.wait_ge(kscale_done, 2 * it + p + 1)
                        link(dve.tensor_tensor(zk[:, p, :], zk[:, p, :], kscale[:, p, :], ALU.mult))
                        dve.scalar_tensor_tensor(sg[:, p, c0:T], zr[:, p, c0:T], vc(l, "rk", p), zk[:, p, c0:T],
                                                 ALU.mult, ALU.mult).then_inc(bonus_in, 1)
                        dve.wait_ge(bonus_in, 2 * it + p + 1)
                        dve.tensor_tensor(zk[:, p, :], zk[:, p, :], winv[:, p, :], ALU.mult).then_inc(kap_done, 1)
                    fill(("norm", l, d))
                    for p in range(2):
                        dve.wait_ge(kroot_done, 2 * it + p + 1)
                        link(dve.scalar_tensor_tensor(kk[:, p, :], kk[:, p, :], KK_SCALE, t1[:, p, :],
                                                      ALU.mult, ALU.mult))
                        dve.tensor_tensor(ar[:, p, :, 0, :], blk(kk[:, p, :]), blk(wprev[:, p, :]), ALU.mult)
                        dve.wait_ge(awinv_done, 2 * it + p + 1)
                        dve.tensor_tensor(kk[:, p, :], kk[:, p, :], awinv[:, p, :], ALU.mult).then_inc(beta_done, 1)
                    dve.tensor_copy(wend[:, :, :], wdec[:, :, CH - 1::CH])
                    dve.memset(nu[:, :, :, :], 0.0)
                    dve.memset(state[:, 0, :, :], 0.0).then_inc(streams_done, 1)
                    fill(("bonus", l, d))
                    dve.wait_ge(rho_done, 2 * it + 2)
                    lm = K("lm", 2 * P).unsqueeze(1).to_broadcast([P, 2, 2 * P])
                    m1t = K("m1t").unsqueeze(1).to_broadcast([P, NB, P])
                    def masked(name, LM, h, b):
                        n = width(l, 2 * b)
                        s = filled(dve, (name, l, d, h, b)).rearrange("p (b n) -> p b n", b=2)
                        dve.tensor_tensor(LM[:, h, 2 * b:2 * b + 2, 0:n], s[:, :, 0:n], lm[:, :, 0:n], ALU.mult)\
                           .then_inc(frees((name, l, d, h, b)), 1)

                    for h in range(HEADS):
                        for b in range(2):
                            masked("LM1", LM1, h, b)
                        for b in range(2):
                            emptied(dve, ("LM1", l, d, h, b))
                        dve.tensor_tensor(TT[:, h, :, :], LM1[:, h, :, 0:P], m1t, ALU.mult).then_inc(tt_masked, 1)
                    dve.wait_ge(bonus_done, 2 * it + 2)
                    for zi, z in enumerate(LEVELS):
                        mz = K(f"m{z}").unsqueeze(1).to_broadcast([P, NB, P])
                        if zi == 0:
                            for b in range(2):
                                masked("LM2", LM2, 0, b)
                        for h in range(HEADS):
                            s = filled(dve, ("sx", l, d, z, h)).rearrange("p (b n) -> p b n", b=NB)
                            dve.tensor_tensor(XS[:, h, :, :], s, mz, ALU.mult).then_inc(frees(("sx", l, d, z, h)), 1)
                        if 0 < zi < HEADS:
                            for b in range(2):
                                masked("LM2", LM2, zi, b)
                        for h in range(HEADS):
                            name, M = (("syt", l, d, z, h), TT) if z == LEVELS[-1] else (("sy", l, d, z, h), TN)
                            s = filled(dve, name).rearrange("p (b n) -> p b n", b=NB)
                            dve.tensor_tensor(M[:, h, :, :], M[:, h, :, :], s, ALU.subtract).then_inc(frees(name), 1)
                    for p in range(2):
                        emptied(dve, ("u0", l, d, p))
                    for c in range(NCH):
                        q = slice(HD * (c % 2), HD * (c % 2) + HD)
                        s = filled(dve, ("cu", l, d, c))
                        dve.scalar_tensor_tensor(nu[q, c % 2, :, :], s[q, 0:256].rearrange("p (h n) -> p h n", h=HEADS),
                                                 -1.0, U0[q, :, c // 2, :], ALU.mult, ALU.subtract)\
                           .then_inc(frees(("cu", l, d, c)), 1)
                        if c < NCH - 1:
                            s = filled(dve, ("ch", l, d, c))
                            for p in range(2):
                                dve.scalar_tensor_tensor(state[:, (c + 1) % 2, p, :], s[:, P * p:P * p + P],
                                                         wend[:, p, c:c + 1], K("heads"), ALU.mult, ALU.mult)\
                                   .then_inc(frees(("ch", l, d, c)) if p else state_half, 1)
                        if l == 0 or c >= NCH // 2:
                            s = filled(dve, ("cy", l, d, c))[:, 0:128].rearrange("p (a t) -> p a t", a=2)
                            if d == 0:
                                dve.tensor_copy(YB[:, 6:8, CH * c:CH * c + CH], s)\
                                   .then_inc(frees(("cy", l, d, c)), 1)
                            else:
                                st, r = c // 4, c % 4
                                e = 256 * st + 256 - CH * r
                                y = YB[:, 6:8, e - CH:e]
                                dve.tensor_tensor(y, y, s[:, :, ::-1], ALU.add).then_inc(frees(("cy", l, d, c)), 1)
                split_until(half_no(("gate", l, 0, 0)) + SPLIT)
                for p in range(2):
                    y = YB[:, 6 + p, c0:c1]
                    s = filled(dve, ("mean", l, p))
                    dve.scalar_tensor_tensor(y, s[:, c0:c1], -1.0 / HD, y, ALU.mult, ALU.add)\
                       .then_inc(frees(("mean", l, p)), 1)

                def readout():
                    for p in range(2):
                        y = YB[:, 6 + p, c0:c1]
                        dve.wait_ge(ln_root, 2 * l + p + 1)
                        link(dve.scalar_tensor_tensor(y, y, vc(l, "ln_w", p), RO[:, 2 + p, c0:c1], ALU.mult, ALU.mult))
                        link(dve.scalar_tensor_tensor(y, y, vc(l, "ln_b", p), bon[:, p, c0:c1], ALU.add, ALU.add))
                        s = filled(dve, ("g2", l, p))
                        dve.tensor_tensor(y, y, s[:, c0:c1], ALU.mult).then_inc(frees(("g2", l, p)), 1)

                for J in range(4):
                    for i in range(4):
                        for j in (2 * J, 2 * J + 1):
                            split_until(min(half_no(("gate", l, j, i)) + SPLIT, half_no(("wo", l, 0)) + SPLIT))
                            no = 8 * J + 2 * i + (j - 2 * J)
                            gt = (rt, rs)[no % 2][:, c0:c1]
                            s = filled(dve, ("br", l, j, i))[:, c0:c1]
                            emptied(dve, ("gate", l, j, i))
                            o = ACC[:, j, c0:c1]
                            dst = o if i == 0 else gt
                            dve.tensor_tensor(dst, gt, s, ALU.mult).then_inc(frees(("br", l, j, i)), 1)
                            emptied(dve, ("br", l, j, i))
                            if i:
                                dve.tensor_tensor(o, o, gt, ALU.add).then_inc(gated, 1)
                        if READOUT.get((J, i)) == "g2":
                            readout()
                    for j in (2 * J, 2 * J + 1):
                        dve.wait_ge(acc_hi, 8 * l + j + 1)
                        dve.tensor_tensor(AR[:, 1, j, c0:c1], ACC[:, j, c0:c1], AR[:, 0, j, c0:c1].bitcast(F32),
                                          ALU.subtract).then_inc(acc_lo, 1)
                for j in range(KT):
                    split_until(min(half_no(("wo", l, j)) + 1 + SPLIT, half_no(("up", l, 0, 0)) + SPLIT))
                gains(l, (1, 2, 3))
                dve.wait_ge(x_back, 32 * l + 16)
                residual(l, 1, OB)
                dve.wait_ge(x_ready, 16 * l + 8)
                norm_apply(l, 2, X, YB, H2)
                def product_lo(j):
                    dve.wait_ge(u_hi, l * FT + j + 1)
                    dve.tensor_tensor(hidden(1, j)[:, c0:c1], CU[:, j % 2, c0:c1],
                                      hidden(0, j)[:, c0:c1].bitcast(F32), ALU.subtract).then_inc(u_lo, 1)

                for j in range(FT):
                    for g in range(2):
                        split_until(min(half_no(("up", l, j, g)) + SPLIT, half_no(("down", l, 0)) + SPLIT))
                        dve.wait_ge(conv_half, 2 * (FT * l + j) + g + 1)
                        s = bank(("up", l, j, g))[:, c0:c1].rearrange("p (s t) -> p s t", s=ns)
                        o = (CU[:, j % 2, c0:c1] if g == 0 else (rs, rt)[j % 2][:, c0:c1])\
                            .rearrange("p (s t) -> p s t", s=ns)
                        link(dve.scalar_tensor_tensor(o[:, :, 1:256], s[:, :, 0:255], vc(l, "ffn_conv", 22 * g + j),
                                                      o[:, :, 1:256], ALU.mult, ALU.add))
                        dve.scalar_tensor_tensor(o[:, :, 0:255], s[:, :, 1:256], vc(l, "ffn_conv", 88 + 22 * g + j),
                                                 o[:, :, 0:255], ALU.mult, ALU.add).then_inc(frees(("up", l, j, g)), 1)
                    if j:
                        product_lo(j - 1)
                product_lo(FT - 1)
                split_until(half_no(("down", l, 0)) + 3 * KT)
                for j in range(KT):
                    emptied(dve, ("down", l, j))
                dve.wait_ge(x_back, 32 * (l + 1))
                residual(l, 3, F)
                fill(("end", l, 0))
                dve.wait_ge(x_ready, 16 * l + 16)

        @block.tensor
        def _(pe):
            def job(name, ahead=0):
                g = JOB[name]
                assert g == count[0] + ahead, (name, g, count[0])
                if g >= NBANK:
                    pe.wait_ge(bank_free[g % NBANK], g // NBANK)
                return ps[:, g % NBANK, :]

            count = [0]

            def done(ins):
                count[0] += 1
                ins.then_inc(mm_done, 1)

            def weights(name):
                n = SLOT[name]
                pe.wait_ge(w_in_slot[n % RING], 16 * (n // RING + 1))
                return ring[:, n % RING, :, :]

            def sum_squares(l, k, src):
                c0, c1 = cols(l) if k else (0, T)
                o = job(("ss", l, k))
                for i in range(KT):
                    pe.wait_ge(sq_ready, 8 * norm_no(l, k) + i + 1)
                    last = pe.matmul(o[:, c0:c1], K("ones"), src[:, i, c0:c1], start=(i == 0), stop=(i == KT - 1))
                done(last)

            def halves(name):
                for raw in blocks_of(name):
                    m = HALF[raw]
                    pe.wait_ge(lo_done, m + 1)
                    yield whi[:, m % SPLIT, :, :], wlo[:, m % SPLIT, :, :]

            def project(name, part, c0, c1, kn=KT, made=None):
                o = job(name)
                k = 0
                for hi, lo in halves(name):
                    for i in range(min(KT, kn - k)):
                        if made:
                            pe.wait_ge(made[0], made[1] + k + 1)
                        pe.matmul(o[:, c0:c1], hi[:, i, :], part(0, k), start=(k == 0), stop=False)
                        pe.matmul(o[:, c0:c1], hi[:, i, :], part(1, k), start=False, stop=False)
                        last = pe.matmul(o[:, c0:c1], lo[:, i, :], part(0, k), start=False, stop=(k == kn - 1))
                        k += 1
                    if k < kn:
                        last.then_inc(w_used, 1)
                done(last)

            def fill(point):
                for name in FILL.get(point, []):
                    if name[0] == "mod":
                        w = weights(("ada",) + name[1:])
                        o = job(name)
                        for k in range(KT):
                            last = pe.matmul(o[0:2, 0:SLOT_N], cvec[:, k, :], w[:, k, :],
                                             start=(k == 0), stop=(k == KT - 1))
                    else:
                        pe.wait_ge(const_in, 16)
                        emptied(pe, ("mod",) + name[1:])
                        o = job(name)
                        for x in range(2):
                            last = pe.transpose(o[:, 2 * x:2 * x + 2], mrow[:, P * x:P * x + P], K("ident")[0:2, 0:2])
                    done(last)

            pe.wait_ge(silu_c, 1)
            for l in range(LAYERS):
                c0, c1 = cols(l)
                fill(("start", l, 0))
                sum_squares(l, 0, YB)
                fill(("start", l, 1))
                for n, t in enumerate(Z_ORDER):
                    z0, z1 = cols(l, t)
                    project(("z", l, t), lambda x, k: HR[:, x, k, z0:z1], z0, z1,
                            made=None if n else (h_ready, 16 * l))
                    if n == 5:
                        for i in range(3):
                            q0, q1 = cols(l, Z_GQ + i)
                            o = job(("qss", l, i))
                            pe.wait_ge(qsq_ready, 3 * l + i + 1)
                            done(pe.matmul(o[:, q0:q1], K("heads"), qsq[i][:, q0:q1], start=True, stop=True))
                    if n == 14:
                        for i in range(3):
                            o = job(("qsw", l, i))
                            pe.wait_ge(qn_ready, 3 * l + i + 1)
                            done(pe.matmul(o[:, 0:LAT], K("swap"), Z[:, Z_GQ + i, CTX:T], start=True, stop=True))
                    if n == 17:
                        for i in range(3):
                            tv = Z_NV + i if i < 2 else Z_GV
                            emptied(pe, ("z", l, tv))
                            o = job(("vt", l, i))
                            for b in range(4):
                                last = pe.transpose(o[:, 128 * b:128 * b + 128], Z[:, tv, 128 * b:128 * b + 128],
                                                    K("ident"))
                            done(last)
                pe.wait_ge(q_scaled, 2 * l + 2)
                pe.wait_ge(qk_ready, 3 * l + 3)
                pe.wait_ge(kz_ready, 6 * l + 6)
                for i in range(3):
                    emptied(pe, ("vt", l, i))
                units = UNITS[l]
                for i in range(len(units) + 3):
                    if i < len(units):
                        g, h, q = units[i]
                        nk = T if q >= 2 else CTX
                        tq, tk = (Z_NQ + h // 2, h) if g == "B" else (Z_GQ + h % 2, 4 + h // 2)
                        o = job(("S", l, i))
                        done(pe.matmul(o[:, 0:nk], Z[:, tq, 128 * q:128 * q + 128], KZ[:, tk, 0:nk],
                                       start=True, stop=True))
                    fill(("att", l, i))
                    if 2 <= i <= len(units) + 1:
                        u = i - 2
                        nt = (T if units[u][2] >= 2 else CTX) // P
                        o = job(("T", l, u))
                        pe.wait_ge(p_ready, UBASE[l] + u + 1)
                        for b in range(nt):
                            last = pe.transpose(o[:, 128 * b:128 * b + 128], pr[:, u % 3, 128 * b:128 * b + 128],
                                                K("ident"))
                        done(last)
                    if i >= 3:
                        g, h, q = units[i - 3]
                        nt = (T if q >= 2 else CTX) // P
                        o = job(("PV", l, i - 3))
                        emptied(pe, ("T", l, i - 3))
                        half = slice(HD * (h % 2), HD * (h % 2) + HD)
                        for b in range(nt):
                            v = vB[:, b, HD * h:HD * h + HD] if g == "B" else vC[:, b, HD * (h // 2):HD * (h // 2) + HD]
                            last = pe.matmul(o[half, 0:128], v, prT[:, (i - 3) % 3, 128 * b:128 * b + 128],
                                             start=(b == 0), stop=(b == nt - 1))
                        done(last)
                for d in range(2):
                    it = 2 * l + d
                    pe.wait_ge(lora_in, 16 * (l + 1))

                    def token_major(m, p, src):
                        o = job(("tok", l, d, m, p))
                        for b in range(NB):
                            last = pe.transpose(o[:, 128 * b:128 * b + 128], src[:, 128 * b:128 * b + 128], K("ident"))
                        done(last)

                    def products(name, h, lhs):
                        for b in range(2):
                            o = job((name, l, d, h, b))
                            for x in range(2):
                                bb = 2 * b + x
                                n = width(l, bb)
                                last = pe.matmul(o[:, 256 * x:256 * x + n], lhs[:, 128 * bb:128 * bb + 128],
                                                 ar[:, h // 2, bb, :, :].rearrange("p a t -> p (a t)")[:, 0:n],
                                                 start=True, stop=True)
                            done(last)

                    for p in range(2):
                        pe.wait_ge(tanh_done, it + 1)
                        o = job(("wl", l, d, p))
                        done(pe.matmul(o, w2a2[:, d, 0, 128 * p:128 * p + 128], lora[:, :], start=True, stop=True))
                        o = job(("al", l, d, p))
                        done(pe.matmul(o, w2a2[:, d, 1, 128 * p:128 * p + 128], lora[:, :], start=True, stop=True))
                    for p in range(2):
                        pe.wait_ge(ksq_done, 2 * it + p + 1)
                        o = job(("kss", l, d, p))
                        done(pe.matmul(o, K("heads"), t1[:, p, :], start=True, stop=True))
                    fill(("lora", l, d))
                    pe.wait_ge(shift_done, 7 * it + 5)
                    for p in range(2):
                        token_major("v", p, vT[:, p, :])
                    fill(("norm", l, d))
                    for p in range(2):
                        pe.wait_ge(bonus_in, 2 * it + p + 1)
                        o = job(("bon", l, d, p))
                        done(pe.matmul(o[:, c0:T], K("heads"), sg[:, p, c0:T], start=True, stop=True))
                    for p in range(2):
                        pe.wait_ge(kap_done, 2 * it + p + 1)
                        token_major("k", p, zk[:, p, :])
                    fill(("bonus", l, d))
                    for h in range(HEADS):
                        p = h // 2
                        pe.wait_ge(betaz_done, 4 * it + h + 1)
                        pe.wait_ge(rho_done, 2 * it + p + 1)
                        products("LM1", h, betaz[:, h, :])
                        if h % 2:
                            pe.wait_ge(beta_done, 2 * it + p + 1)
                            o = job(("tok", l, d, "a", p))
                            for b in range(NB):
                                last = pe.transpose(o[:, 128 * b:128 * b + 128], ar[:, p, b, 0, :], K("ident"))
                            done(last)
                            token_major("b", p, kk[:, p, :])
                    pe.wait_ge(kapz_done, 4 * it + 4)
                    for h in range(HEADS):
                        pe.wait_ge(t_done, 4 * it + h + 1)
                        o = job(("tn", l, d, h))
                        for b in range(NB):
                            last = pe.transpose(o[:, 128 * b:128 * b + 128], TT[:, h, b, :], K("ident"))
                        done(last)
                    for h in range(HEADS):
                        for b in range(2):
                            emptied(pe, ("LM1", l, d, h, b))
                    for zi, z in enumerate(LEVELS):
                        if zi == 0:
                            products("LM2", 0, kapz(0))
                        for h in range(HEADS):
                            emptied(pe, ("sy", l, d, LEVELS[zi - 1], h) if zi else ("tn", l, d, h))
                            o = job(("sx", l, d, z, h))
                            for b in range(NB):
                                last = pe.matmul(o[:, 128 * b:128 * b + 128], LM1[:, h, b, 0:P], TN[:, h, b, :],
                                                 start=True, stop=True)
                            done(last)
                        if zi:
                            for h in range(HEADS):
                                o = job(("tt", l, d, z, h))
                                for b in range(NB):
                                    last = pe.transpose(o[:, 128 * b:128 * b + 128], TN[:, h, b, :], K("ident"))
                                done(last)
                        if 0 < zi < HEADS:
                            products("LM2", zi, kapz(zi))
                        if zi == HEADS:
                            for h in range(HEADS):
                                for b in range(2):
                                    emptied(pe, ("LM2", l, d, h, b))
                            for p in range(2):
                                emptied(pe, ("tok", l, d, "v", p))
                            for p in range(2):
                                o = job(("xv", l, d, p))
                                for x in range(2):
                                    for b in range(NB):
                                        h = 2 * p + x
                                        last = pe.matmul(o[:, 256 * x + 64 * b:256 * x + 64 * b + 64],
                                                         LM2[:, h, b, 0:P], tokm["v"][:, b, HD * h:HD * h + HD],
                                                         start=True, stop=True)
                                done(last)
                        for h in range(HEADS):
                            emptied(pe, ("sx", l, d, z, h))
                            if zi:
                                emptied(pe, ("tt", l, d, z, h))
                            last_level = z == LEVELS[-1]
                            o = job(("syt" if last_level else "sy", l, d, z, h))
                            for b in range(NB):
                                lhs, rhs = (XS, TT) if last_level else (TT, XS)
                                last = pe.matmul(o[:, 128 * b:128 * b + 128], lhs[:, h, b, :], rhs[:, h, b, :],
                                                 start=True, stop=True)
                            done(last)
                    for h in range(HEADS):
                        emptied(pe, ("syt", l, d, LEVELS[-1], h))
                    for m in "akbv":
                        for p in range(2):
                            emptied(pe, ("tok", l, d, m, p))
                    for p in range(2):
                        o = job(("at", l, d, p))
                        for x in range(2):
                            for b in range(NB):
                                h = 2 * p + x
                                last = pe.matmul(o[HD * x:HD * x + HD, 128 * b:128 * b + 128],
                                                 tokm["a"][:, b, HD * h:HD * h + HD], TT[:, h, b, :],
                                                 start=True, stop=True)
                        done(last)
                    for p in range(2):
                        emptied(pe, ("xv", l, d, p))
                        o = job(("u0", l, d, p))
                        for x in range(2):
                            for b in range(NB):
                                h = 2 * p + x
                                last = pe.matmul(o[:, 256 * x + 64 * b:256 * x + 64 * b + 64], TT[:, h, b, :],
                                                 XV[:, h, b, :], start=True, stop=True)
                        done(last)
                    for p in range(2):
                        emptied(pe, ("at", l, d, p))
                    pe.wait_ge(streams_done, it + 1)
                    pe.wait_ge(vm_done, 2 * it + 2)
                    for c in range(NCH):
                        b, qs = c // 2, slice(HD * (c % 2), HD * (c % 2) + HD)
                        tc = slice(HD * (c % 2), HD * (c % 2) + HD)
                        cs = slice(CH * c, CH * c + CH)
                        o = job(("cu", l, d, c))
                        for p in range(2):
                            if c and p == 0:
                                pe.wait_ge(state_half, (NCH - 1) * it + c)
                            elif c:
                                emptied(pe, ("ch", l, d, c - 1))
                            last = pe.matmul(o[qs, P * p:P * p + P], AT[:, p, cs], state[:, c % 2, p, :],
                                             start=True, stop=True)
                        done(last)
                        mc = slice(P + CH * (c % 2), P + CH * (c % 2) + CH)
                        carried, read = c < NCH - 1, l == 0 or c >= NCH // 2
                        if carried:
                            och = job(("ch", l, d, c))
                            for p in range(2):
                                dst, hs = och[:, P * p:P * p + P], slice(P * p, P * p + P)
                                pe.matmul(dst, K("ident"), state[:, c % 2, p, :], start=(p == 0), stop=(p == 0),
                                          skip_group_check=True)
                                pe.matmul(dst, tokm["k"][:, b, hs], VM[:, c % 2, b, hs], start=False, stop=False,
                                          skip_group_check=True)
                        if read:
                            ocy = job(("cy", l, d, c), 1 if carried else 0)
                            for p in range(2):
                                dst = ocy[:, CH * p:CH * p + CH]
                                pe.matmul(dst, state[:, c % 2, p, :], ar[:, p, b, 1, tc], start=(p == 0), stop=(p == 0),
                                          skip_group_check=True)
                                for h in (2 * p, 2 * p + 1):
                                    r, hs = slice(HD * (h % 2), HD * (h % 2) + HD), slice(HD * h, HD * h + HD)
                                    pe.matmul(dst[r, :], tokm["v"][qs, b, hs], LM2[qs, h, b, mc],
                                              start=False, stop=False, skip_group_check=True)
                        emptied(pe, ("cu", l, d, c))
                        if carried:
                            for p in range(2):
                                dst, hs = och[:, P * p:P * p + P], slice(P * p, P * p + P)
                                last = pe.matmul(dst, tokm["b"][:, b, hs],
                                                 nu[:, c % 2, 2 * p:2 * p + 2, :].rearrange("p h n -> p (h n)"),
                                                 start=False, stop=False, skip_group_check=True)
                            done(last)
                        if read:
                            for h in range(HEADS):
                                dst = ocy[HD * (h % 2):HD * (h % 2) + HD, CH * (h // 2):CH * (h // 2) + CH]
                                last = pe.matmul(dst, nu[qs, c % 2, h, :], LM1[qs, h, b, mc],
                                                 start=False, stop=False, skip_group_check=True)
                            done(last)
                for p in range(2):
                    emptied(pe, ("cy", l, 1, NCH - 1))
                    o = job(("mean", l, p))
                    done(pe.matmul(o[:, c0:c1], K("heads"), YB[:, 6 + p, c0:c1], start=True, stop=True))
                pe.wait_ge(ya_ready, 2 * l + 2)
                for i in range(len(units)):
                    if i >= len(units) - NBANK:
                        emptied(pe, ("PV", l, i))
                pe.wait_ge(h_back[l], 32)
                for J in range(4):
                    for i in range(4):
                        for j in (2 * J, 2 * J + 1):
                            project(("gate", l, j, i), lambda x, k: HG[:, x, k, c0:c1], c0, c1)
                            wb = WB[:, J % 2, :, :]
                            pe.wait_ge(wb_in, 16 * (4 * l + J + 1))
                            if (J, i) == (0, 3):
                                for p in range(2):
                                    emptied(pe, ("g2", l, p))
                            o = job(("br", l, j, i))
                            for k in range(2):
                                last = pe.matmul(o[:, c0:c1], wb[:, 2 * i + k, P * (j % 2):P * (j % 2) + P],
                                                 YB[:, 2 * i + k, c0:c1], start=(k == 0), stop=(k == 1))
                            done(last)
                        if READOUT.get((J, i)) == "var":
                            for p in range(2):
                                pe.wait_ge(ln_sq, 2 * l + p + 1)
                                o = job(("var", l, p))
                                done(pe.matmul(o[:, c0:c1], K("heads"), RO[:, p, c0:c1], start=True, stop=True))
                        elif READOUT.get((J, i)) == "g2":
                            pe.wait_ge(lg_done, l + 1)
                            pe.wait_ge(g2_in, 16 * (l + 1))
                            for p in range(2):
                                o = job(("g2", l, p))
                                done(pe.matmul(o[:, c0:c1], g2[:, 128 * p:128 * p + 128], siglg[:, c0:c1],
                                               start=True, stop=True))
                for j in range(KT):
                    project(("wo", l, j), lambda x, k: AR[:, x, k, c0:c1], c0, c1,
                            made=None if j else (acc_lo, 8 * l))
                sum_squares(l, 1, SQB)
                sum_squares(l, 2, SQB)
                for j in range(FT):
                    for g in range(2):
                        project(("up", l, j, g), lambda x, k: H2[:, x, k, c0:c1], c0, c1,
                                made=None if j or g else (h_ready, 16 * l + 8))
                for j in range(KT):
                    project(("down", l, j), lambda x, k: hidden(x, k)[:, c0:c1], c0, c1, FT,
                            made=None if j else (u_lo, FT * l))
                sum_squares(l, 3, SQF)
                fill(("end", l, 0))


IN_NAMES = ["const", "vecs", "cs", "xin", "w2a2", "g2", "na_bias", "ada_w", "w_in", "w_branch", "w_gate", "w_o",
            "ffn_up", "ffn_down"]


def kernel(x, c, ctx, c_ctx, ada_w, ada_b, norm_mix_pre, norm_mix_post, norm_ffn_pre, norm_ffn_post,
           w_in, conv_a, na_bias, q_norm, k_norm, rw_mu, rw_w0, rw_w2, rw_a0, rw_a2, rw_kk, rw_ka, rw_rk,
           rw_g2, rw_ln_w, rw_ln_b, w_branch, w_gate, b_gate, w_o, ffn_up, ffn_conv, ffn_down):
    import concourse.bacc as bacc
    from concourse.bass_utils import run_bass_kernel_spmd

    def columns(v):
        v = np.asarray(v)
        return v.reshape(LAYERS, -1, P).transpose(0, 2, 1)

    twice = lambda v: np.concatenate([v, v], axis=-1)
    q_norm, k_norm = np.asarray(q_norm), np.asarray(k_norm)
    parts = dict(mix_pre=norm_mix_pre, mix_post=norm_mix_post, ffn_pre=norm_ffn_pre, ffn_post=norm_ffn_post,
                 ada_b=ada_b, conv_a=conv_a, q_norm=twice(q_norm), k_norm=twice(k_norm), mu=rw_mu, w0=rw_w0,
                 a0=rw_a0, kk=rw_kk, ka=rw_ka, rk=rw_rk, ln_w=rw_ln_w, ln_b=rw_ln_b, b_gate=b_gate,
                 ffn_conv=ffn_conv)
    vecs = np.concatenate([columns(parts[n]) for n, _ in VEC_COLS], axis=2)
    order = np.arange(ZT * P)
    q0 = Z_GQ * P
    order[q0:q0 + 256] = q0 + np.concatenate([np.arange(64) + 64 * h for h in (0, 2, 1, 3)])
    arrays = dict(
        const=constants(), vecs=vecs,
        cs=np.stack([np.asarray(c_ctx), np.asarray(c)[0]], axis=1),
        xin=np.concatenate([np.asarray(ctx)[0].T, np.asarray(x)[0].T], axis=1),
        w2a2=np.stack([np.pad(np.asarray(rw_w2), ((0, 0), (0, 0), (0, HD), (0, 0))),
                       np.pad(np.asarray(rw_a2), ((0, 0), (0, 0), (HD, 0), (0, 0)))], axis=2).transpose(0, 3, 1, 2, 4),
        g2=rw_g2, na_bias=na_bias, ada_w=ada_w, w_in=np.asarray(w_in)[:, :, order],
        w_branch=np.asarray(w_branch).reshape(LAYERS, DM, DM), w_gate=w_gate, w_o=w_o, ffn_up=ffn_up,
        ffn_down=ffn_down)
    nc = bacc.Bacc("TRN2", target_bir_lowering=False, num_devices=1)
    ins, aps = {}, {}
    for n in IN_NAMES:
        v = np.ascontiguousarray(np.asarray(arrays[n]))
        ins["in_" + n] = v
        aps[n] = nc.dram_tensor("in_" + n, v.shape, mybir.dt.from_np(v.dtype), kind="ExternalInput").ap()
    out = nc.dram_tensor("out", (DM, LAT), F32, kind="ExternalOutput").ap()
    build(nc, aps, out)
    r = run_bass_kernel_spmd(nc, [ins], core_ids=[0])
    return np.ascontiguousarray(r.results[0]["out"].T)[None]
```
